# Optimizing a Trainium2 kernel written in Bass

```python
import jax, jax.numpy as jnp
from jax import lax
import numpy as np

D_MODEL = 1024
BATCH = 1
SEQ = 1024
DEPTH = 1

DN_HEADS = 8
DN_HEAD_DIM = 128
DN_WIDTH = DN_HEADS * DN_HEAD_DIM
DN_CONV = 4
DN_CHUNK = 64
SB_HEADS = 8
SB_HEAD_DIM = 128
SB_WIDTH = SB_HEADS * SB_HEAD_DIM
SB_BLOCK = 128
D_FF = 2816
FFN_CONV = 3
EPS = 1e-6

DN_QKV_END = 3 * DN_WIDTH
DN_A_END = DN_QKV_END + DN_HEADS
DN_B_END = DN_A_END + DN_HEADS
DN_G_END = DN_B_END + DN_WIDTH
SB_QKV_END = DN_G_END + 3 * SB_WIDTH
IN_WIDTH = SB_QKV_END + 2 * D_MODEL
SPLIT_IDX = (DN_QKV_END, DN_A_END, DN_B_END, DN_G_END, SB_QKV_END)

kernel_name = 'hybrid_gdn_stickbreak_convffn'

def rmsnorm(x, w):
    xf = x.astype(jnp.float32)
    y = xf * lax.rsqrt(jnp.mean(xf * xf, axis=-1, keepdims=True) + EPS)
    return (y * w.astype(jnp.float32)).astype(x.dtype)

def l2norm(x):
    xf = x.astype(jnp.float32)
    return (xf * lax.rsqrt(jnp.sum(xf * xf, axis=-1, keepdims=True) + EPS)).astype(x.dtype)

def causal_dwconv(x, w):
    K = w.shape[0]
    T = x.shape[1]
    xp = jnp.pad(x, ((0, 0), (K - 1, 0), (0, 0)))
    y = w[0] * xp[:, 0:T]
    for i in range(1, K):
        y = y + w[i] * xp[:, i:i + T]
    return y

def to_heads(t, n_heads, head_dim):
    B, T, _ = t.shape
    return t.reshape(B, T, n_heads, head_dim).transpose(0, 2, 1, 3)

def gated_delta_rule(q, k, v, g, beta):
    out_dtype = v.dtype
    q, k, v, g, beta = (t.astype(jnp.float32) for t in (q, k, v, g, beta))
    B, H, T, dk = q.shape
    dv = v.shape[-1]
    C = DN_CHUNK
    N = T // C
    q = q * (dk ** -0.5)
    rs = lambda t: t.reshape(B, H, N, C, *t.shape[3:])
    q, k, v, g, beta = rs(q), rs(k), rs(v), rs(g), rs(beta)
    g = jnp.cumsum(g, axis=-1)
    k_beta = k * beta[..., None]
    v_beta = v * beta[..., None]
    lower = jnp.tril(jnp.ones((C, C), dtype=bool))
    strict = jnp.tril(jnp.ones((C, C), dtype=bool), -1)
    diff = g[..., :, None] - g[..., None, :]
    decay = jnp.where(lower, jnp.exp(jnp.where(lower, diff, 0.0)), 0.0)
    L = jnp.where(strict, jnp.einsum('bhncd,bhnsd->bhncs', k_beta, k) * decay, 0.0)
    rhs = jnp.concatenate([v_beta, k_beta * jnp.exp(g)[..., None]], axis=-1)
    sol = lax.linalg.triangular_solve(L, rhs, left_side=True, lower=True, unit_diagonal=True)
    u = sol[..., :dv]
    w = sol[..., dv:]
    a_qk = jnp.where(lower, jnp.einsum('bhncd,bhnsd->bhncs', q, k) * decay, 0.0)

    def step(S, xs):
        q_i, k_i, u_i, w_i, g_i, a_i = xs
        v_new = u_i - jnp.einsum('bhcd,bhde->bhce', w_i, S)
        o_i = (jnp.einsum('bhcd,bhde->bhce', q_i * jnp.exp(g_i)[..., None], S)
               + jnp.einsum('bhcs,bhse->bhce', a_i, v_new))
        g_last = g_i[..., -1]
        S = (S * jnp.exp(g_last)[..., None, None]
             + jnp.einsum('bhcd,bhce->bhde', k_i * jnp.exp(g_last[..., None] - g_i)[..., None], v_new))
        return S, o_i

    xs = tuple(jnp.moveaxis(t, 2, 0) for t in (q, k, u, w, g, a_qk))
    S0 = jnp.zeros((B, H, dk, dv), jnp.float32)
    _, o = lax.scan(step, S0, xs)
    o = jnp.moveaxis(o, 0, 2).reshape(B, H, T, dv)
    return o.astype(out_dtype)

def stick_breaking_attention(q, k, v):
    B, H, T, d = q.shape
    nb = T // SB_BLOCK
    scale = d ** -0.5
    qb = q.reshape(B, H, nb, SB_BLOCK, d).transpose(2, 0, 1, 3, 4)
    key_pos = jnp.arange(T)

    def block(args):
        q_blk, i = args
        z = jnp.einsum('bhqd,bhkd->bhqk', q_blk, k).astype(jnp.float32) * scale
        q_pos = i * SB_BLOCK + jnp.arange(SB_BLOCK)
        mask = key_pos[None, :] < q_pos[:, None]
        log_keep = jnp.where(mask, jax.nn.log_sigmoid(-z), 0.0)
        between = lax.cumsum(log_keep, axis=3, reverse=True) - log_keep
        log_a = jax.nn.log_sigmoid(z) + between
        a = jnp.where(mask, jnp.exp(log_a), 0.0)
        return jnp.einsum('bhqk,bhkd->bhqd', a.astype(v.dtype), v)

    o = lax.map(block, (qb, jnp.arange(nb)))
    return o.transpose(1, 2, 0, 3, 4).reshape(B, H, T, d)

def setup_inputs(seed: int = 0) -> dict:
    key = jax.random.key(seed)
    ks = jax.random.split(key, 20)
    L = DEPTH
    nrm = lambda k, shape, fan_in: jax.random.normal(k, shape, jnp.float32) * (fan_in ** -0.5)
    gain = lambda k, shape: 1.0 + 0.02 * jax.random.normal(k, shape, jnp.float32)
    x = jax.random.normal(ks[0], (BATCH, SEQ, D_MODEL), jnp.float32)
    norm1_w = gain(ks[1], (L, D_MODEL))
    w_in = nrm(ks[2], (L, D_MODEL, IN_WIDTH), D_MODEL)
    dn_conv_w = nrm(ks[3], (L, DN_CONV, 3 * DN_WIDTH), DN_CONV)
    dn_A_log = jnp.log(jax.random.uniform(ks[4], (L, DN_HEADS), jnp.float32, 1.0, 16.0))
    dt = jnp.exp(jax.random.uniform(ks[5], (L, DN_HEADS), jnp.float32, np.log(1e-3), np.log(1e-1)))
    dn_dt_bias = dt + jnp.log(-jnp.expm1(-dt))
    dn_norm_w = gain(ks[6], (L, DN_HEAD_DIM))
    w_proj_dn = nrm(ks[7], (L, DN_WIDTH, D_MODEL), DN_WIDTH)
    w_proj_sb = nrm(ks[8], (L, SB_WIDTH, D_MODEL), SB_WIDTH)
    w_out = nrm(ks[9], (L, D_MODEL, D_MODEL), D_MODEL)
    norm2_w = gain(ks[10], (L, D_MODEL))
    ffn_w_up = nrm(ks[11], (L, D_MODEL, 2 * D_FF), D_MODEL)
    ffn_conv_w = nrm(ks[12], (L, FFN_CONV, 2 * D_FF), FFN_CONV)
    ffn_w_down = nrm(ks[13], (L, D_FF, D_MODEL), D_FF)
    norm_f_w = gain(ks[14], (D_MODEL,))
    return {'x': x, 'norm1_w': norm1_w, 'w_in': w_in, 'dn_conv_w': dn_conv_w,
            'dn_A_log': dn_A_log, 'dn_dt_bias': dn_dt_bias, 'dn_norm_w': dn_norm_w,
            'w_proj_dn': w_proj_dn, 'w_proj_sb': w_proj_sb, 'w_out': w_out,
            'norm2_w': norm2_w, 'ffn_w_up': ffn_w_up, 'ffn_conv_w': ffn_conv_w,
            'ffn_w_down': ffn_w_down, 'norm_f_w': norm_f_w}

def reference(x, norm1_w, w_in, dn_conv_w, dn_A_log, dn_dt_bias, dn_norm_w,
              w_proj_dn, w_proj_sb, w_out, norm2_w, ffn_w_up, ffn_conv_w,
              ffn_w_down, norm_f_w):
    B, T, _ = x.shape
    for l in range(DEPTH):
        n1 = rmsnorm(x, norm1_w[l])
        h = n1 @ w_in[l]
        dn_qkv, dn_a, dn_b, dn_gate, sb_qkv, gate_logits = jnp.split(h, SPLIT_IDX, axis=-1)

        dn_qkv = jax.nn.silu(causal_dwconv(dn_qkv, dn_conv_w[l]))
        dq, dk, dv = jnp.split(dn_qkv, 3, axis=-1)
        dq = l2norm(to_heads(dq, DN_HEADS, DN_HEAD_DIM))
        dk = l2norm(to_heads(dk, DN_HEADS, DN_HEAD_DIM))
        dv = to_heads(dv, DN_HEADS, DN_HEAD_DIM)
        beta = jax.nn.sigmoid(dn_b.astype(jnp.float32)).transpose(0, 2, 1)
        g = (-jnp.exp(dn_A_log[l].astype(jnp.float32))
             * jax.nn.softplus(dn_a.astype(jnp.float32) + dn_dt_bias[l].astype(jnp.float32))).transpose(0, 2, 1)
        o_dn = gated_delta_rule(dq, dk, dv, g, beta)
        o_dn = rmsnorm(o_dn, dn_norm_w[l]).transpose(0, 2, 1, 3)
        o_dn = o_dn * jax.nn.silu(dn_gate.reshape(B, T, DN_HEADS, DN_HEAD_DIM))
        o_dn = o_dn.reshape(B, T, DN_WIDTH)

        sq, sk, sv = jnp.split(sb_qkv, 3, axis=-1)
        o_sb = stick_breaking_attention(to_heads(sq, SB_HEADS, SB_HEAD_DIM),
                                        to_heads(sk, SB_HEADS, SB_HEAD_DIM),
                                        to_heads(sv, SB_HEADS, SB_HEAD_DIM))
        o_sb = o_sb.transpose(0, 2, 1, 3).reshape(B, T, SB_WIDTH)

        gate_dn, gate_sb = jnp.split(jax.nn.sigmoid(gate_logits), 2, axis=-1)
        mixed = gate_dn * (o_dn @ w_proj_dn[l]) + gate_sb * (o_sb @ w_proj_sb[l])
        x = x + mixed @ w_out[l]

        n2 = rmsnorm(x, norm2_w[l])
        u = causal_dwconv(n2 @ ffn_w_up[l], ffn_conv_w[l])
        gate, up = jnp.split(u, 2, axis=-1)
        x = x + (jax.nn.silu(gate) * up) @ ffn_w_down[l]
    return rmsnorm(x, norm_f_w)


_drawn_inputs = setup_inputs


def setup_inputs(seed=0):
    import zlib

    import numpy as np

    out = dict(_drawn_inputs(seed))
    spreads = {}
    factors = {'norm1_w': 3.724, 'dn_norm_w': 8.0, 'norm2_w': 12.62, 'norm_f_w': 8.264}
    for name, (base, spread) in spreads.items():
        noise = np.random.default_rng([zlib.crc32(name.encode()), seed]).standard_normal(out[name].shape)
        drawn = base * np.exp(spread * noise) if base else spread * noise
        out[name] = __import__('jax').numpy.asarray(drawn.astype(out[name].dtype))
    for name, factor in factors.items():
        out[name] = (out[name] * factor).astype(out[name].dtype)
    return out
```

```python
from contextlib import ExitStack

import numpy as np

import concourse.bass as bass
from concourse import mybir

P = 128
F32 = mybir.dt.float32
F32R = mybir.dt.float32r
BF16 = mybir.dt.bfloat16
ALU = mybir.AluOpType
ACT = mybir.ActivationFunctionType

EPS = 1e-6
BIG = 1e30
HEADS = 8
HALF = 512
SLOTS = 64
LEVELS = 7
UNITS = 8


def numbered(names):
    return {name: i + 1 for i, name in enumerate(names)}


def delta_steps():
    two = (0, 1)
    pe = [f"{s}{i}" for s in ("nq", "nk", "g", "v", "k", "kk", "qk", "y") for i in two]
    act = ["sqq", "rq0", "rq1", "rk0", "rk1", "eg0", "eg1", "eD", "eT", "vb0", "vb1", "y0", "y1"]
    dve = ["tab", "cw", "sqk", "csq", "iq0", "q0", "iq1", "q1", "ik0", "k0", "ik1", "k1", "d0", "d1",
           "csk", "kd0", "kd1", "L0", "L1", "at0", "at1", "qg", "cg", "x"]
    for level in range(1, LEVELS):
        pe += [f"P{level}{i}" for i in two] + [f"Y{level}{i}" for i in two]
        act += [f"P{level}{i}" for i in two]
        dve += [f"Y{level}{i}" for i in two]
        if level < LEVELS - 1:
            pe += [f"X{level}{i}" for i in two]
            dve += [f"X{level}{i}" for i in two]
    for n in range(8):
        pe += [f"ks{n}", f"vn{n}", f"ds{n}"]
        dve += ["s_init"] * (n == 0) + [f"r{n}", f"s{n}"]
        act += [f"vn{n}"] + ([f"o{n // 4}"] if n % 4 == 3 else [])
    pe += ["on0", "on1"]
    act += ["sqo", "ro0", "ro1"]
    dve += ["io0", "no0", "fo0", "io1", "no1", "fo1"]
    pool = [f"C{level}" for level in range(LEVELS)]
    return numbered(pe), numbered(act), numbered(dve), numbered(pool)


D_PE, D_ACT, D_DVE, D_POOL = delta_steps()


def attn_steps():
    pe, act, dve = ["v0", "v1"], ["v0", "v1"], []
    for i in range(8):
        rounds = 1 + (i >= 4)
        pe += [f"z{i}"] + [f"t{i}{r}" for r in range(rounds)] + [f"o{i}"]
        act += [f"keep{i}", f"beta{i}"] + ([f"o{i // 4}"] if i % 4 == 3 else [])
        dve += [f"scan{i}", f"a{i}"] + [f"t{i}{r}" for r in range(rounds)]
    return numbered(pe), numbered(act), numbered(dve)


A_PE, A_ACT, A_DVE = attn_steps()

GATE_A, SB_V, DN_V, DN_Q, DN_K, DN_G, SB_Q, SB_K = range(UNITS)
CONVOLVED = (DN_V, DN_Q, DN_K)
SILU = (DN_V, DN_Q, DN_K, DN_G)


def z_slot(i):
    return 9 + 6 * i


def build(nc, x, norm1, w_main, w_ab, conv, a_log, dt_bias, dn_norm, w_proj_dn, w_proj_sb,
          w_out, norm2, w_up, ffn_conv, w_down, norm_f, out, stop_after=9):
    T, D = x.shape[1], x.shape[2]
    KB = D // P
    TB = T // P
    BLOCK = {kind: HEADS * i for i, kind in enumerate((DN_Q, DN_K, DN_V, DN_G, SB_Q, SB_K, SB_V, GATE_A))}
    GATE_B_BLOCK = BLOCK[GATE_A] + KB
    SCALE = float(P) ** -0.5

    gates_d = nc.dram_tensor("gates_d", (2 * KB, P, T), F32).ap()
    o_d = nc.dram_tensor("o_d", (2, HEADS, P, T), F32).ap()

    whole = ExitStack()
    with whole:
        def sem(name, ctx=whole):
            return ctx.enter_context(nc.semaphore(name))

        def sb(name, shape, dt=F32, ctx=whole):
            return ctx.enter_context(nc.sbuf_tensor(name, shape, dt))

        identf = sb("identf", [P, P])
        identb = sb("identb", [P, P], BF16)
        ones = sb("ones", [P, P])
        eps = sb("eps", [P, 1])
        eps_q = sb("eps_q", [P, 1])
        w_raw = [sb(f"w_raw{i}", [P, KB, P]) for i in (0, 1)]
        w_hi = [sb(f"w_hi{i}", [P, KB, P], F32R) for i in (0, 1)]
        w_lo = [sb(f"w_lo{i}", [P, KB, P], F32R) for i in (0, 1)]
        psum = whole.enter_context(nc.psum_tensor("psum", [P, 8, HALF], F32))
        gemm_bank = [psum[:, 0, :], psum[:, 1, :]]

        raw_landed = [sem(f"raw_landed{i}") for i in (0, 1)]
        hi_split = sem("hi_split")
        lo_split = sem("lo_split")
        gemm_halves = sem("gemm_halves")
        gemm_read = sem("gemm_read")

        def load_unit(eng, U, parity, src, raw_wait=True):
            if raw_wait:
                eng.wait_ge(hi_split, U - 1)
                eng.wait_ge(lo_split, U - 1)
            eng.dma_start(w_raw[parity][:, :, :], src).then_inc(raw_landed[parity], 16)

        def split_hi(act, U, parity, landed, free=True):
            act.wait_ge(raw_landed[parity], landed)
            if free:
                act.wait_ge(gemm_halves, 2 * U - 2)
            act.activation(w_hi[parity][:, :, :], w_raw[parity][:, :, :], ACT.Copy).then_inc(hi_split, 1)

        def split_lo(pool, U, parity, free=True):
            pool.wait_ge(hi_split, U + 1)
            if free:
                pool.wait_ge(gemm_halves, 2 * U - 2)
            pool.tensor_tensor(w_lo[parity][:, :, :], w_raw[parity][:, :, :],
                               w_hi[parity][:, :, :].bitcast(F32), ALU.subtract).then_inc(lo_split, 1)

        def unit_products(pe, parity, half, ks, hi, lo):
            cols = slice(half * HALF, (half + 1) * HALF)
            for k in ks:
                for j, (w, a) in enumerate(((w_hi, hi), (w_hi, lo), (w_lo, hi))):
                    mm = pe.matmul(gemm_bank[half], w[parity][:, k, :], a[:, k, cols],
                                   start=(k == 0 and j == 0), stop=(k == KB - 1 and j == 2))
            return mm

        head_ctx = ExitStack()
        with head_ctx:
            def hsb(name, shape, dt=F32):
                return sb(name, shape, dt, head_ctx)

            n1_hi = hsb("n1_hi", [P, KB, T], F32R)
            n1_lo = hsb("n1_lo", [P, KB, T], F32R)
            nq, nk, nv = hsb("nq", [P, T]), hsb("nk", [P, T]), hsb("nv", [P, T])
            ng, nsq, nsk, nsv = hsb("ng", [P, T]), hsb("nsq", [P, T]), hsb("nsk", [P, T]), hsb("nsv", [P, T])
            cq, ck, cg = hsb("cq", [P, T]), hsb("ck", [P, T]), hsb("cg", [P, T])
            csq, csk = hsb("csq", [P, T]), hsb("csk", [P, T])
            dec, decT = hsb("dec", [P, T]), hsb("decT", [P, T])
            X, Y, C, R = hsb("X", [P, T]), hsb("Y", [P, T]), hsb("C", [P, T]), hsb("R", [P, T])
            vb, kd = hsb("vb", [P, T]), hsb("kd", [P, T])
            ob = hsb("ob", [P, T])
            S = hsb("S", [P, P])
            rr, vnew = hsb("rr", [P, P]), hsb("vnew", [P, P])
            keep, beta, aT = hsb("keep", [P, T]), hsb("beta", [P, T]), hsb("aT", [P, TB, P])
            sv = hsb("sv", [P, TB, P])
            ao = hsb("ao", [P, HALF])
            pre = hsb("pre", [P, 3 + T])
            sig = hsb("sig", [P, T])
            G, BETA, NBEG, EGL, EGLAST = range(5)
            tab = hsb("tab", [P, HEADS, 5, TB])
            cur = hsb("cur", [P, 5, TB])
            cwt = hsb("cwt", [P, HEADS, 3, 4])
            cwc = hsb("cwc", [P, 3, 4])
            dnw = hsb("dnw", [P, 1])
            tri = hsb("tri", [P, P])
            pos_mask, neg_mask = hsb("pos_mask", [P, P]), hsb("neg_mask", [P, P])
            z_mask = hsb("z_mask", [P, P], BF16)
            level_mask = hsb("level_mask", [P, LEVELS, P], BF16)

            dbank = [psum[:, 6, :], psum[:, 7, :]]
            z_bank = psum[:, 2:4, :].rearrange("p b n -> p (b n)")
            t_bank, ao_bank = psum[:, 4, :], psum[:, 5, :]

            def conv_tap(v, y, w, half, j, counter, before):
                x_j = pre[:, 3 - j + half * HALF:3 - j + (half + 1) * HALF]
                if j == 0:
                    v.tensor_scalar(y, x_j, w[:, 3:4], None, ALU.mult).then_inc(counter, 1)
                else:
                    v.wait_ge(counter, before)
                    v.scalar_tensor_tensor(out=y, in0=x_j, scalar=w[:, 3 - j:4 - j], in1=y,
                                           op0=ALU.mult, op1=ALU.add).then_inc(counter, 1)

            first = ExitStack()
            with first:
                xs = [X, Y, C, R]
                wab = nsq[:, 0:KB * 2 * HEADS].rearrange("p (k n) -> p k n", k=KB)
                dt_b = nsq[:, 512:520]
                al_b = nsq[:, 520:528]
                y_ab = nsk[:, 0:64].rearrange("p (h n) -> p h n", h=HEADS)
                t1 = nsk[:, 64:128].rearrange("p (h n) -> p h n", h=HEADS)
                t2 = nsk[:, 128:192].rearrange("p (h n) -> p h n", h=HEADS)
                t3 = nsk[:, 192:256].rearrange("p (h n) -> p h n", h=HEADS)
                gstep = nsk[:, 256:320]
                ea = nsk[:, 320:328]
                n1w = nsk[:, 336:344]
                ss = nsk[:, 344:352]
                rstd = nsk[:, 352:360]
                std = nsk[:, 360:368]
                junk = keep

                c_small = sem("c_small", first)
                x_landed = [sem(f"x_landed{i}", first) for i in range(4)]
                masks = sem("masks", first)
                x_ss = sem("x_ss", first)
                x_std = sem("x_std", first)
                x_rstd = sem("x_rstd", first)
                x_norm = sem("x_norm", first)
                x_turned = sem("x_turned", first)
                n_hi = sem("n_hi", first)
                n_lo = sem("n_lo", first)
                ab_sum = sem("ab_sum", first)
                tab_act = sem("tab_act", first)
                tab_dve = sem("tab_dve", first)
                pad = sem("pad", first)
                gate_out = sem("gate_out0", first)
                conv0 = sem("conv0", first)
                sig0 = sem("sig0", first)
                silu0 = sem("silu0", first)

                with nc.Block() as block:
                    @block.sync
                    def _(sp):
                        for i in range(4):
                            sp.dma_start(xs[i][:, :], x[0, i * P:(i + 1) * P, :]).then_inc(x_landed[i], 16)
                        sp.dma_start(n1w, norm1).then_inc(c_small, 16)
                        sp.dma_start(wab, w_ab).then_inc(c_small, 16)
                        sp.dma_start(dt_b, dt_bias[0:1, :].to_broadcast([P, HEADS])).then_inc(c_small, 16)
                        sp.dma_start(al_b, a_log[0:1, :].to_broadcast([P, HEADS])).then_inc(c_small, 16)
                        sp.dma_start(dnw[:, :], dn_norm).then_inc(c_small, 16)
                        sp.dma_start(cwt[:, :, :, :], conv).then_inc(c_small, 16)
                        for U in range(2):
                            load_unit(sp, U, U % 2, w_main[BLOCK[U]], raw_wait=False)
                        for i in range(4, TB):
                            sp.wait_ge(x_turned, 8)
                            sp.dma_start(xs[i % 4][:, :], x[0, i * P:(i + 1) * P, :]).then_inc(x_landed[i % 4], 16)
                        for U in range(2, UNITS):
                            load_unit(sp, U, U % 2, w_main[BLOCK[U]])
                            if U == 3:
                                for half in (0, 1):
                                    sp.wait_ge(gemm_read, half + 1)
                                    sp.dma_start(gates_d[0][:, half * HALF:(half + 1) * HALF],
                                                 sig[:, half * HALF:(half + 1) * HALF]).then_inc(gate_out, 16)
                        sp.wait_ge(gate_out, 32)

                    @block.gpsimd
                    def _(pool):
                        count = [0]

                        def done(ins):
                            count[0] += 1
                            ins.then_inc(masks, 1)
                            pool.wait_ge(masks, count[0])

                        g = nc.gpsimd
                        done(g.memset(identf[:, :], 0.0))
                        done(g.affine_select(out=identf[:, :], in_=identf[:, :], compare_op=ALU.not_equal,
                                             fill=1.0, base=0, pattern=[[-1, P]], channel_multiplier=1))
                        done(g.memset(ones[:, :], 1.0))
                        done(g.memset(eps[:, :], EPS))
                        done(g.memset(eps_q[:, :], EPS * P))
                        done(g.affine_select(out=tri[:, :], in_=ones[:, :], compare_op=ALU.is_ge,
                                             fill=0.0, base=0, pattern=[[1, P]], channel_multiplier=-1))
                        done(g.memset(pos_mask[:, :], 0.0))
                        done(g.affine_select(out=pos_mask[:, :], in_=pos_mask[:, :], compare_op=ALU.is_gt,
                                             fill=BIG, base=0, pattern=[[-1, P]], channel_multiplier=1))
                        done(g.memset(neg_mask[:, :], 0.0))
                        done(g.affine_select(out=neg_mask[:, :], in_=neg_mask[:, :], compare_op=ALU.is_ge,
                                             fill=-BIG, base=0, pattern=[[1, P]], channel_multiplier=-1))
                        done(g.tensor_copy(identb[:, :], identf[:, :]))
                        done(g.memset(z_mask[:, :], 0.0))
                        done(g.affine_select(out=z_mask[:, :], in_=z_mask[:, :], compare_op=ALU.is_gt,
                                             fill=-BIG, base=0, pattern=[[-1, P]], channel_multiplier=1))
                        for level in range(LEVELS):
                            s = 1 << level
                            m = level_mask[:, level, :].rearrange("p (b r) -> p b r", r=2 * s)
                            nb = P // (2 * s)
                            one = ones[:, :].rearrange("p (b r) -> p b r", r=2 * s)
                            done(g.affine_select(out=m, in_=one, compare_op=ALU.is_ge, fill=0.0, base=s - 1,
                                                 pattern=[[0, nb], [-1, 2 * s]], channel_multiplier=0))
                            done(g.affine_select(out=m, in_=m, compare_op=ALU.is_ge, fill=0.0, base=-s,
                                                 pattern=[[-2 * s, nb], [0, 2 * s]], channel_multiplier=1))
                            done(g.affine_select(out=m, in_=m, compare_op=ALU.is_ge, fill=0.0, base=2 * s - 1,
                                                 pattern=[[2 * s, nb], [0, 2 * s]], channel_multiplier=-1))
                        for U in range(UNITS + 1):
                            if U < UNITS:
                                split_lo(pool, U, U % 2, free=U >= 2)
                            for half in (0, 1):
                                n = 2 * (U - 2) + half
                                if U - 2 in SILU:
                                    y = {DN_V: nv, DN_Q: nq, DN_K: nk, DN_G: ng}[U - 2][:, half * HALF:(half + 1) * HALF]
                                    pool.wait_ge(sig0, 2 * (U - 2 - DN_V) + half + 1)
                                    pool.tensor_tensor(y, y, sig[:, half * HALF:(half + 1) * HALF],
                                                       ALU.mult).then_inc(silu0, 1)

                    @block.tensor
                    def _(pe):
                        pe.wait_ge(masks, 2)
                        for i2 in (0, 1):
                            pe.wait_ge(x_norm, 4 * i2 + 4)
                            for k in range(KB):
                                n = KB * i2 + k
                                bank = psum[:, 2 + k % 4, :]
                                if n >= 4:
                                    pe.wait_ge(n_lo, n - 3)
                                for i in range(4):
                                    tr = pe.transpose(bank[:, i * P:(i + 1) * P], xs[i][:, k * P:(k + 1) * P], identf[:, :])
                                tr.then_inc(x_turned, 1)
                        pe.wait_ge(c_small, 16 * 6)
                        pe.wait_ge(n_lo, 16)
                        for i in range(TB):
                            for k in range(KB):
                                for j, a in enumerate((n1_hi, n1_lo)):
                                    mm = pe.matmul(psum[:, 6, 16 * i:16 * i + 16], a[:, k, i * P:(i + 1) * P].bitcast(F32),
                                                   wab[:, k, :], start=(k == 0 and j == 0), stop=(k == KB - 1 and j == 1))
                        mm.then_inc(ab_sum, 1)

                        def unit(U):
                            pe.wait_ge(hi_split, U + 1)
                            pe.wait_ge(lo_split, U + 1)
                            for half in (0, 1):
                                if U:
                                    pe.wait_ge(gemm_read, 2 * U + half - 1)
                                unit_products(pe, U % 2, half, range(KB), n1_hi, n1_lo).then_inc(gemm_halves, 1)

                        unit(0)
                        pe.wait_ge(tab_dve, 5)
                        pe.wait_ge(masks, 6)
                        pe.matmul(psum[:, 7, 0:64], tri[:, :], gstep, start=True, stop=True)
                        pe.matmul(psum[:, 7, 64:128], ones[:, :], gstep, start=True, stop=True).then_inc(ab_sum, 1)
                        for U in range(1, UNITS):
                            unit(U)

                    @block.scalar
                    def _(act):
                        for i in range(TB):
                            act.wait_ge(x_landed[i % 4], 16 * (1 + i // 4))
                            if i:
                                act.wait_ge(x_ss, i)
                            act.activation(junk[:, :], xs[i % 4][:, :], ACT.Square,
                                           accum_out=ss[:, i:i + 1]).then_inc(x_ss, 1)
                            if i == 0:
                                act.wait_ge(masks, 4)
                            act.wait_ge(x_ss, i + 1)
                            act.activation(std[:, i:i + 1], ss[:, i:i + 1], ACT.Sqrt, bias=eps[:, :],
                                           scale=1.0 / D).then_inc(x_std, 1)
                            act.wait_ge(x_rstd, i + 1)
                            act.activation(xs[i % 4][:, :], xs[i % 4][:, :], ACT.Copy,
                                           scale=rstd[:, i:i + 1]).then_inc(x_norm, 1)
                            if i % 4 == 3:
                                act.wait_ge(c_small, 16 * 6)
                                for k in range(KB):
                                    n = KB * (i // 4) + k
                                    act.wait_ge(x_turned, n + 1)
                                    act.activation(n1_hi[:, k, (i // 4) * HALF:(i // 4 + 1) * HALF], psum[:, 2 + k % 4, :],
                                                   ACT.Copy, scale=n1w[:, k:k + 1]).then_inc(n_hi, 1)
                        split_hi(act, 0, 0, 16, free=False)
                        split_hi(act, 1, 1, 16, free=False)
                        act.wait_ge(tab_dve, 3)
                        act.activation(t2, t1, ACT.Exp).then_inc(tab_act, 1)
                        act.activation(ea, al_b, ACT.Exp).then_inc(tab_act, 1)
                        act.wait_ge(tab_act, 1)
                        act.wait_ge(masks, 3)
                        act.activation(t3, t2, ACT.Ln, bias=ones[:, 0:1]).then_inc(tab_act, 1)
                        act.wait_ge(tab_dve, 7)
                        act.activation(t2, tab[:, :, G, :], ACT.Exp).then_inc(tab_act, 1)
                        act.activation(tab[:, :, EGL, :], t1, ACT.Exp).then_inc(tab_act, 1)
                        act.activation(tab[:, :, EGLAST, :],
                                       psum[:, 7, 64:128].rearrange("p (h n) -> p h n", h=HEADS),
                                       ACT.Exp).then_inc(tab_act, 1)
                        act.activation(tab[:, :, BETA, :],
                                       psum[:, 6, 0:128].rearrange("p (n c) -> p c n", n=TB)[:, HEADS:, :],
                                       ACT.Sigmoid).then_inc(tab_act, 1)
                        for U in range(UNITS):
                            if 1 <= U < UNITS - 1:
                                split_hi(act, U + 1, (U + 1) % 2, 16 * ((U + 1) // 2 + 1), free=True)
                            for half in (0, 1):
                                cols = slice(half * HALF, (half + 1) * HALF)
                                act.wait_ge(gemm_halves, 2 * U + half + 1)
                                if (U, half) == (SB_K, 1):
                                    continue
                                if U == GATE_A:
                                    act.activation(sig[:, cols], gemm_bank[half], ACT.Sigmoid).then_inc(gemm_read, 1)
                                elif U in CONVOLVED:
                                    if U > DN_V:
                                        act.wait_ge(conv0, 8 * (U - DN_V))
                                    else:
                                        act.wait_ge(pad, 1)
                                    act.activation(pre[:, 3 + half * HALF:3 + (half + 1) * HALF], gemm_bank[half],
                                                   ACT.Copy).then_inc(gemm_read, 1)
                                else:
                                    dst = {SB_V: nsv, SB_Q: nsq, SB_K: nsk, DN_G: ng}[U]
                                    if U in (SB_Q, SB_K):
                                        act.wait_ge(tab_act, 7)
                                        act.wait_ge(tab_dve, 8)
                                    act.activation(dst[:, cols], gemm_bank[half], ACT.Copy).then_inc(gemm_read, 1)
                            if U in SILU:
                                for half in (0, 1):
                                    cols = slice(half * HALF, (half + 1) * HALF)
                                    y = {DN_V: nv, DN_Q: nq, DN_K: nk, DN_G: ng}[U]
                                    if U == DN_V:
                                        act.wait_ge(gate_out, 32)
                                    else:
                                        act.wait_ge(silu0, 2 * (U - DN_V - 1) + half + 1)
                                    if U in CONVOLVED:
                                        act.wait_ge(conv0, 8 * (U - DN_V) + 4 * half + 4)
                                    else:
                                        act.wait_ge(gemm_read, 2 * U + half + 1)
                                    act.activation(sig[:, cols], y[:, cols], ACT.Sigmoid).then_inc(sig0, 1)

                    @block.vector
                    def _(v):
                        v.memset(pre[:, 0:3], 0.0).then_inc(pad, 1)
                        for i in range(TB):
                            v.wait_ge(x_std, i + 1)
                            v.reciprocal(rstd[:, i:i + 1], std[:, i:i + 1]).then_inc(x_rstd, 1)
                            if i % 4 == 3:
                                for k in range(KB):
                                    n = KB * (i // 4) + k
                                    cols = slice((i // 4) * HALF, (i // 4 + 1) * HALF)
                                    v.wait_ge(n_hi, n + 1)
                                    v.scalar_tensor_tensor(out=n1_lo[:, k, cols], in0=psum[:, 2 + k % 4, :],
                                                           scalar=n1w[:, k:k + 1], in1=n1_hi[:, k, cols].bitcast(F32),
                                                           op0=ALU.mult, op1=ALU.subtract).then_inc(n_lo, 1)
                        ab = psum[:, 6, 0:128].rearrange("p (n c) -> p c n", n=TB)
                        v.wait_ge(ab_sum, 1)
                        v.tensor_tensor(y_ab, ab[:, 0:HEADS, :], dt_b.unsqueeze(2).to_broadcast([P, HEADS, TB]),
                                        ALU.add).then_inc(tab_dve, 1)
                        v.wait_ge(tab_dve, 1)
                        v.tensor_scalar(t1, y_ab, -1.0, None, ALU.mult).then_inc(tab_dve, 1)
                        v.wait_ge(tab_dve, 2)
                        v.tensor_tensor(t1, t1, y_ab, ALU.min).then_inc(tab_dve, 1)
                        v.wait_ge(tab_act, 3)
                        v.scalar_tensor_tensor(out=y_ab, in0=y_ab, scalar=0.0, in1=t3, op0=ALU.max,
                                               op1=ALU.add).then_inc(tab_dve, 1)
                        v.wait_ge(tab_dve, 4)
                        v.scalar_tensor_tensor(out=gstep.rearrange("p (h n) -> p h n", h=HEADS), in0=y_ab, scalar=-1.0,
                                               in1=ea.unsqueeze(2).to_broadcast([P, HEADS, TB]), op0=ALU.mult,
                                               op1=ALU.mult).then_inc(tab_dve, 1)
                        v.wait_ge(ab_sum, 2)
                        v.tensor_copy(tab[:, :, G, :], psum[:, 7, 0:64].rearrange("p (h n) -> p h n", h=HEADS)).then_inc(tab_dve, 1)
                        v.wait_ge(tab_dve, 6)
                        v.tensor_tensor(t1, psum[:, 7, 64:128].rearrange("p (h n) -> p h n", h=HEADS),
                                        tab[:, :, G, :], ALU.subtract).then_inc(tab_dve, 1)
                        v.wait_ge(tab_act, 7)
                        v.scalar_tensor_tensor(out=tab[:, :, NBEG, :], in0=tab[:, :, BETA, :], scalar=-1.0, in1=t2,
                                               op0=ALU.mult, op1=ALU.mult).then_inc(tab_dve, 1)
                        for u in CONVOLVED:
                            for half in (0, 1):
                                v.wait_ge(gemm_read, 2 * u + half + 1)
                                y = {DN_V: nv, DN_Q: nq, DN_K: nk}[u][:, half * HALF:(half + 1) * HALF]
                                w = cwt[:, 0, {DN_Q: 0, DN_K: 1, DN_V: 2}[u], :]
                                for j in range(4):
                                    conv_tap(v, y, w, half, j, conv0, (8 * (u - DN_V) + 4 * half + j) if j else None)

            if stop_after >= 2:
              loop = ExitStack()
              with loop:
                delta_products = sem("delta_products", loop)
                delta_act = sem("delta_act", loop)
                delta_vec = sem("delta_vec", loop)
                delta_pool = sem("delta_pool", loop)
                attn_products = sem("attn_products", loop)
                attn_act = sem("attn_act", loop)
                attn_vec = sem("attn_vec", loop)
                conv_taps = sem("conv_taps", loop)
                sigmoids = sem("sigmoids", loop)
                silus = sem("silus", loop)
                gate_stored = [sem(f"gate_stored{i}", loop) for i in (0, 1)]
                ao_stored = sem("ao_stored", loop)
                ob_stored = sem("ob_stored", loop)

                def d(h, table, step):
                    return h * len(table) + table[step]

                def chunk(n):
                    return slice(n * P, (n + 1) * P)

                def halves(i):
                    return slice(i * HALF, (i + 1) * HALF)

                def col(table, n):
                    return cur[:, table, n:n + 1]

                def pe_delta(pe, h, t):
                    def four(i, step, lhs, rhs, waits):
                        for s_, value in waits:
                            pe.wait_ge(s_, value)
                        for q in range(4):
                            n = 4 * i + q
                            mm = pe.matmul(dbank[i][:, chunk(q)], lhs(n), rhs(n), start=True, stop=True)
                        mm.then_inc(delta_products, 1)

                    def turn(i, src, waits):
                        for s_, value in waits:
                            pe.wait_ge(s_, value)
                        for q in range(4):
                            tr = pe.transpose(dbank[i][:, chunk(q)], src(4 * i + q), identf[:, :])
                        tr.then_inc(delta_products, 1)

                    if t == 1:
                        pe.wait_ge(delta_act, d(h, D_ACT, "sqq"))
                        for i in (0, 1):
                            pe.matmul(dbank[i], ones[:, :], X[:, halves(i)], start=True, stop=True).then_inc(delta_products, 1)
                    if t == 2:
                        pe.wait_ge(delta_vec, d(h, D_DVE, "sqk"))
                        for i in (0, 1):
                            pe.wait_ge(delta_act, d(h, D_ACT, f"rq{i}"))
                            pe.matmul(dbank[i], ones[:, :], Y[:, halves(i)], start=True, stop=True).then_inc(delta_products, 1)
                    if t == 3:
                        for i in (0, 1):
                            turn(i, lambda n: col(G, n).to_broadcast([P, P]),
                                 [(delta_act, d(h, D_ACT, f"rk{i}")), (delta_vec, d(h, D_DVE, "tab"))])
                    if t == 4:
                        for i in (0, 1):
                            turn(i, lambda n: nv[:, chunk(n)],
                                 [(delta_vec, d(h, D_DVE, f"d{i}")), (delta_act, d(h, D_ACT, f"eg{i}"))])
                    if t == 5:
                        for i in (0, 1):
                            turn(i, lambda n: ck[:, chunk(n)],
                                 [(delta_act, d(h, D_ACT, f"vb{i}")), (delta_vec, d(h, D_DVE, f"k{i}"))])
                    if t == 6:
                        for i in (0, 1):
                            four(i, "kk", lambda n: ck[:, chunk(n)], lambda n: ck[:, chunk(n)],
                                 [(delta_vec, d(h, D_DVE, f"kd{i}"))])
                    if t == 7:
                        for i in (0, 1):
                            four(i, "qk", lambda n: ck[:, chunk(n)], lambda n: cq[:, chunk(n)],
                                 [(delta_vec, d(h, D_DVE, f"L{i}"))])
                    if t == 9:
                        for i in (0, 1):
                            turn(i, lambda n: X[:, chunk(n)],
                                 [(delta_vec, d(h, D_DVE, "x"))])
                    if 10 <= t < 10 + 3 * (LEVELS - 1) and (t - 10) // 3 < LEVELS - 1:
                        level, part = 1 + (t - 10) // 3, (t - 10) % 3
                        for i in (0, 1):
                            if part == 0:
                                if level == 1:
                                    ready = [(delta_act, d(h, D_ACT, f"y{i}"))]
                                else:
                                    ready = [(delta_vec, d(h, D_DVE, f"X{level - 1}{i}"))]
                                four(i, "P", lambda n: C[:, chunk(n)], lambda n: Y[:, chunk(n)],
                                     ready + [(delta_pool, d(h, D_POOL, f"C{level}"))])
                            if part == 1:
                                four(i, "Y", lambda n: X[:, chunk(n)], lambda n: R[:, chunk(n)],
                                     [(delta_act, d(h, D_ACT, f"P{level}{i}"))])
                            if part == 2 and level < LEVELS - 1:
                                four(i, "X", lambda n: R[:, chunk(n)], lambda n: X[:, chunk(n)],
                                     [(delta_vec, d(h, D_DVE, f"Y{level}{i}"))])
                    if 27 <= t < 51:
                        n, part = (t - 27) // 3, (t - 27) % 3
                        if part == 0:
                            pe.wait_ge(delta_vec, d(h, D_DVE, f"s{n - 1}" if n else "s_init"))
                            pe.matmul(dbank[1][:, chunk(0)], ck[:, chunk(n)], S[:, :], start=True,
                                      stop=True).then_inc(delta_products, 1)
                        if part == 1:
                            pe.wait_ge(delta_vec, d(h, D_DVE, f"r{n}"))
                            pe.matmul(dbank[1][:, chunk(1)], Y[:, chunk(n)], rr[:, :], start=True,
                                      stop=True).then_inc(delta_products, 1)
                        if part == 2:
                            pe.wait_ge(delta_act, d(h, D_ACT, f"vn{n}"))
                            if n == 4:
                                pe.wait_ge(delta_act, d(h, D_ACT, "o0"))
                            bank = dbank[0][:, chunk(n % 4)]
                            pe.matmul(bank, S[:, :], cq[:, chunk(n)], start=True, stop=False)
                            pe.matmul(bank, vnew[:, :], decT[:, chunk(n)], start=False, stop=True)
                            pe.matmul(dbank[1][:, chunk(2)], kd[:, chunk(n)], vnew[:, :], start=True,
                                      stop=True).then_inc(delta_products, 1)
                    if t == 57:
                        pe.wait_ge(delta_act, d(h, D_ACT, "sqo"))
                        pe.wait_ge(delta_vec, d(h, D_DVE, "s7"))
                        for i in (0, 1):
                            pe.matmul(dbank[i], ones[:, :], R[:, halves(i)], start=True, stop=True).then_inc(delta_products, 1)

                def pe_attn(pe, h, t):
                    if t in (5, 6):
                        i = t - 5
                        if i:
                            pe.wait_ge(attn_act, d(h, A_ACT, "v0"))
                        for q in range(4):
                            tr = pe.transpose(t_bank[:, chunk(q)], nsv[:, chunk(4 * i + q)], identf[:, :])
                        tr.then_inc(attn_products, 1)
                    for i in range(TB):
                        w = (i + 1) * P
                        if t == z_slot(i):
                            pe.wait_ge(delta_vec, d(h, D_DVE, "csk"))
                            if i:
                                pe.wait_ge(attn_act, d(h, A_ACT, f"beta{i - 1}"))
                            for lo in range(0, w, HALF):
                                hi = min(w, lo + HALF)
                                pe.matmul(z_bank[:, lo:hi], csq[:, chunk(i)], csk[:, lo:hi], start=True, stop=True)
                            pe.matmul(z_bank[:, w - P:w], identb[:, :], z_mask[:, :], start=False, stop=True,
                                      skip_group_check=True).then_inc(attn_products, 1)
                        for r in range(1 + (i >= 4)):
                            if t == z_slot(i) + 3 + r:
                                pe.wait_ge(attn_vec, d(h, A_DVE, f"a{i}"))
                                if r:
                                    pe.wait_ge(attn_vec, d(h, A_DVE, f"t{i}0"))
                                for j in range(4 * r, min(4 * r + 4, i + 1)):
                                    tr = pe.transpose(t_bank[:, chunk(j % 4)], beta[:, chunk(j)], identf[:, :])
                                tr.then_inc(attn_products, 1)
                        if t == z_slot(i) + 5:
                            pe.wait_ge(attn_vec, d(h, A_DVE, f"t{i}{int(i >= 4)}"))
                            if i == 4:
                                pe.wait_ge(attn_act, d(h, A_ACT, "o0"))
                            for j in range(i + 1):
                                mm = pe.matmul(ao_bank[:, chunk(i % 4)], sv[:, j, :], aT[:, j, :],
                                               start=(j == 0), stop=(j == i))
                            mm.then_inc(attn_products, 1)

                def pe_gemm(pe, h, t):
                    u, half, part = t // 8, t % 8 // 4, t % 4
                    U = h * UNITS + UNITS + u
                    if part == 0:
                        pe.wait_ge(gemm_read, 2 * U + half - 1)
                        if half == 0:
                            pe.wait_ge(hi_split, U + 1)
                            pe.wait_ge(lo_split, U + 1)
                    mm = unit_products(pe, u % 2, half, (2 * part, 2 * part + 1), n1_hi, n1_lo)
                    if part == 3:
                        mm.then_inc(gemm_halves, 1)

                def act_delta(act, h, t):
                    def out(dst, src, func=ACT.Copy, **kw):
                        return act.activation(dst, src, func, **kw)

                    if t == 0:
                        out(X[:, :], nq[:, :], ACT.Square).then_inc(delta_act, 1)
                    if t == 1:
                        for i in (0, 1):
                            act.wait_ge(delta_products, d(h, D_PE, f"nq{i}"))
                            out(R[:, halves(i)], dbank[i], ACT.Sqrt, bias=eps_q[:, :], scale=float(P)).then_inc(delta_act, 1)
                    if t == 2:
                        for i in (0, 1):
                            act.wait_ge(delta_products, d(h, D_PE, f"nk{i}"))
                            out(C[:, halves(i)], dbank[i], ACT.Sqrt, bias=eps[:, :]).then_inc(delta_act, 1)
                    if t == 3:
                        for i in (0, 1):
                            act.wait_ge(delta_products, d(h, D_PE, f"g{i}"))
                            act.wait_ge(delta_vec, d(h, D_DVE, f"q{i}"))
                            out(R[:, halves(i)], dbank[i], ACT.Exp).then_inc(delta_act, 1)
                        act.wait_ge(delta_vec, d(h, D_DVE, "d1"))
                        out(dec[:, :], dec[:, :], ACT.Exp, scale=-1.0).then_inc(delta_act, 1)
                        out(decT[:, :], decT[:, :], ACT.Exp).then_inc(delta_act, 1)
                    if t == 4:
                        for i in (0, 1):
                            act.wait_ge(delta_products, d(h, D_PE, f"v{i}"))
                            for q in range(4):
                                n = 4 * i + q
                                last = out(vb[:, chunk(n)], dbank[i][:, chunk(q)], scale=col(BETA, n))
                            last.then_inc(delta_act, 1)
                    if t == 9:
                        for i in (0, 1):
                            act.wait_ge(delta_products, d(h, D_PE, f"y{i}"))
                            out(Y[:, halves(i)], dbank[i]).then_inc(delta_act, 1)
                    if 10 <= t < 10 + 3 * (LEVELS - 1) and (t - 10) % 3 == 0:
                        level = 1 + (t - 10) // 3
                        for i in (0, 1):
                            act.wait_ge(delta_products, d(h, D_PE, f"P{level}{i}"))
                            if level == 1:
                                act.wait_ge(delta_vec, d(h, D_DVE, "qg"))
                            out(R[:, halves(i)], dbank[i]).then_inc(delta_act, 1)
                    if 27 <= t < 51:
                        n, part = (t - 27) // 3, (t - 27) % 3
                        if part == 1:
                            act.wait_ge(delta_products, d(h, D_PE, f"vn{n}"))
                            out(vnew[:, :], dbank[1][:, chunk(1)]).then_inc(delta_act, 1)
                        if part == 2 and n % 4 == 3:
                            act.wait_ge(delta_products, d(h, D_PE, f"ds{n}"))
                            if n == 3:
                                act.wait_ge(ob_stored, h * 32)
                            out(ob[:, halves(n // 4)], dbank[0]).then_inc(delta_act, 1)
                    if t == 56:
                        act.wait_ge(delta_act, d(h, D_ACT, "o1"))
                        out(R[:, :], ob[:, :], ACT.Square).then_inc(delta_act, 1)
                    if t == 57:
                        for i in (0, 1):
                            act.wait_ge(delta_products, d(h, D_PE, f"on{i}"))
                            out(C[:, halves(i)], dbank[i], ACT.Sqrt, bias=eps[:, :], scale=1.0 / P).then_inc(delta_act, 1)
                    if t == 61:
                        for i in (0, 1):
                            act.wait_ge(delta_vec, d(h, D_DVE, f"fo{i}"))
                            act.dma_start(o_d[0][bass.ds(h, 1), :, halves(i)].rearrange("o p n -> (o p) n"),
                                          ob[:, halves(i)]).then_inc(ob_stored, 16)

                def act_attn(act, h, t):
                    if t in (5, 6):
                        i = t - 5
                        act.wait_ge(attn_products, d(h, A_PE, f"v{i}"))
                        act.activation(sv[:, 4 * i:4 * i + 4, :], t_bank, ACT.Copy).then_inc(attn_act, 1)
                    for i in range(TB):
                        w = (i + 1) * P
                        if t == z_slot(i):
                            act.wait_ge(attn_products, d(h, A_PE, f"z{i}"))
                            if i:
                                act.wait_ge(attn_products, d(h, A_PE, f"t{i - 1}{int(i > 4)}"))
                            act.activation(keep[:, 0:w], z_bank[:, 0:w], ACT.Sigmoid, scale=-SCALE).then_inc(attn_act, 1)
                            act.activation(beta[:, 0:w], z_bank[:, 0:w], ACT.Sigmoid, scale=SCALE).then_inc(attn_act, 1)
                        if t == z_slot(i) + 5 and i % 4 == 3:
                            act.wait_ge(attn_products, d(h, A_PE, f"o{i}"))
                            act.wait_ge(ao_stored, h * 32 + (i // 4) * 16)
                            act.activation(ao[:, :], ao_bank, ACT.Copy).then_inc(attn_act, 1)
                            act.wait_ge(attn_act, d(h, A_ACT, f"o{i // 4}"))
                            act.dma_start(o_d[1][bass.ds(h, 1), :, halves(i // 4)].rearrange("o p n -> (o p) n"),
                                          ao[:, :]).then_inc(ao_stored, 16)

                def half_before(t, slots):
                    return (t - slots) // 4 // 2, (t - slots) // 4 % 2

                def act_gemm(act, h, t, last):
                    U0 = h * UNITS + UNITS
                    if t % 4 == 0:
                        u, half = half_before(t, 4) if t else (SB_K, 1)
                        act.wait_ge(gemm_halves, 2 * U0 + t // 4)
                        if last and t:
                            gate(act, u, half, bass_gate(KB + u), h)
                        elif u == GATE_A:
                            gate(act, u, half, None, h)
                        elif u in CONVOLVED:
                            if half == 0:
                                act.wait_ge(conv_taps, h * 24 + 8 * (u - DN_V))
                            act.activation(pre[:, 3 + half * HALF:3 + (half + 1) * HALF], gemm_bank[half],
                                           ACT.Copy).then_inc(gemm_read, 1)
                        else:
                            dst = {SB_V: nsv, SB_Q: nsq, SB_K: nsk, DN_G: ng}[u]
                            if u == SB_V:
                                act.wait_ge(attn_products, d(h, A_PE, "v1"))
                            if u == DN_G:
                                act.wait_ge(delta_vec, d(h, D_DVE, "cg"))
                            if u == SB_Q:
                                act.wait_ge(delta_vec, d(h, D_DVE, "csk"))
                            act.activation(dst[:, halves(half)], gemm_bank[half], ACT.Copy).then_inc(gemm_read, 1)
                    if t % 8 == 1 and not (last and t // 8 == UNITS - 1):
                        u = t // 8 + 1
                        split_hi(act, U0 + u, u % 2, 16 * (4 * h + 4 + u // 2 + 1))
                    if t % 4 == 2 and t >= 6 and not last:
                        u, half = half_before(t, 8) if t >= 8 else (0, 0)
                        if t >= 8 and u in SILU:
                            n = 2 * (u - DN_V) + half
                            if u in CONVOLVED:
                                act.wait_ge(conv_taps, h * 24 + 4 * n + 4)
                            else:
                                act.wait_ge(gemm_read, 2 * (U0 + u) + half + 1)
                            if n >= 2:
                                act.wait_ge(silus, h * 8 + n - 1)
                            else:
                                act.wait_ge(gate_stored[half], h * 16 + 16)
                            y = {DN_V: nv, DN_Q: nq, DN_K: nk, DN_G: ng}[u]
                            act.activation(sig[:, halves(half)], y[:, halves(half)], ACT.Sigmoid).then_inc(sigmoids, 1)

                def bass_gate(m):
                    return m

                def gate(act, u, half, row, h):
                    if row is None:
                        if half == 0:
                            act.wait_ge(silus, h * 8)
                        dst = gates_d[bass.ds(h + 1, 1), :, halves(half)].rearrange("o p n -> (o p) n")
                        U = h * UNITS + UNITS
                    else:
                        act.wait_ge(gate_stored[half], 16 * (HEADS - 1 + u))
                        dst = gates_d[row][:, halves(half)]
                        U = h * UNITS + UNITS + u
                    act.activation(sig[:, halves(half)], gemm_bank[half], ACT.Sigmoid).then_inc(gemm_read, 1)
                    act.wait_ge(gemm_read, 2 * U + half + 1)
                    act.dma_start(dst, sig[:, halves(half)]).then_inc(gate_stored[half], 16)

                def vec_delta(v, h, t):
                    if t == 0:
                        v.tensor_copy(cur[:, :, :], tab[:, bass.ds(h, 1), :, :].rearrange("p o a n -> p (o a) n")).then_inc(delta_vec, 1)
                        v.tensor_copy(cwc[:, :, :], cwt[:, bass.ds(cw_head(h), 1), :, :].rearrange("p o a n -> p (o a) n")).then_inc(delta_vec, 1)
                        v.tensor_tensor(Y[:, :], nk[:, :], nk[:, :], ALU.mult).then_inc(delta_vec, 1)
                        v.wait_ge(gemm_read, 2 * (h * UNITS + UNITS))
                        v.tensor_copy(csq[:, :], nsq[:, :]).then_inc(delta_vec, 1)
                    if t == 4:
                        v.tensor_copy(csk[:, :], nsk[:, :]).then_inc(delta_vec, 1)
                    if t == 8:
                        v.tensor_copy(cg[:, :], ng[:, :]).then_inc(delta_vec, 1)
                    if t in (1, 2):
                        s, cs, ns, room = (("q", cq, nq, R), ("k", ck, nk, C))[t - 1]
                        for i in (0, 1):
                            v.wait_ge(delta_act, d(h, D_ACT, f"r{s}{i}"))
                            v.reciprocal(room[:, halves(i)], room[:, halves(i)]).then_inc(delta_vec, 1)
                            v.wait_ge(delta_vec, d(h, D_DVE, f"i{s}{i}"))
                            v.tensor_tensor(cs[:, halves(i)], ns[:, halves(i)], room[:, halves(i)], ALU.mult).then_inc(delta_vec, 1)
                    if t == 3:
                        for i in (0, 1):
                            v.wait_ge(delta_act, d(h, D_ACT, f"eg{i}"))
                            for q in range(4):
                                n = 4 * i + q
                                v.scalar_tensor_tensor(out=dec[:, chunk(n)], in0=dbank[i][:, chunk(q)], scalar=col(G, n),
                                                       in1=pos_mask[:, :], op0=ALU.subtract, op1=ALU.max)
                                last = v.scalar_tensor_tensor(out=decT[:, chunk(n)], in0=dbank[i][:, chunk(q)], scalar=col(G, n),
                                                              in1=neg_mask[:, :], op0=ALU.subtract, op1=ALU.min)
                            last.then_inc(delta_vec, 1)
                    if t == 5:
                        for i in (0, 1):
                            v.wait_ge(delta_products, d(h, D_PE, f"k{i}"))
                            for q in range(4):
                                n = 4 * i + q
                                last = v.tensor_scalar(kd[:, chunk(n)], dbank[i][:, chunk(q)], col(EGL, n), None, ALU.mult)
                            last.then_inc(delta_vec, 1)
                    if t == 6:
                        v.wait_ge(delta_act, d(h, D_ACT, "eD"))
                        for i in (0, 1):
                            v.wait_ge(delta_products, d(h, D_PE, f"kk{i}"))
                            for q in range(4):
                                n = 4 * i + q
                                last = v.scalar_tensor_tensor(out=dec[:, chunk(n)], in0=dbank[i][:, chunk(q)], scalar=col(BETA, n),
                                                              in1=dec[:, chunk(n)], op0=ALU.mult, op1=ALU.mult)
                            last.then_inc(delta_vec, 1)
                    if t == 7:
                        v.wait_ge(delta_act, d(h, D_ACT, "eT"))
                        for i in (0, 1):
                            v.wait_ge(delta_products, d(h, D_PE, f"qk{i}"))
                            v.tensor_tensor(decT[:, halves(i)], dbank[i], decT[:, halves(i)], ALU.mult).then_inc(delta_vec, 1)
                        v.tensor_tensor(cq[:, :], cq[:, :], R[:, :], ALU.mult).then_inc(delta_vec, 1)
                    if t == 8:
                        v.wait_ge(delta_pool, d(h, D_POOL, "C0"))
                        v.tensor_tensor(X[:, :].rearrange("p (n c) -> p n c", n=TB),
                                        identf[:, :].unsqueeze(1).to_broadcast([P, TB, P]),
                                        C[:, :].rearrange("p (n c) -> p n c", n=TB), ALU.subtract).then_inc(delta_vec, 1)
                    if 10 <= t < 10 + 3 * (LEVELS - 1) and (t - 10) % 3:
                        level, part = 1 + (t - 10) // 3, (t - 10) % 3
                        if part == 1 or level < LEVELS - 1:
                            s, M = (("Y", Y), ("X", X))[part - 1]
                            for i in (0, 1):
                                v.wait_ge(delta_products, d(h, D_PE, f"{s}{level}{i}"))
                                v.tensor_tensor(M[:, halves(i)], M[:, halves(i)], dbank[i], ALU.subtract).then_inc(delta_vec, 1)
                    if 27 <= t < 51:
                        n, part = (t - 27) // 3, (t - 27) % 3
                        if part == 0:
                            if n == 0:
                                v.memset(S[:, :], 0.0).then_inc(delta_vec, 1)
                            v.wait_ge(delta_products, d(h, D_PE, f"ks{n}"))
                            v.scalar_tensor_tensor(out=rr[:, :], in0=dbank[1][:, chunk(0)], scalar=col(NBEG, n),
                                                   in1=vb[:, chunk(n)], op0=ALU.mult, op1=ALU.add).then_inc(delta_vec, 1)
                        if part == 2:
                            v.wait_ge(delta_products, d(h, D_PE, f"ds{n}"))
                            v.scalar_tensor_tensor(out=S[:, :], in0=S[:, :], scalar=col(EGLAST, n),
                                                   in1=dbank[1][:, chunk(2)], op0=ALU.mult, op1=ALU.add).then_inc(delta_vec, 1)
                    if t in (58, 60):
                        i = (t - 58) // 2
                        v.wait_ge(delta_act, d(h, D_ACT, f"ro{i}"))
                        v.reciprocal(C[:, halves(i)], C[:, halves(i)]).then_inc(delta_vec, 1)
                        v.wait_ge(delta_vec, d(h, D_DVE, f"io{i}"))
                        v.tensor_tensor(ob[:, halves(i)], ob[:, halves(i)], C[:, halves(i)], ALU.mult).then_inc(delta_vec, 1)
                        v.wait_ge(delta_vec, d(h, D_DVE, f"no{i}"))
                        v.scalar_tensor_tensor(out=ob[:, halves(i)], in0=ob[:, halves(i)], scalar=dnw[:, :],
                                               in1=cg[:, halves(i)], op0=ALU.mult, op1=ALU.mult).then_inc(delta_vec, 1)

                def vec_attn(v, h, t):
                    for i in range(TB):
                        w = (i + 1) * P
                        if t == z_slot(i) + 1:
                            v.wait_ge(attn_act, d(h, A_ACT, f"keep{i}"))
                            v.tensor_tensor_scan(keep[:, w - 1::-1], keep[:, w - 1::-1], keep[:, w - 1::-1], 1.0,
                                                 ALU.mult, ALU.bypass).then_inc(attn_vec, 1)
                        if t == z_slot(i) + 2:
                            v.wait_ge(attn_act, d(h, A_ACT, f"beta{i}"))
                            v.wait_ge(attn_vec, d(h, A_DVE, f"scan{i}"))
                            v.tensor_tensor(beta[:, 0:w - 1], beta[:, 0:w - 1], keep[:, 1:w], ALU.mult).then_inc(attn_vec, 1)
                        for r in range(1 + (i >= 4)):
                            if t == z_slot(i) + 3 + r:
                                v.wait_ge(attn_products, d(h, A_PE, f"t{i}{r}"))
                                if i and r == 0:
                                    v.wait_ge(attn_products, d(h, A_PE, f"o{i - 1}"))
                                n = min(4, i + 1 - 4 * r)
                                v.tensor_copy(aT[:, 4 * r:4 * r + n, :], t_bank[:, 0:n * P]).then_inc(attn_vec, 1)

                def vec_gemm(v, h, t, last):
                    if last or t < 4:
                        return
                    u, half = half_before(t, 4)
                    if u in CONVOLVED:
                        n = 2 * (u - DN_V) + half
                        j = t % 4
                        if j == 0:
                            v.wait_ge(gemm_read, 2 * (h * UNITS + UNITS + u) + half + 1)
                            if half == 0:
                                used = {DN_V: (delta_products, d(h, D_PE, "v1")),
                                        DN_Q: (delta_vec, d(h, D_DVE, "q1")),
                                        DN_K: (delta_vec, d(h, D_DVE, "k1"))}[u]
                                v.wait_ge(*used)
                        y = {DN_V: nv, DN_Q: nq, DN_K: nk}[u][:, halves(half)]
                        w = cwc[:, {DN_Q: 0, DN_K: 1, DN_V: 2}[u], :]
                        conv_tap(v, y, w, half, j, conv_taps, h * 24 + 4 * n + j)

                def pool_delta(pool, h, t):
                    g = nc.gpsimd
                    level = {7: 0, 9: 1, **{5 + 3 * n: n for n in range(2, LEVELS)}}.get(t)
                    if level is not None:
                        if level == 0:
                            pool.wait_ge(delta_vec, d(h, D_DVE, "L1"))
                        elif level == 1:
                            pool.wait_ge(delta_vec, d(h, D_DVE, "x"))
                        else:
                            pool.wait_ge(delta_products, d(h, D_PE, f"P{level - 1}1"))
                        g.tensor_tensor(C[:, :].rearrange("p (n c) -> p n c", n=TB),
                                        dec[:, :].rearrange("p (n c) -> p n c", n=TB),
                                        level_mask[:, level, :].unsqueeze(1).to_broadcast([P, TB, P]),
                                        ALU.mult).then_inc(delta_pool, 1)

                def pool_gemm(pool, h, t, last):
                    U0 = h * UNITS + UNITS
                    if t % 8 == 1 and not (last and t // 8 == UNITS - 1):
                        u = t // 8 + 1
                        split_lo(pool, U0 + u, u % 2)
                    if t % 4 == 2 and t >= 8 and not last:
                        u, half = half_before(t, 8)
                        if u in SILU:
                            n = 2 * (u - DN_V) + half
                            y = {DN_V: nv, DN_Q: nq, DN_K: nk, DN_G: ng}[u][:, halves(half)]
                            pool.wait_ge(sigmoids, h * 8 + n + 1)
                            pool.tensor_tensor(y, y, sig[:, halves(half)], ALU.mult).then_inc(silus, 1)

                def cw_head(h):
                    return h + 1 if not isinstance(h, int) or h < HEADS - 1 else HEADS - 1

                with nc.Block() as block:
                    @block.sync
                    def _(sp):
                        with sp.Fori(0, HEADS - 1) as h:
                            for u in range(UNITS):
                                load_unit(sp, h * UNITS + UNITS + u, u % 2,
                                          w_main[bass.ds(h + (BLOCK[u] + 1), 1)].rearrange("o p k n -> (o p) k n"))
                        for u in range(KB):
                            load_unit(sp, HEADS * UNITS + u, u % 2,
                                      w_main[GATE_B_BLOCK + u])

                    @block.tensor
                    def _(pe):
                        def head(h):
                            for t in range(SLOTS):
                                pe_delta(pe, h, t)
                                pe_attn(pe, h, t)
                                pe_gemm(pe, h, t)

                        with pe.Fori(0, HEADS - 1) as h:
                            head(h)
                        head(HEADS - 1)

                    @block.scalar
                    def _(act):
                        def head(h, last):
                            for t in range(SLOTS):
                                if t == 0:
                                    act_gemm(act, h, t, last)
                                act_delta(act, h, t)
                                act_attn(act, h, t)
                                if t:
                                    act_gemm(act, h, t, last)

                        split_hi(act, UNITS, 0, 16 * (UNITS // 2 + 1))
                        with act.Fori(0, HEADS - 1) as h:
                            head(h, False)
                        head(HEADS - 1, True)
                        act.wait_ge(gemm_halves, 2 * UNITS * (HEADS + 1))
                        gate(act, KB - 1, 1, 2 * KB - 1, HEADS - 1)
                        for i in (0, 1):
                            act.wait_ge(gate_stored[i], 16 * (HEADS - 1 + KB))
                        act.wait_ge(ao_stored, 32 * HEADS)
                        act.wait_ge(ob_stored, 32 * HEADS)

                    @block.vector
                    def _(v):
                        def head(h, last):
                            for t in range(SLOTS):
                                vec_delta(v, h, t)
                                vec_attn(v, h, t)
                                vec_gemm(v, h, t, last)

                        with v.Fori(0, HEADS - 1) as h:
                            head(h, False)
                        head(HEADS - 1, True)

                    @block.gpsimd
                    def _(pool):
                        def head(h, last):
                            for t in range(SLOTS):
                                pool_gemm(pool, h, t, last)
                                pool_delta(pool, h, t)

                        split_lo(pool, UNITS, 0)
                        with pool.Fori(0, HEADS - 1) as h:
                            head(h, False)
                        head(HEADS - 1, True)

        if stop_after < 3:
            return
        M0 = UNITS * (HEADS + 1)
        tail = ExitStack()
        with tail:
            x1 = sb("x1", [P, TB, D], F32, tail)
            merge = ExitStack()
            with merge:
                mix_hi = sb("mix_hi", [P, KB, T], F32R, merge)
                mix_lo = sb("mix_lo", [P, KB, T], F32R, merge)
                gather = ExitStack()
                with gather:
                    so_hi = sb("so_hi", [P, KB, T], F32R, gather)
                    so_lo = sb("so_lo", [P, KB, T], F32R, gather)
                    stage = [sb(f"stage{i}", [P, T], F32, gather) for i in (0, 1)]
                    gbuf = [sb(f"gbuf{i}", [P, T], F32, gather) for i in (0, 1)]
                    mixa = x1

                    o_landed = [sem(f"o_landed{i}", gather) for i in (0, 1)]
                    g_landed = [sem(f"g_landed{i}", gather) for i in (0, 1)]
                    o_hi = sem("o_hi", gather)
                    o_lo = sem("o_lo", gather)
                    gated = sem("gated", gather)
                    summed = sem("summed", gather)
                    m_hi = sem("m_hi", gather)
                    m_lo = sem("m_lo", gather)

                    with nc.Block() as block:
                        @block.sync
                        def _(sp):
                            def load_o(n):
                                if n >= 2:
                                    sp.wait_ge(o_lo, n - 1)
                                sp.dma_start(stage[n % 2][:, :], o_d[n // HEADS][n % HEADS]).then_inc(o_landed[n % 2], 16)

                            load_unit(sp, M0, 0, w_proj_dn[0])
                            load_unit(sp, M0 + 1, 1, w_proj_dn[1])
                            for n in range(HEADS):
                                load_o(n)
                            for m in range(2 * KB):
                                if m >= 2:
                                    load_unit(sp, M0 + m, m % 2, (w_proj_dn if m < KB else w_proj_sb)[m % KB])
                                    sp.wait_ge(gated, 2 * (m - 1))
                                    if m >= KB + 2:
                                        sp.wait_ge(summed, 2 * (m - 1 - KB))
                                sp.dma_start(gbuf[m % 2][:, :], gates_d[m]).then_inc(g_landed[m % 2], 16)
                                if m < HEADS:
                                    load_o(HEADS + m)
                            load_unit(sp, M0 + 2 * KB, 0, w_up[0])
                            load_unit(sp, M0 + 2 * KB + 1, 1, w_up[w_up.shape[0] // 2])

                        @block.scalar
                        def _(act):
                            def split_o(n):
                                act.wait_ge(o_landed[n % 2], 16 * (n // 2 + 1))
                                act.activation((mix_hi if n < HEADS else so_hi)[:, n % HEADS, :], stage[n % 2][:, :],
                                               ACT.Copy).then_inc(o_hi, 1)

                            split_hi(act, M0, 0, 16 * (M0 // 2 + 1))
                            for n in range(HEADS):
                                split_o(n)
                            for m in range(2 * KB):
                                if m < 2 * KB - 1:
                                    split_hi(act, M0 + m + 1, (m + 1) % 2, 16 * ((M0 + m + 1) // 2 + 1))
                                if m < HEADS:
                                    split_o(HEADS + m)
                                if m >= KB:
                                    for half in (0, 1):
                                        cols = slice(half * HALF, (half + 1) * HALF)
                                        act.wait_ge(summed, 2 * (m - KB) + half + 1)
                                        act.activation(mix_hi[:, m - KB, cols], mixa[:, m - KB, cols],
                                                       ACT.Copy).then_inc(m_hi, 1)

                        @block.gpsimd
                        def _(pool):
                            split_lo(pool, M0, 0)
                            for m in range(2 * KB):
                                if m < 2 * KB - 1:
                                    split_lo(pool, M0 + m + 1, (m + 1) % 2)
                                if m >= KB:
                                    for half in (0, 1):
                                        cols = slice(half * HALF, (half + 1) * HALF)
                                        pool.wait_ge(m_hi, 2 * (m - KB) + half + 1)
                                        pool.tensor_tensor(mix_lo[:, m - KB, cols], mixa[:, m - KB, cols],
                                                           mix_hi[:, m - KB, cols].bitcast(F32),
                                                           ALU.subtract).then_inc(m_lo, 1)

                        @block.vector
                        def _(v):
                            def low_o(n):
                                v.wait_ge(o_hi, n + 1)
                                hi, lo = (mix_hi, mix_lo) if n < HEADS else (so_hi, so_lo)
                                v.tensor_tensor(lo[:, n % HEADS, :], stage[n % 2][:, :], hi[:, n % HEADS, :].bitcast(F32),
                                                ALU.subtract).then_inc(o_lo, 1)

                            for n in range(HEADS):
                                low_o(n)
                            for m in range(2 * KB):
                                if m < HEADS:
                                    low_o(HEADS + m)
                                v.wait_ge(g_landed[m % 2], 16 * (m // 2 + 1))
                                for half in (0, 1):
                                    cols = slice(half * HALF, (half + 1) * HALF)
                                    v.wait_ge(gemm_halves, 2 * (M0 + m) + half + 1)
                                    dst = mixa[:, m, cols] if m < KB else gbuf[m % 2][:, cols]
                                    v.tensor_tensor(dst, gemm_bank[half], gbuf[m % 2][:, cols], ALU.mult)\
                                        .then_inc(gated, 1)
                                    if m >= KB:
                                        v.wait_ge(gated, 2 * m + half + 1)
                                        v.tensor_tensor(mixa[:, m - KB, cols], mixa[:, m - KB, cols], dst,
                                                        ALU.add).then_inc(summed, 1)

                        @block.tensor
                        def _(pe):
                            for m in range(2 * KB):
                                U = M0 + m
                                pe.wait_ge(hi_split, U + 1)
                                pe.wait_ge(lo_split, U + 1)
                                for half in (0, 1):
                                    if m:
                                        pe.wait_ge(gated, 2 * m + half - 1)
                                    else:
                                        pe.wait_ge(gemm_read, 2 * M0)
                                    for k in range(KB):
                                        if m % KB == 0 and half == 0:
                                            pe.wait_ge(o_lo, (m // KB) * HEADS + k + 1)
                                        hi, lo = (mix_hi, mix_lo) if m < KB else (so_hi, so_lo)
                                        mm = unit_products(pe, m % 2, half, (k,), hi, lo)
                                    mm.then_inc(gemm_halves, 1)

                outp = ExitStack()
                with outp:
                    wo_raw = [sb(f"wo_raw{i}", [P, KB // 2, HALF], F32, outp) for i in (0, 1)]
                    wo_hi = [sb(f"wo_hi{i}", [P, KB, HALF], F32R, outp) for i in (0, 1)]
                    wo_lo = [sb(f"wo_lo{i}", [P, KB, HALF], F32R, outp) for i in (0, 1)]
                    wo_landed = [sem(f"wo_landed{i}", outp) for i in (0, 1)]
                    x_in = [sem(f"x_in{i}", outp) for i in range(TB)]
                    wo_h = sem("wo_h", outp)
                    wo_l = sem("wo_l", outp)
                    rows = sem("rows", outp)
                    added = sem("added", outp)

                    with nc.Block() as block:
                        @block.sync
                        def _(sp):
                            for n in range(4):
                                f, part = n // 2, n % 2
                                if n >= 2:
                                    sp.wait_ge(wo_l, n - 1)
                                sp.dma_start(wo_raw[part][:, :, :], w_out[f][:, part * KB // 2:(part + 1) * KB // 2, :]
                                             ).then_inc(wo_landed[part], 16)
                                if n == 1:
                                    for i in range(TB):
                                        sp.dma_start(x1[:, i, :], x[0, i * P:(i + 1) * P, :]).then_inc(x_in[i], 16)

                        @block.scalar
                        def _(act):
                            for n in range(4):
                                f, part = n // 2, n % 2
                                act.wait_ge(wo_landed[part], 16 * (f + 1))
                                act.activation(wo_hi[f][:, part * KB // 2:(part + 1) * KB // 2, :], wo_raw[part][:, :, :],
                                               ACT.Copy).then_inc(wo_h, 1)

                        @block.vector
                        def _(v):
                            for n in range(4):
                                f, part = n // 2, n % 2
                                ks = slice(part * KB // 2, (part + 1) * KB // 2)
                                v.wait_ge(wo_h, n + 1)
                                v.tensor_tensor(wo_lo[f][:, ks, :], wo_raw[part][:, :, :],
                                                wo_hi[f][:, ks, :].bitcast(F32), ALU.subtract).then_inc(wo_l, 1)
                            for n in range(2 * TB):
                                f, i = n // TB, n % TB
                                cols = slice(f * HALF, (f + 1) * HALF)
                                if f == 0:
                                    v.wait_ge(x_in[i], 16)
                                v.wait_ge(rows, n + 1)
                                v.tensor_tensor(x1[:, i, cols], psum[:, n % 4, :], x1[:, i, cols], ALU.add)\
                                    .then_inc(added, 1)

                        @block.tensor
                        def _(pe):
                            for n in range(2 * TB):
                                f, i = n // TB, n % TB
                                if n >= 4:
                                    pe.wait_ge(added, n - 3)
                                for k in range(KB):
                                    if i == 0 and k % (KB // 2) == 0:
                                        pe.wait_ge(wo_l, 2 * f + k // (KB // 2) + 1)
                                    for j, (a, w) in enumerate(((mix_hi, wo_hi), (mix_hi, wo_lo), (mix_lo, wo_hi))):
                                        mm = pe.matmul(psum[:, n % 4, :], a[:, k, i * P:(i + 1) * P], w[f][:, k, :],
                                                       start=(k == 0 and j == 0), stop=(k == KB - 1 and j == 2))
                                mm.then_inc(rows, 1)

            FB = w_up.shape[0] // 2
            GROUPS = FB // 2
            F0 = M0 + 2 * KB
            n2_hi = sb("n2_hi", [P, KB, T], F32R, tail)
            n2_lo = sb("n2_lo", [P, KB, T], F32R, tail)
            ss2 = sb("ss2", [P, TB], F32, tail)
            rstd2 = sb("rstd2", [P, TB], F32, tail)
            n2w = sb("n2w", [P, KB], F32, tail)
            norm2p = ExitStack()
            with norm2p:
                xr = [sb(f"xr{i}", [P, D], F32, norm2p) for i in range(4)]
                sq2 = [sb(f"sq2{i}", [P, D], F32, norm2p) for i in (0, 1)]
                n2w_in = sem("n2w_in", norm2p)
                r_ss, r_std, r_rec, r_norm = (sem(n, norm2p) for n in ("r_ss", "r_std", "r_rec", "r_norm"))
                r_turn, r_hi, r_lo = (sem(n, norm2p) for n in ("r_turn", "r_hi", "r_lo"))
                with nc.Block() as block:
                    @block.sync
                    def _(sp):
                        sp.dma_start(n2w[:, :], norm2).then_inc(n2w_in, 16)

                    @block.scalar
                    def _(act):
                        for i in range(TB):
                            if i >= 2:
                                act.wait_ge(r_ss, i - 1)
                            act.activation(sq2[i % 2][:, :], x1[:, i, :], ACT.Square, accum_out=ss2[:, i:i + 1]).then_inc(r_ss, 1)
                        for i in range(TB):
                            if i == 0:
                                act.wait_ge(r_ss, TB)
                                act.activation(ss2[:, :], ss2[:, :], ACT.Sqrt, bias=eps[:, :], scale=1.0 / D).then_inc(r_std, 1)
                                act.wait_ge(r_rec, 1)
                            if i >= 4:
                                act.wait_ge(r_turn, KB)
                            act.activation(xr[i % 4][:, :], x1[:, i, :], ACT.Copy, scale=rstd2[:, i:i + 1]).then_inc(r_norm, 1)
                            if i % 4 == 3:
                                act.wait_ge(n2w_in, 16)
                                for k in range(KB):
                                    act.wait_ge(r_turn, KB * (i // 4) + k + 1)
                                    act.activation(n2_hi[:, k, (i // 4) * HALF:(i // 4 + 1) * HALF], psum[:, 2 + k % 4, :],
                                                   ACT.Copy, scale=n2w[:, k:k + 1]).then_inc(r_hi, 1)

                    @block.vector
                    def _(v):
                        v.wait_ge(r_std, 1)
                        v.reciprocal(rstd2[:, :], ss2[:, :]).then_inc(r_rec, 1)
                        for n in range(2 * KB):
                            k, cols = n % KB, slice((n // KB) * HALF, (n // KB + 1) * HALF)
                            v.wait_ge(r_hi, n + 1)
                            v.scalar_tensor_tensor(out=n2_lo[:, k, cols], in0=psum[:, 2 + k % 4, :], scalar=n2w[:, k:k + 1],
                                                   in1=n2_hi[:, k, cols].bitcast(F32), op0=ALU.mult,
                                                   op1=ALU.subtract).then_inc(r_lo, 1)

                    @block.tensor
                    def _(pe):
                        for n in range(2 * KB):
                            k = n % KB
                            if k == 0:
                                pe.wait_ge(r_norm, 4 * (n // KB) + 4)
                            if n >= 4:
                                pe.wait_ge(r_lo, n - 3)
                            for i in range(4):
                                tr = pe.transpose(psum[:, 2 + k % 4, i * P:(i + 1) * P], xr[i][:, k * P:(k + 1) * P], identf[:, :])
                            tr.then_inc(r_turn, 1)

            FSLOTS = 32
            gb, ub = sb("gb", [P, T], F32, tail), sb("ub", [P, T], F32, tail)
            fpre = sb("fpre", [P, 2 + T], F32, tail)
            a_hi = sb("a_hi", [P, 2, T], F32R, tail)
            a_lo = sb("a_lo", [P, 2, T], F32R, tail)
            wd_raw = sb("wd_raw", [P, 2, D], F32, tail)
            wd_hi = sb("wd_hi", [P, 2, D], F32R, tail)
            wd_lo = sb("wd_lo", [P, 2, D], F32R, tail)
            taps = sb("taps", [P, 2, FB, 3], F32, tail)
            tapc = sb("tapc", [P, 2, 2, 3], F32, tail)
            wf = sb("wf", [P, D], F32, tail)
            sqf = [sb(f"sqf{i}", [P, D], F32, tail) for i in (0, 1)]
            stdf = sb("stdf", [P, TB], F32, tail)
            small_in = sem("small_in", tail)
            wd_landed = sem("wd_landed", tail)
            wd_his = sem("wd_his", tail)
            wd_los = sem("wd_los", tail)
            f_read = sem("f_read", tail)
            f_pad = sem("f_pad", tail)
            tap_in = sem("tap_in", tail)
            f_conv = sem("f_conv", tail)
            f_silu = sem("f_silu", tail)
            f_prod = sem("f_prod", tail)
            f_hi = sem("f_hi", tail)
            f_lo = sem("f_lo", tail)
            down = sem("down", tail)
            down_added = sem("down_added", tail)
            e_ss, e_std, e_rec, e_out, stored = (sem(n, tail) for n in ("e_ss", "e_std", "e_rec", "e_out", "stored"))

            def down_output(pe, g, n):
                i, f = n // 2, n % 2
                if n >= 4 or not (isinstance(g, int) and g == 0):
                    pe.wait_ge(down_added, 16 * g + n - 3)
                if n == 0:
                    pe.wait_ge(wd_los, g + 1)
                    pe.wait_ge(f_lo, 4 * g + 3)
                if n == 8:
                    pe.wait_ge(f_lo, 4 * g + 4)
                bank = psum[:, 2 + n % 4, :]
                for k in (0, 1):
                    for j, (a, w) in enumerate(((a_hi, wd_hi), (a_hi, wd_lo), (a_lo, wd_hi))):
                        mm = pe.matmul(bank, a[:, k, i * P:(i + 1) * P], w[:, k, f * HALF:(f + 1) * HALF],
                                       start=(k == 0 and j == 0), stop=(k == 1 and j == 2))
                mm.then_inc(down, 1)

            def down_add(v, g, n):
                i, f = n // 2, n % 2
                v.wait_ge(down, 16 * g + n + 1)
                v.tensor_tensor(x1[:, i, f * HALF:(f + 1) * HALF], psum[:, 2 + n % 4, :],
                                x1[:, i, f * HALF:(f + 1) * HALF], ALU.add).then_inc(down_added, 1)

            def events(t):
                H = t // 4 - 1
                return (H, t % 4, 0) if H >= 0 else (7, t % 4, 1)

            def hcols(half):
                return slice(half * HALF, (half + 1) * HALF)

            def act_ffn(act, g, t, only_events=False):
                H, phase, back = events(t)
                u, half = H // 2, H % 2
                gg = g - back
                if not (isinstance(gg, int) and gg < 0):
                    if phase == 0:
                        act.wait_ge(gemm_halves, 2 * F0 + 8 * gg + H + 1)
                        if half == 0:
                            if not (isinstance(gg, int) and gg == 0 and H == 0):
                                act.wait_ge(f_conv, 24 * gg + 3 * H)
                            else:
                                act.wait_ge(f_pad, 1)
                        act.activation(fpre[:, 2 + half * HALF:2 + (half + 1) * HALF], gemm_bank[half],
                                       ACT.Copy).then_inc(f_read, 1)
                    if phase == 3:
                        act.wait_ge(f_conv, 24 * gg + 3 * H + 3)
                        if u % 2 == 0:
                            act.activation(gb[:, hcols(half)], gb[:, hcols(half)], ACT.Silu).then_inc(f_silu, 1)
                        else:
                            act.wait_ge(f_prod, 4 * gg + 2 * (u // 2) + half + 1)
                            if not (isinstance(gg, int) and gg == 0):
                                act.wait_ge(down, 16 * gg - 8 + 8 * half)
                            act.activation(a_hi[:, u // 2, hcols(half)], ub[:, hcols(half)], ACT.Copy).then_inc(f_hi, 1)
                if only_events:
                    return
                if t % 8 == 1:
                    u = t // 8 + 1
                    if not (isinstance(g, int) and g == GROUPS - 1 and u == 4):
                        split_hi(act, F0 + 4 * g + u, u % 2, 16 * (F0 // 2 + 2 * g + u // 2 + 1))
                if t == 20:
                    act.wait_ge(wd_landed, 16 * (g + 1))
                    if not (isinstance(g, int) and g == 0):
                        act.wait_ge(down, 16 * g)
                    act.activation(wd_hi[:, :, :], wd_raw[:, :, :], ACT.Copy).then_inc(wd_his, 1)

            def vec_ffn(v, g, t, only_events=False):
                H, phase, back = events(t)
                u, half = H // 2, H % 2
                gg = g - back
                if t >= 1 and t <= 16 and not (isinstance(g, int) and g == 0):
                    down_add(v, g - 1, t - 1)
                if not (isinstance(gg, int) and gg < 0):
                    buf = (gb if u % 2 == 0 else ub)[:, hcols(half)]
                    if phase < 3:
                        w = tapc[:, u % 2, u // 2, :]
                        x_j = fpre[:, 2 - phase + half * HALF:2 - phase + (half + 1) * HALF]
                        if phase == 0:
                            v.wait_ge(f_read, 8 * gg + H + 1)
                            if H == 0:
                                v.wait_ge(tap_in, 1 + gg)
                            if u % 2:
                                if not (isinstance(gg, int) and gg == 0 and u == 1):
                                    v.wait_ge(f_lo, 4 * gg + 2 * (u // 2) + half - 1)
                            v.tensor_scalar(buf, x_j, w[:, 2:3], None, ALU.mult).then_inc(f_conv, 1)
                        else:
                            v.wait_ge(f_conv, 24 * gg + 3 * H + phase)
                            v.scalar_tensor_tensor(out=buf, in0=x_j, scalar=w[:, 2 - phase:3 - phase], in1=buf,
                                                   op0=ALU.mult, op1=ALU.add).then_inc(f_conv, 1)
                    elif u % 2:
                        v.wait_ge(f_silu, 4 * gg + 2 * (u // 2) + half + 1)
                        v.wait_ge(f_conv, 24 * gg + 3 * H + 3)
                        v.tensor_tensor(buf, gb[:, hcols(half)], buf, ALU.mult).then_inc(f_prod, 1)
                if only_events:
                    return
                if t == 3:
                    v.tensor_copy(tapc[:, :, :, :], taps[:, :, bass.ds(2 * g, 2), :]).then_inc(tap_in, 1)

            def pool_ffn(pool, g, t, only_events=False):
                H, phase, back = events(t)
                u, half = H // 2, H % 2
                gg = g - back
                if not (isinstance(gg, int) and gg < 0) and phase == 3 and u % 2:
                    pool.wait_ge(f_hi, 4 * gg + 2 * (u // 2) + half + 1)
                    pool.tensor_tensor(a_lo[:, u // 2, hcols(half)], ub[:, hcols(half)],
                                       a_hi[:, u // 2, hcols(half)].bitcast(F32), ALU.subtract).then_inc(f_lo, 1)
                if only_events:
                    return
                if t % 8 == 1:
                    u = t // 8 + 1
                    if not (isinstance(g, int) and g == GROUPS - 1 and u == 4):
                        split_lo(pool, F0 + 4 * g + u, u % 2)
                if t == 20:
                    pool.wait_ge(wd_his, g + 1)
                    if not (isinstance(g, int) and g == 0):
                        pool.wait_ge(down, 16 * g)
                    pool.tensor_tensor(wd_lo[:, :, :], wd_raw[:, :, :], wd_hi[:, :, :].bitcast(F32),
                                       ALU.subtract).then_inc(wd_los, 1)

            def pe_ffn(pe, g, t):
                if t >= 1 and t <= 16 and not (isinstance(g, int) and g == 0):
                    down_output(pe, g - 1, t - 1)
                u, half, part = t // 8, t % 8 // 4, t % 4
                U = F0 + 4 * g + u
                if part == 0:
                    if half == 0:
                        pe.wait_ge(hi_split, U + 1)
                        pe.wait_ge(lo_split, U + 1)
                    if not (isinstance(g, int) and g == 0 and u == 0):
                        pe.wait_ge(f_read, 8 * g + 2 * u + half - 1)
                mm = unit_products(pe, u % 2, half, (2 * part, 2 * part + 1), n2_hi, n2_lo)
                if part == 3:
                    mm.then_inc(gemm_halves, 1)

            with nc.Block() as block:
                @block.sync
                def _(sp):
                    sp.dma_start(taps[:, :, :, :], ffn_conv.rearrange("p (s b) j -> p s b j", s=2)).then_inc(small_in, 16)
                    sp.dma_start(wf[:, :], norm_f.to_broadcast([P, D])).then_inc(small_in, 16)

                    def group(g, units):
                        for u in units:
                            src = w_up[bass.ds(2 * g + (u % 2 * FB + u // 2), 1)].rearrange("o p k n -> (o p) k n")
                            load_unit(sp, F0 + 4 * g + u, u % 2, src)
                        if not (isinstance(g, int) and g == 0):
                            sp.wait_ge(wd_los, g)
                        sp.dma_start(wd_raw[:, :, :], w_down[bass.ds(g, 1)].rearrange("o p k n -> (o p) k n")).then_inc(wd_landed, 16)

                    group(0, (2, 3))
                    with sp.Fori(1, GROUPS) as g:
                        group(g, range(4))

                @block.tensor
                def _(pe):
                    for g in (0, 1):
                        for t in range(FSLOTS):
                            pe_ffn(pe, g, t)
                    with pe.Fori(2, GROUPS) as g:
                        for t in range(FSLOTS):
                            pe_ffn(pe, g, t)
                    for n in range(2 * TB):
                        down_output(pe, GROUPS - 1, n)

                @block.scalar
                def _(act):
                    split_hi(act, F0, 0, 16 * (F0 // 2 + 1))
                    for t in range(FSLOTS):
                        act_ffn(act, 0, t)
                    with act.Fori(1, GROUPS - 1) as g:
                        for t in range(FSLOTS):
                            act_ffn(act, g, t)
                    for t in range(FSLOTS):
                        act_ffn(act, GROUPS - 1, t)
                    for t in range(4):
                        act_ffn(act, GROUPS, t, only_events=True)
                    for i in range(TB):
                        act.wait_ge(down_added, 16 * (GROUPS - 1) + 2 * i + 2)
                        if i >= 2:
                            act.wait_ge(e_out, i - 1)
                        act.activation(sqf[i % 2][:, :], x1[:, i, :], ACT.Square, accum_out=stdf[:, i:i + 1]).then_inc(e_ss, 1)
                        act.wait_ge(e_ss, i + 1)
                        act.activation(stdf[:, i:i + 1], stdf[:, i:i + 1], ACT.Sqrt, bias=eps[:, :], scale=1.0 / D).then_inc(e_std, 1)

                @block.gpsimd
                def _(pool):
                    split_lo(pool, F0, 0)
                    for t in range(FSLOTS):
                        pool_ffn(pool, 0, t)
                    with pool.Fori(1, GROUPS - 1) as g:
                        for t in range(FSLOTS):
                            pool_ffn(pool, g, t)
                    for t in range(FSLOTS):
                        pool_ffn(pool, GROUPS - 1, t)
                    for t in range(4):
                        pool_ffn(pool, GROUPS, t, only_events=True)

                @block.vector
                def _(v):
                    v.memset(fpre[:, 0:2], 0.0).then_inc(f_pad, 1)
                    v.wait_ge(small_in, 32)
                    for t in range(FSLOTS):
                        vec_ffn(v, 0, t)
                    with v.Fori(1, GROUPS) as g:
                        for t in range(FSLOTS):
                            vec_ffn(v, g, t)
                    def final(i):
                        v.wait_ge(e_std, i + 1)
                        v.reciprocal(stdf[:, i:i + 1], stdf[:, i:i + 1]).then_inc(e_rec, 1)
                        v.wait_ge(e_rec, i + 1)
                        v.scalar_tensor_tensor(out=x1[:, i, :], in0=x1[:, i, :], scalar=stdf[:, i:i + 1], in1=wf[:, :],
                                               op0=ALU.mult, op1=ALU.mult).then_inc(e_out, 1)
                    for t in range(4):
                        vec_ffn(v, GROUPS, t, only_events=True)
                    for n in range(3, 2 * TB):
                        down_add(v, GROUPS - 1, n)
                        if n % 2 and n >= 5:
                            final(n // 2 - 2)
                    final(TB - 2)
                    final(TB - 1)

            with nc.Block() as block:
                @block.sync
                def _(sp):
                    for i in range(TB):
                        sp.wait_ge(e_out, i + 1)
                        sp.dma_start(out[0, i * P:(i + 1) * P, :], x1[:, i, :]).then_inc(stored, 16)
                    sp.wait_ge(stored, 16 * TB)

def kernel(**inputs):
    import concourse.bacc as bacc
    from concourse.bass_utils import run_bass_kernel_spmd

    nc = bacc.Bacc("TRN2", target_bir_lowering=False, num_devices=1)
    arrays, args = {}, []
    for name, a in layout(inputs).items():
        arrays[name] = a
        args.append(nc.dram_tensor(name, a.shape, mybir.dt.from_np(a.dtype), kind="ExternalInput").ap())
    shape = inputs["x"].shape
    out = nc.dram_tensor("out", shape, F32, kind="ExternalOutput").ap()
    build(nc, *args, out)
    results = run_bass_kernel_spmd(nc, [arrays], core_ids=[0])
    return results.results[0]["out"]


def layout(inputs):
    def units(w):
        k, n = w.shape
        return np.ascontiguousarray(w.reshape(k // P, P, n // P, P).transpose(2, 1, 0, 3))

    def columns(v):
        return np.ascontiguousarray(v.reshape(-1, P).T)

    a = {k: np.asarray(v) for k, v in inputs.items()}
    w = a["w_in"][0]
    qkv = 3 * HEADS * P
    taps = a["dn_conv_w"][0]
    up_taps = a["ffn_conv_w"][0]
    return {
        "x_in": a["x"],
        "norm1": columns(a["norm1_w"][0]),
        "w_main": units(np.concatenate([w[:, :qkv], w[:, qkv + 2 * HEADS:]], axis=1)),
        "w_ab": np.ascontiguousarray(w[:, qkv:qkv + 2 * HEADS].reshape(-1, P, 2 * HEADS).transpose(1, 0, 2)),
        "conv": np.ascontiguousarray(taps.reshape(taps.shape[0], 3, HEADS, P).transpose(3, 2, 1, 0)),
        "a_log": a["dn_A_log"],
        "dt_bias": a["dn_dt_bias"],
        "dn_norm": columns(a["dn_norm_w"][0]),
        "proj_dn": units(a["w_proj_dn"][0]),
        "proj_sb": units(a["w_proj_sb"][0]),
        "w_out_u": np.ascontiguousarray(a["w_out"][0].reshape(-1, P, 2, HALF).transpose(2, 1, 0, 3)),
        "norm2": columns(a["norm2_w"][0]),
        "w_up": units(a["ffn_w_up"][0]),
        "ffn_conv": np.ascontiguousarray(up_taps.reshape(up_taps.shape[0], -1, P).transpose(2, 1, 0)),
        "w_down": np.ascontiguousarray(a["ffn_w_down"][0].reshape(-1, 2, P, a["x"].shape[-1]).transpose(0, 2, 1, 3)),
        "norm_f": a["norm_f_w"].reshape(1, -1),
    }
```

```python
from contextlib import ExitStack

import numpy as np

import concourse.bass as bass
from concourse import mybir

P = 128
F32 = mybir.dt.float32
F32R = mybir.dt.float32r
BF16 = mybir.dt.bfloat16
ALU = mybir.AluOpType
ACT = mybir.ActivationFunctionType

EPS = 1e-6
BIG = 1e30
HEADS = 8
HALF = 512
SLOTS = 64
LEVELS = 7
UNITS = 8


def numbered(names):
    return {name: i + 1 for i, name in enumerate(names)}


def delta_steps():
    two = (0, 1)
    pe = [f"{s}{i}" for s in ("k", "q", "gk", "gq", "v", "kk", "qk", "y") for i in two]
    act = ["sqk", "sqq", "lnq", "lnk", "rk", "ck", "kd0", "kd1", "eg", "eD", "eT", "vb0", "vb1", "cg", "y0", "y1"]
    dve = ["tab", "cw", "gk", "gc", "gq", "nb", "D0", "D1", "T0", "T1", "L0", "L1", "at0", "at1", "cq", "x"]
    pool = [f"C{level}" for level in range(LEVELS)]
    for level in range(1, LEVELS):
        pe += [f"P{level}"] + [f"X{level}{i}" for i in two if level > 1] + [f"Y{level}"]
        act += [f"P{level}"]
        dve += [f"X{level}{i}" for i in two if level > 1] + [f"Y{level}"]
    for n in range(8):
        pe += [f"ks{n}", f"vn{n}", f"ds{n}"]
        dve += ["s_init"] * (n == 0) + [f"r{n}", f"s{n}"]
        act += [f"vn{n}"] + ([f"o{n // 4}"] if n % 4 == 3 else []) + ["sqo0"] * (n == 4)
    pe += ["to0", "to1"]
    act += ["sqo1", "lno", "ero"]
    dve += ["no", "fo0", "fo1"]
    return numbered(pe), numbered(act), numbered(dve), numbered(pool)


D_PE, D_ACT, D_DVE, D_POOL = delta_steps()


TAB_DVE = numbered(["ab0", "ab1", "y", "neg", "negabs", "softplus", "step", "G", "left", "nbeg"])
TAB_ACT = numbered(["exp", "ea", "ln", "eg", "egl", "eglast", "beta"])


def attn_steps():
    pe, act, dve = ["v0", "v1"], ["v0", "v1"], []
    for i in range(8):
        rounds = 1 + (i >= 4)
        pe += [f"z{i}"] + [f"t{i}{r}" for r in range(rounds)] + [f"o{i}"]
        act += [f"keep{i}", f"beta{i}"] + ([f"o{i // 4}"] if i % 4 == 3 else [])
        dve += [f"scan{i}", f"a{i}"] + [f"t{i}{r}" for r in range(rounds)]
    return numbered(pe), numbered(act), numbered(dve)


A_PE, A_ACT, A_DVE = attn_steps()

GATE_A, SB_V, DN_V, DN_Q, DN_K, DN_G, SB_Q, SB_K = range(UNITS)
CONVOLVED = (DN_V, DN_Q, DN_K)
SILU = (DN_V, DN_Q, DN_K, DN_G)


LEVEL_SLOT = 14
CHUNK_SLOT = 27
NORM_SLOT = 54


def z_slot(i):
    return 10 + 5 * i


def build(nc, x, norm1, w_main, w_ab, conv, a_log, dt_bias, dn_norm, w_proj_dn, w_proj_sb,
          w_out, norm2, w_up, ffn_conv, w_down, norm_f, out, stop_after=9):
    T, D = x.shape[1], x.shape[2]
    KB = D // P
    TB = T // P
    BLOCK = {kind: HEADS * i for i, kind in enumerate((DN_Q, DN_K, DN_V, DN_G, SB_Q, SB_K, SB_V, GATE_A))}
    GATE_B_BLOCK = BLOCK[GATE_A] + KB
    SCALE = float(P) ** -0.5

    gates_d = nc.dram_tensor("gates_d", (2 * KB, P, T), F32).ap()
    o_d = nc.dram_tensor("o_d", (2, HEADS, P, T), F32).ap()

    whole = ExitStack()
    with whole:
        def sem(name, ctx=whole):
            return ctx.enter_context(nc.semaphore(name))

        def sb(name, shape, dt=F32, ctx=whole):
            return ctx.enter_context(nc.sbuf_tensor(name, shape, dt))

        identf = sb("identf", [P, P])
        identb = sb("identb", [P, P], BF16)
        ones = sb("ones", [P, P])
        eps = sb("eps", [P, 1])
        eps_q = sb("eps_q", [P, 1])
        w_raw = [sb(f"w_raw{i}", [P, KB, P]) for i in (0, 1)]
        w_hi = [sb(f"w_hi{i}", [P, KB, P], F32R) for i in (0, 1)]
        w_lo = [sb(f"w_lo{i}", [P, KB, P], F32R) for i in (0, 1)]
        psum = whole.enter_context(nc.psum_tensor("psum", [P, 8, HALF], F32))
        gemm_bank = [psum[:, 0, :], psum[:, 1, :]]

        raw_landed = [sem(f"raw_landed{i}") for i in (0, 1)]
        hi_split = sem("hi_split")
        lo_split = sem("lo_split")
        gemm_halves = sem("gemm_halves")
        gemm_read = sem("gemm_read")

        def load_unit(eng, U, parity, src, raw_wait=True):
            if raw_wait:
                eng.wait_ge(hi_split, U - 1)
                eng.wait_ge(lo_split, U - 1)
            eng.dma_start(w_raw[parity][:, :, :], src).then_inc(raw_landed[parity], 16)

        def split_hi(act, U, parity, landed, free=True):
            act.wait_ge(raw_landed[parity], landed)
            if free:
                act.wait_ge(gemm_halves, 2 * U - 2)
            act.activation(w_hi[parity][:, :, :], w_raw[parity][:, :, :], ACT.Copy).then_inc(hi_split, 1)

        def split_lo(pool, U, parity, free=True):
            pool.wait_ge(hi_split, U + 1)
            if free:
                pool.wait_ge(gemm_halves, 2 * U - 2)
            pool.tensor_tensor(w_lo[parity][:, :, :], w_raw[parity][:, :, :],
                               w_hi[parity][:, :, :].bitcast(F32), ALU.subtract).then_inc(lo_split, 1)

        def unit_products(pe, parity, half, ks, hi, lo):
            cols = slice(half * HALF, (half + 1) * HALF)
            for k in ks:
                for j, (w, a) in enumerate(((w_hi, hi), (w_hi, lo), (w_lo, hi))):
                    mm = pe.matmul(gemm_bank[half], w[parity][:, k, :], a[:, k, cols],
                                   start=(k == 0 and j == 0), stop=(k == KB - 1 and j == 2))
            return mm

        head_ctx = ExitStack()
        with head_ctx:
            def hsb(name, shape, dt=F32):
                return sb(name, shape, dt, head_ctx)

            n1_hi = hsb("n1_hi", [P, KB, T], F32R)
            n1_lo = hsb("n1_lo", [P, KB, T], F32R)
            nq, nk, nv = hsb("nq", [P, T]), hsb("nk", [P, T]), hsb("nv", [P, T])
            ng, nsq, nsk, nsv = hsb("ng", [P, T]), hsb("nsq", [P, T]), hsb("nsk", [P, T]), hsb("nsv", [P, T])
            cq, ck, cg = hsb("cq", [P, T]), hsb("ck", [P, T]), hsb("cg", [P, T])
            sums = hsb("sums", [P, 3, TB])
            logs = hsb("logs", [P, 3, TB])
            rows = hsb("rows", [P, 3, TB])
            inv = hsb("inv", [P, 2, TB])
            dec, decT = hsb("dec", [P, T]), hsb("decT", [P, T])
            X, Y, R = hsb("X", [P, T]), hsb("Y", [P, T]), hsb("R", [P, T])
            Cs = [hsb("C0", [P, T]), hsb("C1", [P, T])]
            vb, kd = hsb("vb", [P, T]), hsb("kd", [P, T])
            ob = hsb("ob", [P, T])
            S = hsb("S", [P, P])
            rr, vnew = hsb("rr", [P, P]), hsb("vnew", [P, P])
            keep, beta, aT = hsb("keep", [P, T]), hsb("beta", [P, T]), hsb("aT", [P, TB, P])
            sv = hsb("sv", [P, TB, P])
            ao = hsb("ao", [P, HALF])
            pre = hsb("pre", [P, 3 + T])
            sig = hsb("sig", [P, T])
            G, BETA, NBEG, EGL, EGLAST = range(5)
            tab = hsb("tab", [P, HEADS, 5, TB])
            cur = hsb("cur", [P, 5, TB])
            cwt = hsb("cwt", [P, HEADS, 3, 4])
            cwc = hsb("cwc", [P, 3, 4])
            dnw = hsb("dnw", [P, 1])
            tri = hsb("tri", [P, P])
            pos_mask, neg_mask = hsb("pos_mask", [P, P]), hsb("neg_mask", [P, P])
            z_mask = hsb("z_mask", [P, P], BF16)
            level_mask = hsb("level_mask", [P, LEVELS, P], BF16)

            dbank = [psum[:, 6, :], psum[:, 7, :]]
            z_bank = psum[:, 2:4, :].rearrange("p b n -> p (b n)")
            z_pair = [psum[:, 2, :], psum[:, 3, :]]
            t_bank, ao_bank = psum[:, 4, :], psum[:, 5, :]
            side_bank = [t_bank, ao_bank]

            def conv_tap(v, y, w, half, j, counter, before):
                x_j = pre[:, 3 - j + half * HALF:3 - j + (half + 1) * HALF]
                if j == 0:
                    v.tensor_scalar(y, x_j, w[:, 3:4], None, ALU.mult).then_inc(counter, 1)
                else:
                    v.wait_ge(counter, before)
                    v.scalar_tensor_tensor(out=y, in0=x_j, scalar=w[:, 3 - j:4 - j], in1=y,
                                           op0=ALU.mult, op1=ALU.add).then_inc(counter, 1)

            first = ExitStack()
            with first:
                xs = [X, Y, Cs[0], R, dec, decT, vb, kd]
                wab_hi = sb("wab_hi", [P, KB, 2 * HEADS], F32R, first)
                wab_lo = sb("wab_lo", [P, KB, 2 * HEADS], F32R, first)
                abT = beta[0:2 * HEADS, :]
                wab = nsq[:, 0:KB * 2 * HEADS].rearrange("p (k n) -> p k n", k=KB)
                dt_b = nsq[:, 512:520]
                al_b = nsq[:, 520:528]
                y_ab = nsk[:, 0:64].rearrange("p (h n) -> p h n", h=HEADS)
                t1 = nsk[:, 64:128].rearrange("p (h n) -> p h n", h=HEADS)
                t2 = nsk[:, 128:192].rearrange("p (h n) -> p h n", h=HEADS)
                t3 = nsk[:, 192:256].rearrange("p (h n) -> p h n", h=HEADS)
                gstep = nsk[:, 256:320]
                ea = nsk[:, 320:328]
                n1w = nsk[:, 336:344]
                ss = nsk[:, 344:352]
                rstd = nsk[:, 352:360]
                std = nsk[:, 360:368]
                junk = keep

                c_small = sem("c_small", first)
                x_landed = [sem(f"x_landed{i}", first) for i in range(TB)]
                masks = sem("masks", first)
                x_ss = sem("x_ss", first)
                x_std = sem("x_std", first)
                x_rstd = sem("x_rstd", first)
                x_norm = sem("x_norm", first)
                x_turned = sem("x_turned", first)
                n_hi = sem("n_hi", first)
                n_lo = sem("n_lo", first)
                ab_hi = sem("ab_hi", first)
                ab_lo = sem("ab_lo", first)
                ab_sum = sem("ab_sum", first)
                tab_act = sem("tab_act", first)
                tab_dve = sem("tab_dve", first)
                pad = sem("pad", first)
                gate_out = sem("gate_out0", first)
                conv0 = sem("conv0", first)
                sig0 = sem("sig0", first)
                silu0 = sem("silu0", first)

                with nc.Block() as block:
                    @block.sync
                    def _(sp):
                        def load_x(i):
                            sp.dma_start(xs[i][:, :], x[0, i * P:(i + 1) * P, :]).then_inc(x_landed[i], 16)

                        for i in range(4):
                            load_x(i)
                        sp.dma_start(n1w, norm1).then_inc(c_small, 16)
                        sp.dma_start(wab, w_ab).then_inc(c_small, 16)
                        sp.dma_start(dt_b, dt_bias[0:1, :].to_broadcast([P, HEADS])).then_inc(c_small, 16)
                        sp.dma_start(al_b, a_log[0:1, :].to_broadcast([P, HEADS])).then_inc(c_small, 16)
                        sp.dma_start(dnw[:, :], dn_norm).then_inc(c_small, 16)
                        sp.dma_start(cwt[:, :, :, :], conv).then_inc(c_small, 16)
                        load_unit(sp, 0, 0, w_main[BLOCK[0]], raw_wait=False)
                        for i in range(4, TB):
                            load_x(i)
                        load_unit(sp, 1, 1, w_main[BLOCK[1]], raw_wait=False)
                        for U in range(2, UNITS):
                            load_unit(sp, U, U % 2, w_main[BLOCK[U]])
                            if U == 3:
                                for half in (0, 1):
                                    sp.wait_ge(gemm_read, half + 1)
                                    sp.dma_start(gates_d[0][:, half * HALF:(half + 1) * HALF],
                                                 sig[:, half * HALF:(half + 1) * HALF]).then_inc(gate_out, 16)
                        load_unit(sp, UNITS, 0, w_main[BLOCK[0] + 1])
                        sp.wait_ge(gate_out, 32)

                    @block.gpsimd
                    def _(pool):
                        count = [0]

                        def done(ins):
                            count[0] += 1
                            ins.then_inc(masks, 1)
                            pool.wait_ge(masks, count[0])

                        g = nc.gpsimd
                        done(g.memset(identf[:, :], 0.0))
                        done(g.affine_select(out=identf[:, :], in_=identf[:, :], compare_op=ALU.not_equal,
                                             fill=1.0, base=0, pattern=[[-1, P]], channel_multiplier=1))
                        done(g.memset(ones[:, :], 1.0))
                        done(g.memset(eps[:, :], EPS))
                        done(g.memset(eps_q[:, :], EPS * P))
                        done(g.affine_select(out=tri[:, :], in_=ones[:, :], compare_op=ALU.is_ge,
                                             fill=0.0, base=0, pattern=[[1, P]], channel_multiplier=-1))
                        done(g.memset(pos_mask[:, :], 0.0))
                        done(g.affine_select(out=pos_mask[:, :], in_=pos_mask[:, :], compare_op=ALU.is_gt,
                                             fill=BIG, base=0, pattern=[[-1, P]], channel_multiplier=1))
                        done(g.memset(neg_mask[:, :], 0.0))
                        done(g.affine_select(out=neg_mask[:, :], in_=neg_mask[:, :], compare_op=ALU.is_ge,
                                             fill=-BIG, base=0, pattern=[[1, P]], channel_multiplier=-1))
                        done(g.tensor_copy(identb[:, :], identf[:, :]))
                        done(g.memset(z_mask[:, :], 0.0))
                        done(g.affine_select(out=z_mask[:, :], in_=z_mask[:, :], compare_op=ALU.is_gt,
                                             fill=-BIG, base=0, pattern=[[-1, P]], channel_multiplier=1))
                        for level in range(LEVELS):
                            s = 1 << level
                            m = level_mask[:, level, :].rearrange("p (b r) -> p b r", r=2 * s)
                            nb = P // (2 * s)
                            one = ones[:, :].rearrange("p (b r) -> p b r", r=2 * s)
                            done(g.affine_select(out=m, in_=one, compare_op=ALU.is_ge, fill=0.0, base=s - 1,
                                                 pattern=[[0, nb], [-1, 2 * s]], channel_multiplier=0))
                            done(g.affine_select(out=m, in_=m, compare_op=ALU.is_ge, fill=0.0, base=-s,
                                                 pattern=[[-2 * s, nb], [0, 2 * s]], channel_multiplier=1))
                            done(g.affine_select(out=m, in_=m, compare_op=ALU.is_ge, fill=0.0, base=2 * s - 1,
                                                 pattern=[[2 * s, nb], [0, 2 * s]], channel_multiplier=-1))
                        for U in range(UNITS + 1):
                            split_lo(pool, U, U % 2, free=U >= 2)
                            for half in (0, 1):
                                n = 2 * (U - 2) + half
                                if U - 2 in SILU:
                                    y = {DN_V: nv, DN_Q: nq, DN_K: nk, DN_G: ng}[U - 2][:, half * HALF:(half + 1) * HALF]
                                    pool.wait_ge(sig0, 2 * (U - 2 - DN_V) + half + 1)
                                    pool.tensor_tensor(y, y, sig[:, half * HALF:(half + 1) * HALF],
                                                       ALU.mult).then_inc(silu0, 1)

                    @block.tensor
                    def _(pe):
                        def turn_rows(i2, k):
                            n = KB * i2 + k
                            if k == 0:
                                pe.wait_ge(x_norm, 4 * i2 + 4)
                            if n >= 4:
                                pe.wait_ge(n_lo, n - 3)
                            for i in range(4):
                                tr = pe.transpose(psum[:, 2 + k % 4, i * P:(i + 1) * P],
                                                  xs[4 * i2 + i][:, k * P:(k + 1) * P], identf[:, :])
                            tr.then_inc(x_turned, 1)

                        def logits(half, k):
                            if k == 0:
                                pe.wait_ge(ab_lo, 1)
                            for j, (w, a) in enumerate(((wab_hi, n1_hi), (wab_hi, n1_lo), (wab_lo, n1_hi))):
                                mm = pe.matmul(psum[0:2 * HEADS, 6 + half, :], w[:, k, :],
                                               a[:, k, half * HALF:(half + 1) * HALF],
                                               start=(k == 0 and j == 0), stop=(k == KB - 1 and j == 2))
                            if k == KB - 1:
                                mm.then_inc(ab_sum, 1)

                        def unit_half(U, half, k):
                            if k == 0 and half == 0:
                                pe.wait_ge(hi_split, U + 1)
                                pe.wait_ge(lo_split, U + 1)
                            if k == 0 and U:
                                pe.wait_ge(gemm_read, 2 * U + half - 1)
                            mm = unit_products(pe, U % 2, half, (k,), n1_hi, n1_lo)
                            if k == KB - 1:
                                mm.then_inc(gemm_halves, 1)

                        pe.wait_ge(masks, 2)
                        for k in range(KB + 2):
                            if k < KB:
                                turn_rows(0, k)
                            if k >= 2:
                                pe.wait_ge(n_lo, k - 1)
                                unit_half(0, 0, k - 2)
                        for k in range(KB):
                            turn_rows(1, k)
                            logits(0, k)
                        for k in range(KB):
                            pe.wait_ge(n_lo, KB + k + 1)
                            unit_half(0, 1, k)
                        for k in range(KB):
                            logits(1, k)
                        for U in range(1, UNITS):
                            for half in (0, 1):
                                for k in range(KB):
                                    unit_half(U, half, k)
                            if U == 1:
                                pe.wait_ge(tab_dve, TAB_DVE["ab1"])
                                for i in range(TB):
                                    tr = pe.transpose(psum[:, 5, 16 * i:16 * i + 16], abT[:, i * P:(i + 1) * P],
                                                      identf[0:2 * HEADS, 0:2 * HEADS])
                                tr.then_inc(ab_sum, 1)
                            if U == 2:
                                pe.wait_ge(tab_dve, TAB_DVE["step"])
                                pe.wait_ge(masks, 6)
                                pe.matmul(psum[:, 4, 0:64], tri[:, :], gstep, start=True, stop=True)
                                pe.matmul(psum[:, 4, 64:128], ones[:, :], gstep, start=True, stop=True).then_inc(ab_sum, 1)

                    @block.scalar
                    def _(act):
                        for i in range(TB):
                            act.wait_ge(x_landed[i], 16)
                            if i:
                                act.wait_ge(x_ss, i)
                            act.activation(junk[:, :], xs[i][:, :], ACT.Square,
                                           accum_out=ss[:, i:i + 1]).then_inc(x_ss, 1)
                            if i == 0:
                                act.wait_ge(masks, 4)
                            act.wait_ge(x_ss, i + 1)
                            act.activation(std[:, i:i + 1], ss[:, i:i + 1], ACT.Sqrt, bias=eps[:, :],
                                           scale=1.0 / D).then_inc(x_std, 1)
                            if i % 4 == 3:
                                if i == 3:
                                    act.wait_ge(c_small, 16 * 6)
                                    act.activation(wab_hi[:, :, :], wab, ACT.Copy).then_inc(ab_hi, 1)
                                    split_hi(act, 0, 0, 16, free=False)
                                for k in range(KB):
                                    n = KB * (i // 4) + k
                                    act.wait_ge(x_turned, n + 1)
                                    act.activation(n1_hi[:, k, (i // 4) * HALF:(i // 4 + 1) * HALF], psum[:, 2 + k % 4, :],
                                                   ACT.Copy, scale=n1w[:, k:k + 1]).then_inc(n_hi, 1)
                        split_hi(act, 1, 1, 16, free=False)

                        def softplus():
                            act.wait_ge(tab_dve, TAB_DVE["negabs"])
                            act.activation(t2, t1, ACT.Exp).then_inc(tab_act, 1)
                            act.activation(ea, al_b, ACT.Exp).then_inc(tab_act, 1)
                            act.wait_ge(tab_act, TAB_ACT["exp"])
                            act.wait_ge(masks, 3)
                            act.activation(t3, t2, ACT.Ln, bias=ones[:, 0:1]).then_inc(tab_act, 1)

                        def decays():
                            act.wait_ge(tab_dve, TAB_DVE["left"])
                            act.activation(t2, tab[:, :, G, :], ACT.Exp).then_inc(tab_act, 1)
                            act.activation(tab[:, :, EGL, :], t1, ACT.Exp).then_inc(tab_act, 1)
                            act.activation(tab[:, :, EGLAST, :],
                                           psum[:, 4, 64:128].rearrange("p (h n) -> p h n", h=HEADS),
                                           ACT.Exp).then_inc(tab_act, 1)
                            act.activation(tab[:, :, BETA, :],
                                           psum[:, 5, 0:128].rearrange("p (n c) -> p c n", n=TB)[:, HEADS:, :],
                                           ACT.Sigmoid).then_inc(tab_act, 1)

                        for U in range(UNITS):
                            if U >= 1:
                                split_hi(act, U + 1, (U + 1) % 2, 16 * ((U + 1) // 2 + 1))
                            if U == 2:
                                softplus()
                            for half in (0, 1):
                                cols = slice(half * HALF, (half + 1) * HALF)
                                act.wait_ge(gemm_halves, 2 * U + half + 1)
                                if (U, half) == (SB_K, 1):
                                    continue
                                if U == GATE_A:
                                    act.activation(sig[:, cols], gemm_bank[half], ACT.Sigmoid).then_inc(gemm_read, 1)
                                elif U in CONVOLVED:
                                    if U > DN_V:
                                        act.wait_ge(conv0, 8 * (U - DN_V))
                                    else:
                                        act.wait_ge(pad, 1)
                                    act.activation(pre[:, 3 + half * HALF:3 + (half + 1) * HALF], gemm_bank[half],
                                                   ACT.Copy).then_inc(gemm_read, 1)
                                else:
                                    dst = {SB_V: nsv, SB_Q: nsq, SB_K: nsk, DN_G: ng}[U]
                                    if U in (SB_Q, SB_K):
                                        act.wait_ge(tab_act, len(TAB_ACT))
                                        act.wait_ge(tab_dve, len(TAB_DVE))
                                    act.activation(dst[:, cols], gemm_bank[half], ACT.Copy).then_inc(gemm_read, 1)
                            if U in SILU:
                                for half in (0, 1):
                                    cols = slice(half * HALF, (half + 1) * HALF)
                                    y = {DN_V: nv, DN_Q: nq, DN_K: nk, DN_G: ng}[U]
                                    if U == DN_V:
                                        act.wait_ge(gate_out, 32)
                                    else:
                                        act.wait_ge(silu0, 2 * (U - DN_V - 1) + half + 1)
                                    if U in CONVOLVED:
                                        act.wait_ge(conv0, 8 * (U - DN_V) + 4 * half + 4)
                                    else:
                                        act.wait_ge(gemm_read, 2 * U + half + 1)
                                    act.activation(sig[:, cols], y[:, cols], ACT.Sigmoid).then_inc(sig0, 1)
                            if U == 2:
                                decays()

                    @block.vector
                    def _(v):
                        v.memset(pre[:, 0:3], 0.0).then_inc(pad, 1)
                        for i in range(TB):
                            v.wait_ge(x_std, i + 1)
                            v.reciprocal(rstd[:, i:i + 1], std[:, i:i + 1]).then_inc(x_rstd, 1)
                            v.wait_ge(x_rstd, i + 1)
                            v.tensor_scalar(xs[i][:, :], xs[i][:, :], rstd[:, i:i + 1], None, ALU.mult).then_inc(x_norm, 1)
                            if i == 3:
                                v.wait_ge(ab_hi, 1)
                                v.tensor_tensor(wab_lo[:, :, :], wab, wab_hi[:, :, :].bitcast(F32), ALU.subtract).then_inc(ab_lo, 1)
                            if i % 4 == 3:
                                for k in range(KB):
                                    n = KB * (i // 4) + k
                                    cols = slice((i // 4) * HALF, (i // 4 + 1) * HALF)
                                    v.wait_ge(n_hi, n + 1)
                                    v.scalar_tensor_tensor(out=n1_lo[:, k, cols], in0=psum[:, 2 + k % 4, :],
                                                           scalar=n1w[:, k:k + 1], in1=n1_hi[:, k, cols].bitcast(F32),
                                                           op0=ALU.mult, op1=ALU.subtract).then_inc(n_lo, 1)
                        for half in (0, 1):
                            v.wait_ge(ab_sum, half + 1)
                            v.tensor_copy(abT[:, half * HALF:(half + 1) * HALF], psum[0:2 * HEADS, 6 + half, :]).then_inc(tab_dve, 1)
                        ab = psum[:, 5, 0:128].rearrange("p (n c) -> p c n", n=TB)
                        v.wait_ge(ab_sum, 3)
                        v.tensor_tensor(y_ab, ab[:, 0:HEADS, :], dt_b.unsqueeze(2).to_broadcast([P, HEADS, TB]),
                                        ALU.add).then_inc(tab_dve, 1)
                        v.wait_ge(tab_dve, TAB_DVE["y"])
                        v.tensor_scalar(t1, y_ab, -1.0, None, ALU.mult).then_inc(tab_dve, 1)
                        v.wait_ge(tab_dve, TAB_DVE["neg"])
                        v.tensor_tensor(t1, t1, y_ab, ALU.min).then_inc(tab_dve, 1)
                        v.wait_ge(tab_act, TAB_ACT["ln"])
                        v.scalar_tensor_tensor(out=y_ab, in0=y_ab, scalar=0.0, in1=t3, op0=ALU.max,
                                               op1=ALU.add).then_inc(tab_dve, 1)
                        v.wait_ge(tab_dve, TAB_DVE["softplus"])
                        v.scalar_tensor_tensor(out=gstep.rearrange("p (h n) -> p h n", h=HEADS), in0=y_ab, scalar=-1.0,
                                               in1=ea.unsqueeze(2).to_broadcast([P, HEADS, TB]), op0=ALU.mult,
                                               op1=ALU.mult).then_inc(tab_dve, 1)

                        def taps_of(u):
                            for half in (0, 1):
                                v.wait_ge(gemm_read, 2 * u + half + 1)
                                y = {DN_V: nv, DN_Q: nq, DN_K: nk}[u][:, half * HALF:(half + 1) * HALF]
                                w = cwt[:, 0, {DN_Q: 0, DN_K: 1, DN_V: 2}[u], :]
                                for j in range(4):
                                    conv_tap(v, y, w, half, j, conv0, (8 * (u - DN_V) + 4 * half + j) if j else None)

                        taps_of(DN_V)
                        v.wait_ge(ab_sum, 4)
                        v.tensor_copy(tab[:, :, G, :], psum[:, 4, 0:64].rearrange("p (h n) -> p h n", h=HEADS)).then_inc(tab_dve, 1)
                        v.wait_ge(tab_dve, TAB_DVE["G"])
                        v.tensor_tensor(t1, psum[:, 4, 64:128].rearrange("p (h n) -> p h n", h=HEADS),
                                        tab[:, :, G, :], ALU.subtract).then_inc(tab_dve, 1)
                        taps_of(DN_Q)
                        v.wait_ge(tab_act, TAB_ACT["beta"])
                        v.scalar_tensor_tensor(out=tab[:, :, NBEG, :], in0=tab[:, :, BETA, :], scalar=-1.0, in1=t2,
                                               op0=ALU.mult, op1=ALU.mult).then_inc(tab_dve, 1)
                        taps_of(DN_K)

            if stop_after >= 2:
              loop = ExitStack()
              with loop:
                delta_products = sem("delta_products", loop)
                delta_act = sem("delta_act", loop)
                delta_vec = sem("delta_vec", loop)
                delta_pool = sem("delta_pool", loop)
                attn_products = sem("attn_products", loop)
                attn_act = sem("attn_act", loop)
                attn_vec = sem("attn_vec", loop)
                conv_taps = sem("conv_taps", loop)
                sigmoids = sem("sigmoids", loop)
                silus = sem("silus", loop)
                gate_stored = [sem(f"gate_stored{i}", loop) for i in (0, 1)]
                ao_stored = sem("ao_stored", loop)
                ob_stored = sem("ob_stored", loop)

                def d(h, table, step):
                    return h * len(table) + table[step]

                def chunk(n):
                    return slice(n * P, (n + 1) * P)

                def halves(i):
                    return slice(i * HALF, (i + 1) * HALF)

                def blocks(tile, level):
                    return tile[:, :].rearrange("p (b r s) -> p b r s", r=2, s=1 << level)

                def first_half(tile, level, n):
                    return tile[:, chunk(n)].rearrange("p (b r s) -> p b r s", r=2, s=1 << level)[:, :, 0, :]

                def second(tile, level, n):
                    return tile[:, chunk(n)].rearrange("p (b r s) -> p b r s", r=2, s=1 << level)[:, :, 1, :]

                def packed(bank, level):
                    return bank.rearrange("p (b s) -> p b s", s=1 << level)

                def col(table, n):
                    return cur[:, table, n:n + 1]

                def pe_delta(pe, h, t):
                    def four(bank, lhs, rhs, waits):
                        for s_, value in waits:
                            pe.wait_ge(s_, value)
                        for q in range(4):
                            n = 4 * i + q
                            mm = pe.matmul(bank[:, chunk(q)], lhs(n), rhs(n), start=True, stop=True)
                        mm.then_inc(delta_products, 1)

                    def turn(bank, src, waits):
                        for s_, value in waits:
                            pe.wait_ge(s_, value)
                        for q in range(4):
                            tr = pe.transpose(bank[:, chunk(q)], src(4 * i + q), identf[:, :])
                        tr.then_inc(delta_products, 1)

                    def eight(lhs, rhs, bank, waits):
                        for s_, value in waits:
                            pe.wait_ge(s_, value)
                        for n in range(TB):
                            mm = pe.matmul(dbank[bank][:, n * P // 2:(n + 1) * P // 2], lhs(n), rhs(n),
                                           start=True, stop=True)
                        mm.then_inc(delta_products, 1)

                    if t == 1:
                        pe.wait_ge(delta_vec, d(h, D_DVE, "tab"))
                        pe.wait_ge(gemm_read, 2 * (h * UNITS + UNITS))
                        for i in (0, 1):
                            turn(side_bank[i], lambda n: nk[:, chunk(n)], [])
                    if t == 2:
                        for i in (0, 1):
                            turn(dbank[i], lambda n: nq[:, chunk(n)], [])
                    if t == 5:
                        for i in (0, 1):
                            turn(z_pair[i], lambda n: rows[:, 1, n:n + 1].to_broadcast([P, P]),
                                 [(delta_vec, d(h, D_DVE, "gq"))])
                    if t == 6:
                        for i in (0, 1):
                            turn(dbank[i], lambda n: rows[:, 0, n:n + 1].to_broadcast([P, P]),
                                 [(delta_act, d(h, D_ACT, "sqq"))])
                    if t == 7:
                        for i in (0, 1):
                            turn(side_bank[i], lambda n: nv[:, chunk(n)],
                                 [(delta_act, d(h, D_ACT, f"kd{i}"))])
                    if t == 8:
                        for i in (0, 1):
                            four(z_pair[i], lambda n: ck[:, chunk(n)], lambda n: ck[:, chunk(n)],
                                 [(delta_vec, d(h, D_DVE, f"D{i}"))])
                    if t == 9:
                        for i in (0, 1):
                            four(dbank[i], lambda n: ck[:, chunk(n)], lambda n: nq[:, chunk(n)],
                                 [(delta_vec, d(h, D_DVE, f"T{i}")), (delta_act, d(h, D_ACT, "eg"))])
                    if t == 12:
                        for i in (0, 1):
                            turn(dbank[i], lambda n: X[:, chunk(n)],
                                 [(delta_vec, d(h, D_DVE, "x"))])
                    if LEVEL_SLOT <= t < LEVEL_SLOT + 2 * (LEVELS - 1):
                        level, part = 1 + (t - LEVEL_SLOT) // 2, (t - LEVEL_SLOT) % 2
                        if part == 0:
                            if level == 1:
                                ready = [(delta_act, d(h, D_ACT, "y1"))]
                            else:
                                ready = [(delta_vec, d(h, D_DVE, f"Y{level - 1}"))]
                            eight(lambda n: Cs[level % 2][:, chunk(n)], lambda n: second(Y, level, n), 0,
                                  ready + [(delta_pool, d(h, D_POOL, f"C{level}"))])
                            if level > 1:
                                for i, bank in ((0, dbank[1]), (1, z_pair[1])):
                                    turn(bank, lambda n: Y[:, chunk(n)], [])
                        else:
                            eight(lambda n: X[:, chunk(n)], lambda n: second(R, level, n), 1,
                                  [(delta_act, d(h, D_ACT, f"P{level}"))]
                                  + ([(delta_vec, d(h, D_DVE, f"X{level}1"))] if level > 1 else []))
                    if CHUNK_SLOT <= t < CHUNK_SLOT + 24:
                        n, part = (t - CHUNK_SLOT) // 3, (t - CHUNK_SLOT) % 3
                        if part == 0:
                            pe.wait_ge(delta_vec, d(h, D_DVE, f"s{n - 1}" if n else "s_init"))
                            pe.matmul(dbank[1][:, chunk(0)], ck[:, chunk(n)], S[:, :], start=True,
                                      stop=True).then_inc(delta_products, 1)
                        if part == 1:
                            pe.wait_ge(delta_vec, d(h, D_DVE, f"r{n}"))
                            pe.matmul(dbank[1][:, chunk(1)], Y[:, chunk(n)], rr[:, :], start=True,
                                      stop=True).then_inc(delta_products, 1)
                        if part == 2:
                            pe.wait_ge(delta_act, d(h, D_ACT, f"vn{n}"))
                            if n == 4:
                                pe.wait_ge(delta_act, d(h, D_ACT, "o0"))
                            bank = dbank[0][:, chunk(n % 4)]
                            pe.matmul(bank, cq[:, chunk(n)], S[:, :], start=True, stop=False)
                            pe.matmul(bank, decT[:, chunk(n)], vnew[:, :], start=False, stop=True)
                            pe.matmul(dbank[1][:, chunk(2)], kd[:, chunk(n)], vnew[:, :], start=True,
                                      stop=True).then_inc(delta_products, 1)
                    if t == NORM_SLOT + 2:
                        pe.wait_ge(delta_vec, d(h, D_DVE, "no"))
                        for i in (0, 1):
                            turn(dbank[i], lambda n: ob[:, chunk(n)], [])

                def pe_attn(pe, h, t):
                    if t in (9, 10):
                        i = t - 9
                        pe.wait_ge(delta_act, d(h, D_ACT, f"vb{i}"))
                        for q in range(4):
                            tr = pe.transpose(side_bank[i][:, chunk(q)], nsv[:, chunk(4 * i + q)], identf[:, :])
                        tr.then_inc(attn_products, 1)
                    for i in range(TB):
                        w = (i + 1) * P
                        if t == z_slot(i):
                            if i:
                                pe.wait_ge(attn_act, d(h, A_ACT, f"beta{i - 1}"))
                            else:
                                pe.wait_ge(delta_vec, d(h, D_DVE, "L1"))
                            for lo in range(0, w, HALF):
                                hi = min(w, lo + HALF)
                                pe.matmul(z_bank[:, lo:hi], nsq[:, chunk(i)], nsk[:, lo:hi], start=True, stop=True)
                            pe.matmul(z_bank[:, w - P:w], identb[:, :], z_mask[:, :], start=False, stop=True,
                                      skip_group_check=True).then_inc(attn_products, 1)
                        for r in range(1 + (i >= 4)):
                            if t == z_slot(i) + 3 + r:
                                pe.wait_ge(attn_vec, d(h, A_DVE, f"a{i}"))
                                if r:
                                    pe.wait_ge(attn_vec, d(h, A_DVE, f"t{i}0"))
                                for j in range(4 * r, min(4 * r + 4, i + 1)):
                                    tr = pe.transpose(t_bank[:, chunk(j % 4)], beta[:, chunk(j)], identf[:, :])
                                tr.then_inc(attn_products, 1)
                        if t == z_slot(i) + 5:
                            pe.wait_ge(attn_vec, d(h, A_DVE, f"t{i}{int(i >= 4)}"))
                            if i == 4:
                                pe.wait_ge(attn_act, d(h, A_ACT, "o0"))
                            for j in range(i + 1):
                                mm = pe.matmul(ao_bank[:, chunk(i % 4)], sv[:, j, :], aT[:, j, :],
                                               start=(j == 0), stop=(j == i))
                            mm.then_inc(attn_products, 1)

                def pe_gemm(pe, h, t):
                    u, half, part = t // 8, t % 8 // 4, t % 4
                    U = h * UNITS + UNITS + u
                    if part == 0:
                        pe.wait_ge(gemm_read, 2 * U + half - 1)
                        if half == 0:
                            pe.wait_ge(hi_split, U + 1)
                            pe.wait_ge(lo_split, U + 1)
                    mm = unit_products(pe, u % 2, half, (2 * part, 2 * part + 1), n1_hi, n1_lo)
                    if part == 3:
                        mm.then_inc(gemm_halves, 1)

                def act_delta(act, h, t):
                    def out(dst, src, func=ACT.Copy, **kw):
                        return act.activation(dst, src, func, **kw)

                    def squares(src, junk, log, chunks):
                        for n in chunks:
                            last = out(junk[:, chunk(n)], src(n), ACT.Square, accum_out=sums[:, log, n:n + 1])
                        last.then_inc(delta_act, 1)

                    if t == 1:
                        act.wait_ge(delta_products, d(h, D_PE, "k1"))
                        squares(lambda n: side_bank[n // 4][:, chunk(n % 4)], X, 1, range(TB))
                    if t == 2:
                        act.wait_ge(delta_products, d(h, D_PE, "q1"))
                        squares(lambda n: dbank[n // 4][:, chunk(n % 4)], Y, 0, range(TB))
                    if t == 3:
                        act.wait_ge(delta_act, d(h, D_ACT, "sqq"))
                        out(logs[:, 0, :], sums[:, 0, :], ACT.Ln, bias=eps_q[:, :], scale=float(P)).then_inc(delta_act, 1)
                        out(logs[:, 1, :], sums[:, 1, :], ACT.Ln, bias=eps[:, :]).then_inc(delta_act, 1)
                        act.wait_ge(delta_act, d(h, D_ACT, "lnk"))
                        out(inv[:, 0, :], logs[:, 1, :], ACT.Exp, scale=-0.5).then_inc(delta_act, 1)
                    if t == 4:
                        out(ck[:, :], nk[:, :]).then_inc(delta_act, 1)
                        act.wait_ge(delta_vec, d(h, D_DVE, "nb"))
                        for i in (0, 1):
                            for q in range(4):
                                n = 4 * i + q
                                last = out(kd[:, chunk(n)], side_bank[i][:, chunk(q)], scale=col(EGL, n))
                            last.then_inc(delta_act, 1)
                    if t == 6:
                        act.wait_ge(delta_products, d(h, D_PE, "gq1"))
                        out(R[:, :], psum[:, 6:8, :].rearrange("p b n -> p (b n)"), ACT.Exp).then_inc(delta_act, 1)
                        act.wait_ge(delta_vec, d(h, D_DVE, "D1"))
                        out(dec[:, :], dec[:, :], ACT.Exp, scale=-1.0).then_inc(delta_act, 1)
                    if t == 7:
                        act.wait_ge(delta_vec, d(h, D_DVE, "T1"))
                        out(decT[:, :], decT[:, :], ACT.Exp).then_inc(delta_act, 1)
                        for i in (0, 1):
                            act.wait_ge(delta_products, d(h, D_PE, f"v{i}"))
                            for q in range(4):
                                n = 4 * i + q
                                last = out(vb[:, chunk(n)], side_bank[i][:, chunk(q)], scale=col(BETA, n))
                            last.then_inc(delta_act, 1)
                    if t == 10:
                        out(cg[:, :], ng[:, :]).then_inc(delta_act, 1)
                    if t == 12:
                        for i in (0, 1):
                            act.wait_ge(delta_products, d(h, D_PE, f"y{i}"))
                            out(Y[:, halves(i)], dbank[i]).then_inc(delta_act, 1)
                    if LEVEL_SLOT <= t < LEVEL_SLOT + 2 * (LEVELS - 1) and (t - LEVEL_SLOT) % 2 == 0:
                        level = 1 + (t - LEVEL_SLOT) // 2
                        act.wait_ge(delta_products, d(h, D_PE, f"P{level}"))
                        if level == 1:
                            act.wait_ge(delta_vec, d(h, D_DVE, "cq"))
                        out(blocks(R, level)[:, :, 1, :], packed(dbank[0], level)).then_inc(delta_act, 1)
                    if CHUNK_SLOT <= t < CHUNK_SLOT + 24:
                        n, part = (t - CHUNK_SLOT) // 3, (t - CHUNK_SLOT) % 3
                        if part == 1:
                            act.wait_ge(delta_products, d(h, D_PE, f"vn{n}"))
                            out(vnew[:, :], dbank[1][:, chunk(1)]).then_inc(delta_act, 1)
                        if part == 2 and n % 4 == 3:
                            act.wait_ge(delta_products, d(h, D_PE, f"ds{n}"))
                            if n == 3:
                                act.wait_ge(ob_stored, h * 32)
                            out(ob[:, halves(n // 4)], dbank[0]).then_inc(delta_act, 1)
                        if part == 2 and n == 4:
                            act.wait_ge(delta_act, d(h, D_ACT, "o0"))
                            squares(lambda n: ob[:, chunk(n)], R, 2, range(4))
                    if t == NORM_SLOT - 2:
                        act.wait_ge(delta_act, d(h, D_ACT, "o1"))
                        squares(lambda n: ob[:, chunk(n)], R, 2, range(4, TB))
                    if t == NORM_SLOT:
                        act.wait_ge(delta_act, d(h, D_ACT, "sqo1"))
                        out(logs[:, 2, :], sums[:, 2, :], ACT.Ln, bias=eps[:, :], scale=1.0 / P).then_inc(delta_act, 1)
                        act.wait_ge(delta_act, d(h, D_ACT, "lno"))
                        out(inv[:, 1, :], logs[:, 2, :], ACT.Exp, scale=-0.5).then_inc(delta_act, 1)
                    if t == 61:
                        for i in (0, 1):
                            act.wait_ge(delta_vec, d(h, D_DVE, f"fo{i}"))
                            act.dma_start(o_d[0][bass.ds(h, 1), :, halves(i)].rearrange("o p n -> (o p) n"),
                                          ob[:, halves(i)]).then_inc(ob_stored, 16)

                def act_attn(act, h, t):
                    if t in (9, 10):
                        i = t - 9
                        act.wait_ge(attn_products, d(h, A_PE, f"v{i}"))
                        act.activation(sv[:, 4 * i:4 * i + 4, :], side_bank[i], ACT.Copy).then_inc(attn_act, 1)
                    for i in range(TB):
                        w = (i + 1) * P
                        if t == z_slot(i):
                            act.wait_ge(attn_products, d(h, A_PE, f"z{i}"))
                            if i:
                                act.wait_ge(attn_products, d(h, A_PE, f"t{i - 1}{int(i > 4)}"))
                            act.activation(keep[:, 0:w], z_bank[:, 0:w], ACT.Sigmoid, scale=-SCALE).then_inc(attn_act, 1)
                            act.activation(beta[:, 0:w], z_bank[:, 0:w], ACT.Sigmoid, scale=SCALE).then_inc(attn_act, 1)
                        if t == z_slot(i) + 5 and i % 4 == 3:
                            act.wait_ge(attn_products, d(h, A_PE, f"o{i}"))
                            act.wait_ge(ao_stored, h * 32 + (i // 4) * 16)
                            act.activation(ao[:, :], ao_bank, ACT.Copy).then_inc(attn_act, 1)
                            act.wait_ge(attn_act, d(h, A_ACT, f"o{i // 4}"))
                            act.dma_start(o_d[1][bass.ds(h, 1), :, halves(i // 4)].rearrange("o p n -> (o p) n"),
                                          ao[:, :]).then_inc(ao_stored, 16)

                def half_before(t, slots):
                    return (t - slots) // 4 // 2, (t - slots) // 4 % 2

                def act_gemm(act, h, t, last):
                    U0 = h * UNITS + UNITS
                    if t % 4 == 0:
                        u, half = half_before(t, 4) if t else (SB_K, 1)
                        act.wait_ge(gemm_halves, 2 * U0 + t // 4)
                        if last and t:
                            gate(act, u, half, bass_gate(KB + u), h)
                        elif u == GATE_A:
                            gate(act, u, half, None, h)
                        elif u in CONVOLVED:
                            if half == 0:
                                act.wait_ge(conv_taps, h * 24 + 8 * (u - DN_V))
                            act.activation(pre[:, 3 + half * HALF:3 + (half + 1) * HALF], gemm_bank[half],
                                           ACT.Copy).then_inc(gemm_read, 1)
                        else:
                            dst = {SB_V: nsv, SB_Q: nsq, SB_K: nsk, DN_G: ng}[u]
                            if u == SB_V:
                                act.wait_ge(attn_products, d(h, A_PE, "v1"))
                            if u == DN_G:
                                act.wait_ge(delta_act, d(h, D_ACT, "cg"))
                            if u == SB_Q:
                                act.wait_ge(attn_products, d(h, A_PE, "z7"))
                            act.activation(dst[:, halves(half)], gemm_bank[half], ACT.Copy).then_inc(gemm_read, 1)
                    if t % 8 == 1 and not (last and t // 8 == UNITS - 1):
                        u = t // 8 + 1
                        split_hi(act, U0 + u, u % 2, 16 * (4 * h + 4 + u // 2 + 1))
                    if t % 4 == 2 and t >= 6 and not last:
                        u, half = half_before(t, 8) if t >= 8 else (0, 0)
                        if t >= 8 and u in SILU:
                            n = 2 * (u - DN_V) + half
                            if u in CONVOLVED:
                                act.wait_ge(conv_taps, h * 24 + 4 * n + 4)
                            else:
                                act.wait_ge(gemm_read, 2 * (U0 + u) + half + 1)
                            if n >= 2:
                                act.wait_ge(silus, h * 8 + n - 1)
                            else:
                                act.wait_ge(gate_stored[half], h * 16 + 16)
                            y = {DN_V: nv, DN_Q: nq, DN_K: nk, DN_G: ng}[u]
                            act.activation(sig[:, halves(half)], y[:, halves(half)], ACT.Sigmoid).then_inc(sigmoids, 1)

                def bass_gate(m):
                    return m

                def gate(act, u, half, row, h):
                    if row is None:
                        if half == 0:
                            act.wait_ge(silus, h * 8)
                        dst = gates_d[bass.ds(h + 1, 1), :, halves(half)].rearrange("o p n -> (o p) n")
                        U = h * UNITS + UNITS
                    else:
                        act.wait_ge(gate_stored[half], 16 * (HEADS - 1 + u))
                        dst = gates_d[row][:, halves(half)]
                        U = h * UNITS + UNITS + u
                    act.activation(sig[:, halves(half)], gemm_bank[half], ACT.Sigmoid).then_inc(gemm_read, 1)
                    act.wait_ge(gemm_read, 2 * U + half + 1)
                    act.dma_start(dst, sig[:, halves(half)]).then_inc(gate_stored[half], 16)

                def vec_delta(v, h, t):
                    if t == 0:
                        v.tensor_copy(cur[:, :, :], tab[:, bass.ds(h, 1), :, :].rearrange("p o a n -> p (o a) n")).then_inc(delta_vec, 1)
                        v.tensor_copy(cwc[:, :, :], cwt[:, bass.ds(cw_head(h), 1), :, :].rearrange("p o a n -> p (o a) n")).then_inc(delta_vec, 1)
                    if t == 3:
                        for step, (row, log, half) in enumerate(((1, 1, 0.5), (2, 1, -0.5), (0, 0, -0.5))):
                            if step == 0:
                                v.wait_ge(delta_act, d(h, D_ACT, "lnk"))
                            v.scalar_tensor_tensor(out=rows[:, row, :], in0=logs[:, log, :], scalar=half,
                                                   in1=cur[:, G, :], op0=ALU.mult, op1=ALU.add).then_inc(delta_vec, 1)
                        v.wait_ge(delta_act, d(h, D_ACT, "rk"))
                        v.tensor_tensor(cur[:, NBEG:EGL + 1, :], cur[:, NBEG:EGL + 1, :],
                                        inv[:, 0:1, :].to_broadcast([P, 2, TB]), ALU.mult).then_inc(delta_vec, 1)
                    if t == 5:
                        for i in (0, 1):
                            v.wait_ge(delta_products, d(h, D_PE, f"gk{i}"))
                            if i == 0:
                                v.wait_ge(delta_vec, d(h, D_DVE, "gc"))
                            for q in range(4):
                                n = 4 * i + q
                                last = v.scalar_tensor_tensor(out=dec[:, chunk(n)], in0=z_pair[i][:, chunk(q)],
                                                              scalar=rows[:, 2, n:n + 1], in1=pos_mask[:, :],
                                                              op0=ALU.subtract, op1=ALU.max)
                            last.then_inc(delta_vec, 1)
                    if t == 6:
                        for i in (0, 1):
                            if i == 0:
                                v.wait_ge(delta_act, d(h, D_ACT, "eg"))
                            for q in range(4):
                                n = 4 * i + q
                                last = v.scalar_tensor_tensor(out=decT[:, chunk(n)], in0=dbank[i][:, chunk(q)],
                                                              scalar=rows[:, 1, n:n + 1], in1=neg_mask[:, :],
                                                              op0=ALU.subtract, op1=ALU.min)
                            last.then_inc(delta_vec, 1)
                    if t == 8:
                        v.wait_ge(delta_act, d(h, D_ACT, "eD"))
                        for i in (0, 1):
                            v.wait_ge(delta_products, d(h, D_PE, f"kk{i}"))
                            for q in range(4):
                                n = 4 * i + q
                                last = v.scalar_tensor_tensor(out=dec[:, chunk(n)], in0=z_pair[i][:, chunk(q)], scalar=col(BETA, n),
                                                              in1=dec[:, chunk(n)], op0=ALU.mult, op1=ALU.mult)
                            last.then_inc(delta_vec, 1)
                    if t == 9:
                        v.wait_ge(delta_act, d(h, D_ACT, "eT"))
                        for i in (0, 1):
                            v.wait_ge(delta_products, d(h, D_PE, f"qk{i}"))
                            v.tensor_tensor(decT[:, halves(i)], dbank[i], decT[:, halves(i)], ALU.mult).then_inc(delta_vec, 1)
                    if t == 10:
                        v.tensor_tensor(cq[:, :], nq[:, :], R[:, :], ALU.mult).then_inc(delta_vec, 1)
                    if t == 11:
                        v.wait_ge(delta_pool, d(h, D_POOL, "C0"))
                        v.tensor_tensor(X[:, :].rearrange("p (n c) -> p n c", n=TB),
                                        identf[:, :].unsqueeze(1).to_broadcast([P, TB, P]),
                                        Cs[0][:, :].rearrange("p (n c) -> p n c", n=TB), ALU.subtract).then_inc(delta_vec, 1)
                    if LEVEL_SLOT < t < LEVEL_SLOT + 2 * (LEVELS - 1) and (t - LEVEL_SLOT) % 2 == 0:
                        level = 1 + (t - LEVEL_SLOT) // 2
                        for i, bank in ((0, dbank[1]), (1, z_pair[1])):
                            v.wait_ge(delta_products, d(h, D_PE, f"X{level}{i}"))
                            v.tensor_copy(X[:, halves(i)], bank).then_inc(delta_vec, 1)
                    if LEVEL_SLOT <= t < LEVEL_SLOT + 2 * (LEVELS - 1) and (t - LEVEL_SLOT) % 2:
                        level = 1 + (t - LEVEL_SLOT) // 2
                        v.wait_ge(delta_products, d(h, D_PE, f"Y{level}"))
                        cols = blocks(Y, level)[:, :, 1, :]
                        v.tensor_tensor(cols, cols, packed(dbank[1], level), ALU.subtract).then_inc(delta_vec, 1)
                    if CHUNK_SLOT <= t < CHUNK_SLOT + 24:
                        n, part = (t - CHUNK_SLOT) // 3, (t - CHUNK_SLOT) % 3
                        if part == 0:
                            if n == 0:
                                v.memset(S[:, :], 0.0).then_inc(delta_vec, 1)
                            v.wait_ge(delta_products, d(h, D_PE, f"ks{n}"))
                            v.scalar_tensor_tensor(out=rr[:, :], in0=dbank[1][:, chunk(0)], scalar=col(NBEG, n),
                                                   in1=vb[:, chunk(n)], op0=ALU.mult, op1=ALU.add).then_inc(delta_vec, 1)
                        if part == 2:
                            v.wait_ge(delta_products, d(h, D_PE, f"ds{n}"))
                            v.scalar_tensor_tensor(out=S[:, :], in0=S[:, :], scalar=col(EGLAST, n),
                                                   in1=dbank[1][:, chunk(2)], op0=ALU.mult, op1=ALU.add).then_inc(delta_vec, 1)
                    if t == NORM_SLOT + 1:
                        v.wait_ge(delta_act, d(h, D_ACT, "ero"))
                        v.tensor_tensor(ob[:, :].rearrange("p (n c) -> p n c", n=TB),
                                        ob[:, :].rearrange("p (n c) -> p n c", n=TB),
                                        inv[:, 1, :].unsqueeze(2).to_broadcast([P, TB, P]), ALU.mult).then_inc(delta_vec, 1)
                    if t in (NORM_SLOT + 3, NORM_SLOT + 4):
                        i = t - NORM_SLOT - 3
                        v.wait_ge(delta_products, d(h, D_PE, f"to{i}"))
                        v.scalar_tensor_tensor(out=ob[:, halves(i)], in0=dbank[i], scalar=dnw[:, :],
                                               in1=cg[:, halves(i)], op0=ALU.mult, op1=ALU.mult).then_inc(delta_vec, 1)

                def vec_attn(v, h, t):
                    for i in range(TB):
                        w = (i + 1) * P
                        if t == z_slot(i) + 1:
                            v.wait_ge(attn_act, d(h, A_ACT, f"keep{i}"))
                            v.tensor_tensor_scan(keep[:, w - 1::-1], keep[:, w - 1::-1], keep[:, w - 1::-1], 1.0,
                                                 ALU.mult, ALU.bypass).then_inc(attn_vec, 1)
                        if t == z_slot(i) + 2:
                            v.wait_ge(attn_act, d(h, A_ACT, f"beta{i}"))
                            v.wait_ge(attn_vec, d(h, A_DVE, f"scan{i}"))
                            v.tensor_tensor(beta[:, 0:w - 1], beta[:, 0:w - 1], keep[:, 1:w], ALU.mult).then_inc(attn_vec, 1)
                        for r in range(1 + (i >= 4)):
                            if t == z_slot(i) + 3 + r:
                                v.wait_ge(attn_products, d(h, A_PE, f"t{i}{r}"))
                                if i and r == 0:
                                    v.wait_ge(attn_products, d(h, A_PE, f"o{i - 1}"))
                                n = min(4, i + 1 - 4 * r)
                                v.tensor_copy(aT[:, 4 * r:4 * r + n, :], t_bank[:, 0:n * P]).then_inc(attn_vec, 1)

                def vec_gemm(v, h, t, last):
                    if last or t < 4:
                        return
                    u, half = half_before(t, 4)
                    if u in CONVOLVED:
                        n = 2 * (u - DN_V) + half
                        j = t % 4
                        if j == 0:
                            v.wait_ge(gemm_read, 2 * (h * UNITS + UNITS + u) + half + 1)
                            if half == 0:
                                used = {DN_V: (delta_products, d(h, D_PE, "v1")),
                                        DN_Q: (delta_products, d(h, D_PE, "qk1")),
                                        DN_K: (delta_act, d(h, D_ACT, "ck"))}[u]
                                v.wait_ge(*used)
                        y = {DN_V: nv, DN_Q: nq, DN_K: nk}[u][:, halves(half)]
                        w = cwc[:, {DN_Q: 0, DN_K: 1, DN_V: 2}[u], :]
                        conv_tap(v, y, w, half, j, conv_taps, h * 24 + 4 * n + j)

                def pool_delta(pool, h, t):
                    g = nc.gpsimd
                    slot = [8, 8, 12] + [LEVEL_SLOT + 2 * n - 5 for n in range(3, LEVELS)]
                    for level in [n for n in range(LEVELS) if slot[n] == t]:
                        if level == 0:
                            pool.wait_ge(delta_vec, d(h, D_DVE, "L1"))
                        elif level == 2:
                            pool.wait_ge(delta_vec, d(h, D_DVE, "x"))
                        elif level > 2:
                            pool.wait_ge(delta_products, d(h, D_PE, f"P{level - 2}"))
                        g.tensor_tensor(Cs[level % 2][:, :].rearrange("p (n c) -> p n c", n=TB),
                                        dec[:, :].rearrange("p (n c) -> p n c", n=TB),
                                        level_mask[:, level, :].unsqueeze(1).to_broadcast([P, TB, P]),
                                        ALU.mult).then_inc(delta_pool, 1)

                def pool_gemm(pool, h, t, last):
                    U0 = h * UNITS + UNITS
                    if t % 8 == 1 and not (last and t // 8 == UNITS - 1):
                        u = t // 8 + 1
                        split_lo(pool, U0 + u, u % 2)
                    if t % 4 == 2 and t >= 8 and not last:
                        u, half = half_before(t, 8)
                        if u in SILU:
                            n = 2 * (u - DN_V) + half
                            y = {DN_V: nv, DN_Q: nq, DN_K: nk, DN_G: ng}[u][:, halves(half)]
                            pool.wait_ge(sigmoids, h * 8 + n + 1)
                            pool.tensor_tensor(y, y, sig[:, halves(half)], ALU.mult).then_inc(silus, 1)

                def cw_head(h):
                    return h + 1 if not isinstance(h, int) or h < HEADS - 1 else HEADS - 1

                with nc.Block() as block:
                    @block.sync
                    def _(sp):
                        with sp.Fori(0, HEADS - 1) as h:
                            for u in range(1, UNITS + 1):
                                load_unit(sp, h * UNITS + UNITS + u, u % 2,
                                          w_main[bass.ds(h + (BLOCK[u % UNITS] + 1 + u // UNITS), 1)].rearrange("o p k n -> (o p) k n"))
                        for u in range(1, KB):
                            load_unit(sp, HEADS * UNITS + u, u % 2,
                                      w_main[GATE_B_BLOCK + u])

                    @block.tensor
                    def _(pe):
                        def head(h):
                            for t in range(SLOTS):
                                pe_delta(pe, h, t)
                                pe_attn(pe, h, t)
                                pe_gemm(pe, h, t)

                        with pe.Fori(0, HEADS - 1) as h:
                            head(h)
                        head(HEADS - 1)

                    @block.scalar
                    def _(act):
                        def head(h, last):
                            for t in range(SLOTS):
                                if t == 0:
                                    act_gemm(act, h, t, last)
                                act_delta(act, h, t)
                                act_attn(act, h, t)
                                if t:
                                    act_gemm(act, h, t, last)

                        with act.Fori(0, HEADS - 1) as h:
                            head(h, False)
                        head(HEADS - 1, True)
                        act.wait_ge(gemm_halves, 2 * UNITS * (HEADS + 1))
                        gate(act, KB - 1, 1, 2 * KB - 1, HEADS - 1)
                        for i in (0, 1):
                            act.wait_ge(gate_stored[i], 16 * (HEADS - 1 + KB))
                        act.wait_ge(ao_stored, 32 * HEADS)
                        act.wait_ge(ob_stored, 32 * HEADS)

                    @block.vector
                    def _(v):
                        def head(h, last):
                            for t in range(SLOTS):
                                vec_delta(v, h, t)
                                vec_attn(v, h, t)
                                vec_gemm(v, h, t, last)

                        with v.Fori(0, HEADS - 1) as h:
                            head(h, False)
                        head(HEADS - 1, True)

                    @block.gpsimd
                    def _(pool):
                        def head(h, last):
                            for t in range(SLOTS):
                                pool_gemm(pool, h, t, last)
                                pool_delta(pool, h, t)

                        with pool.Fori(0, HEADS - 1) as h:
                            head(h, False)
                        head(HEADS - 1, True)

        if stop_after < 3:
            return
        M0 = UNITS * (HEADS + 1)
        tail = ExitStack()
        with tail:
            x1 = sb("x1", [P, TB, D], F32, tail)
            merge = ExitStack()
            with merge:
                mix_hi = sb("mix_hi", [P, KB, T], F32R, merge)
                mix_lo = sb("mix_lo", [P, KB, T], F32R, merge)
                gather = ExitStack()
                with gather:
                    so_hi = sb("so_hi", [P, KB, T], F32R, gather)
                    so_lo = sb("so_lo", [P, KB, T], F32R, gather)
                    stage = [sb(f"stage{i}", [P, T], F32, gather) for i in (0, 1)]
                    gbuf = [sb(f"gbuf{i}", [P, T], F32, gather) for i in (0, 1)]
                    mixa = x1

                    o_landed = [sem(f"o_landed{i}", gather) for i in (0, 1)]
                    g_landed = [sem(f"g_landed{i}", gather) for i in (0, 1)]
                    o_hi = sem("o_hi", gather)
                    o_lo = sem("o_lo", gather)
                    gated = sem("gated", gather)
                    summed = sem("summed", gather)
                    m_hi = sem("m_hi", gather)
                    m_lo = sem("m_lo", gather)

                    with nc.Block() as block:
                        @block.sync
                        def _(sp):
                            def load_o(n):
                                if n >= 2:
                                    sp.wait_ge(o_lo, n - 1)
                                sp.dma_start(stage[n % 2][:, :], o_d[n // HEADS][n % HEADS]).then_inc(o_landed[n % 2], 16)

                            load_unit(sp, M0, 0, w_proj_dn[0])
                            load_unit(sp, M0 + 1, 1, w_proj_dn[1])
                            for n in range(HEADS):
                                load_o(n)
                            for m in range(2 * KB):
                                if m >= 2:
                                    load_unit(sp, M0 + m, m % 2, (w_proj_dn if m < KB else w_proj_sb)[m % KB])
                                    sp.wait_ge(gated, 2 * (m - 1))
                                    if m >= KB + 2:
                                        sp.wait_ge(summed, 2 * (m - 1 - KB))
                                sp.dma_start(gbuf[m % 2][:, :], gates_d[m]).then_inc(g_landed[m % 2], 16)
                                if m < HEADS:
                                    load_o(HEADS + m)
                            load_unit(sp, M0 + 2 * KB, 0, w_up[0])
                            load_unit(sp, M0 + 2 * KB + 1, 1, w_up[w_up.shape[0] // 2])

                        @block.scalar
                        def _(act):
                            def split_o(n):
                                act.wait_ge(o_landed[n % 2], 16 * (n // 2 + 1))
                                act.activation((mix_hi if n < HEADS else so_hi)[:, n % HEADS, :], stage[n % 2][:, :],
                                               ACT.Copy).then_inc(o_hi, 1)

                            split_hi(act, M0, 0, 16 * (M0 // 2 + 1))
                            for n in range(HEADS):
                                split_o(n)
                            for m in range(2 * KB):
                                if m < 2 * KB - 1:
                                    split_hi(act, M0 + m + 1, (m + 1) % 2, 16 * ((M0 + m + 1) // 2 + 1))
                                if m < HEADS:
                                    split_o(HEADS + m)
                                if m >= KB:
                                    for half in (0, 1):
                                        cols = slice(half * HALF, (half + 1) * HALF)
                                        act.wait_ge(summed, 2 * (m - KB) + half + 1)
                                        act.activation(mix_hi[:, m - KB, cols], mixa[:, m - KB, cols],
                                                       ACT.Copy).then_inc(m_hi, 1)

                        @block.gpsimd
                        def _(pool):
                            split_lo(pool, M0, 0)
                            for m in range(2 * KB):
                                if m < 2 * KB - 1:
                                    split_lo(pool, M0 + m + 1, (m + 1) % 2)
                                if m >= KB:
                                    for half in (0, 1):
                                        cols = slice(half * HALF, (half + 1) * HALF)
                                        pool.wait_ge(m_hi, 2 * (m - KB) + half + 1)
                                        pool.tensor_tensor(mix_lo[:, m - KB, cols], mixa[:, m - KB, cols],
                                                           mix_hi[:, m - KB, cols].bitcast(F32),
                                                           ALU.subtract).then_inc(m_lo, 1)

                        @block.vector
                        def _(v):
                            def low_o(n):
                                v.wait_ge(o_hi, n + 1)
                                hi, lo = (mix_hi, mix_lo) if n < HEADS else (so_hi, so_lo)
                                v.tensor_tensor(lo[:, n % HEADS, :], stage[n % 2][:, :], hi[:, n % HEADS, :].bitcast(F32),
                                                ALU.subtract).then_inc(o_lo, 1)

                            for n in range(HEADS):
                                low_o(n)
                            for m in range(2 * KB):
                                if m < HEADS:
                                    low_o(HEADS + m)
                                v.wait_ge(g_landed[m % 2], 16 * (m // 2 + 1))
                                for half in (0, 1):
                                    cols = slice(half * HALF, (half + 1) * HALF)
                                    v.wait_ge(gemm_halves, 2 * (M0 + m) + half + 1)
                                    dst = mixa[:, m, cols] if m < KB else gbuf[m % 2][:, cols]
                                    v.tensor_tensor(dst, gemm_bank[half], gbuf[m % 2][:, cols], ALU.mult)\
                                        .then_inc(gated, 1)
                                    if m >= KB:
                                        v.wait_ge(gated, 2 * m + half + 1)
                                        v.tensor_tensor(mixa[:, m - KB, cols], mixa[:, m - KB, cols], dst,
                                                        ALU.add).then_inc(summed, 1)

                        @block.tensor
                        def _(pe):
                            for m in range(2 * KB):
                                U = M0 + m
                                pe.wait_ge(hi_split, U + 1)
                                pe.wait_ge(lo_split, U + 1)
                                for half in (0, 1):
                                    if m:
                                        pe.wait_ge(gated, 2 * m + half - 1)
                                    else:
                                        pe.wait_ge(gemm_read, 2 * M0)
                                    for k in range(KB):
                                        if m % KB == 0 and half == 0:
                                            pe.wait_ge(o_lo, (m // KB) * HEADS + k + 1)
                                        hi, lo = (mix_hi, mix_lo) if m < KB else (so_hi, so_lo)
                                        mm = unit_products(pe, m % 2, half, (k,), hi, lo)
                                    mm.then_inc(gemm_halves, 1)

                outp = ExitStack()
                with outp:
                    wo_raw = [sb(f"wo_raw{i}", [P, KB // 2, HALF], F32, outp) for i in (0, 1)]
                    wo_hi = [sb(f"wo_hi{i}", [P, KB, HALF], F32R, outp) for i in (0, 1)]
                    wo_lo = [sb(f"wo_lo{i}", [P, KB, HALF], F32R, outp) for i in (0, 1)]
                    wo_landed = [sem(f"wo_landed{i}", outp) for i in (0, 1)]
                    x_in = [sem(f"x_in{i}", outp) for i in range(TB)]
                    wo_h = sem("wo_h", outp)
                    wo_l = sem("wo_l", outp)
                    rows = sem("rows", outp)
                    added = sem("added", outp)

                    with nc.Block() as block:
                        @block.sync
                        def _(sp):
                            for n in range(4):
                                f, part = n // 2, n % 2
                                if n >= 2:
                                    sp.wait_ge(wo_l, n - 1)
                                sp.dma_start(wo_raw[part][:, :, :], w_out[f][:, part * KB // 2:(part + 1) * KB // 2, :]
                                             ).then_inc(wo_landed[part], 16)
                                if n == 1:
                                    for i in range(TB):
                                        sp.dma_start(x1[:, i, :], x[0, i * P:(i + 1) * P, :]).then_inc(x_in[i], 16)

                        @block.scalar
                        def _(act):
                            for n in range(4):
                                f, part = n // 2, n % 2
                                act.wait_ge(wo_landed[part], 16 * (f + 1))
                                act.activation(wo_hi[f][:, part * KB // 2:(part + 1) * KB // 2, :], wo_raw[part][:, :, :],
                                               ACT.Copy).then_inc(wo_h, 1)

                        @block.vector
                        def _(v):
                            for n in range(4):
                                f, part = n // 2, n % 2
                                ks = slice(part * KB // 2, (part + 1) * KB // 2)
                                v.wait_ge(wo_h, n + 1)
                                v.tensor_tensor(wo_lo[f][:, ks, :], wo_raw[part][:, :, :],
                                                wo_hi[f][:, ks, :].bitcast(F32), ALU.subtract).then_inc(wo_l, 1)
                            for n in range(2 * TB):
                                f, i = n // TB, n % TB
                                cols = slice(f * HALF, (f + 1) * HALF)
                                if f == 0:
                                    v.wait_ge(x_in[i], 16)
                                v.wait_ge(rows, n + 1)
                                v.tensor_tensor(x1[:, i, cols], psum[:, n % 4, :], x1[:, i, cols], ALU.add)\
                                    .then_inc(added, 1)

                        @block.tensor
                        def _(pe):
                            for n in range(2 * TB):
                                f, i = n // TB, n % TB
                                if n >= 4:
                                    pe.wait_ge(added, n - 3)
                                for k in range(KB):
                                    if i == 0 and k % (KB // 2) == 0:
                                        pe.wait_ge(wo_l, 2 * f + k // (KB // 2) + 1)
                                    for j, (a, w) in enumerate(((mix_hi, wo_hi), (mix_hi, wo_lo), (mix_lo, wo_hi))):
                                        mm = pe.matmul(psum[:, n % 4, :], a[:, k, i * P:(i + 1) * P], w[f][:, k, :],
                                                       start=(k == 0 and j == 0), stop=(k == KB - 1 and j == 2))
                                mm.then_inc(rows, 1)

            FB = w_up.shape[0] // 2
            GROUPS = FB // 2
            F0 = M0 + 2 * KB
            n2_hi = sb("n2_hi", [P, KB, T], F32R, tail)
            n2_lo = sb("n2_lo", [P, KB, T], F32R, tail)
            ss2 = sb("ss2", [P, TB], F32, tail)
            rstd2 = sb("rstd2", [P, TB], F32, tail)
            n2w = sb("n2w", [P, KB], F32, tail)
            norm2p = ExitStack()
            with norm2p:
                xr = [sb(f"xr{i}", [P, D], F32, norm2p) for i in range(4)]
                sq2 = [sb(f"sq2{i}", [P, D], F32, norm2p) for i in (0, 1)]
                n2w_in = sem("n2w_in", norm2p)
                r_ss, r_std, r_rec, r_norm = (sem(n, norm2p) for n in ("r_ss", "r_std", "r_rec", "r_norm"))
                r_turn, r_hi, r_lo = (sem(n, norm2p) for n in ("r_turn", "r_hi", "r_lo"))
                with nc.Block() as block:
                    @block.sync
                    def _(sp):
                        sp.dma_start(n2w[:, :], norm2).then_inc(n2w_in, 16)

                    @block.scalar
                    def _(act):
                        for i in range(TB):
                            if i >= 2:
                                act.wait_ge(r_ss, i - 1)
                            act.activation(sq2[i % 2][:, :], x1[:, i, :], ACT.Square, accum_out=ss2[:, i:i + 1]).then_inc(r_ss, 1)
                        for i in range(TB):
                            if i == 0:
                                act.wait_ge(r_ss, TB)
                                act.activation(ss2[:, :], ss2[:, :], ACT.Sqrt, bias=eps[:, :], scale=1.0 / D).then_inc(r_std, 1)
                                act.wait_ge(r_rec, 1)
                            if i >= 4:
                                act.wait_ge(r_turn, KB)
                            act.activation(xr[i % 4][:, :], x1[:, i, :], ACT.Copy, scale=rstd2[:, i:i + 1]).then_inc(r_norm, 1)
                            if i % 4 == 3:
                                act.wait_ge(n2w_in, 16)
                                for k in range(KB):
                                    act.wait_ge(r_turn, KB * (i // 4) + k + 1)
                                    act.activation(n2_hi[:, k, (i // 4) * HALF:(i // 4 + 1) * HALF], psum[:, 2 + k % 4, :],
                                                   ACT.Copy, scale=n2w[:, k:k + 1]).then_inc(r_hi, 1)

                    @block.vector
                    def _(v):
                        v.wait_ge(r_std, 1)
                        v.reciprocal(rstd2[:, :], ss2[:, :]).then_inc(r_rec, 1)
                        for n in range(2 * KB):
                            k, cols = n % KB, slice((n // KB) * HALF, (n // KB + 1) * HALF)
                            v.wait_ge(r_hi, n + 1)
                            v.scalar_tensor_tensor(out=n2_lo[:, k, cols], in0=psum[:, 2 + k % 4, :], scalar=n2w[:, k:k + 1],
                                                   in1=n2_hi[:, k, cols].bitcast(F32), op0=ALU.mult,
                                                   op1=ALU.subtract).then_inc(r_lo, 1)

                    @block.tensor
                    def _(pe):
                        for n in range(2 * KB):
                            k = n % KB
                            if k == 0:
                                pe.wait_ge(r_norm, 4 * (n // KB) + 4)
                            if n >= 4:
                                pe.wait_ge(r_lo, n - 3)
                            for i in range(4):
                                tr = pe.transpose(psum[:, 2 + k % 4, i * P:(i + 1) * P], xr[i][:, k * P:(k + 1) * P], identf[:, :])
                            tr.then_inc(r_turn, 1)

            FSLOTS = 32
            gb, ub = sb("gb", [P, T], F32, tail), sb("ub", [P, T], F32, tail)
            fpre = sb("fpre", [P, 2 + T], F32, tail)
            a_hi = sb("a_hi", [P, 2, T], F32R, tail)
            a_lo = sb("a_lo", [P, 2, T], F32R, tail)
            wd_raw = sb("wd_raw", [P, 2, D], F32, tail)
            wd_hi = sb("wd_hi", [P, 2, D], F32R, tail)
            wd_lo = sb("wd_lo", [P, 2, D], F32R, tail)
            taps = sb("taps", [P, 2, FB, 3], F32, tail)
            tapc = sb("tapc", [P, 2, 2, 3], F32, tail)
            wf = sb("wf", [P, D], F32, tail)
            sqf = [sb(f"sqf{i}", [P, D], F32, tail) for i in (0, 1)]
            stdf = sb("stdf", [P, TB], F32, tail)
            small_in = sem("small_in", tail)
            wd_landed = sem("wd_landed", tail)
            wd_his = sem("wd_his", tail)
            wd_los = sem("wd_los", tail)
            f_read = sem("f_read", tail)
            f_pad = sem("f_pad", tail)
            tap_in = sem("tap_in", tail)
            f_conv = sem("f_conv", tail)
            f_silu = sem("f_silu", tail)
            f_prod = sem("f_prod", tail)
            f_hi = sem("f_hi", tail)
            f_lo = sem("f_lo", tail)
            down = sem("down", tail)
            down_added = sem("down_added", tail)
            e_ss, e_std, e_rec, e_out, stored = (sem(n, tail) for n in ("e_ss", "e_std", "e_rec", "e_out", "stored"))

            def down_output(pe, g, n):
                i, f = n // 2, n % 2
                if n >= 4 or not (isinstance(g, int) and g == 0):
                    pe.wait_ge(down_added, 16 * g + n - 3)
                if n == 0:
                    pe.wait_ge(wd_los, g + 1)
                    pe.wait_ge(f_lo, 4 * g + 3)
                if n == 8:
                    pe.wait_ge(f_lo, 4 * g + 4)
                bank = psum[:, 2 + n % 4, :]
                for k in (0, 1):
                    for j, (a, w) in enumerate(((a_hi, wd_hi), (a_hi, wd_lo), (a_lo, wd_hi))):
                        mm = pe.matmul(bank, a[:, k, i * P:(i + 1) * P], w[:, k, f * HALF:(f + 1) * HALF],
                                       start=(k == 0 and j == 0), stop=(k == 1 and j == 2))
                mm.then_inc(down, 1)

            def down_add(v, g, n):
                i, f = n // 2, n % 2
                v.wait_ge(down, 16 * g + n + 1)
                v.tensor_tensor(x1[:, i, f * HALF:(f + 1) * HALF], psum[:, 2 + n % 4, :],
                                x1[:, i, f * HALF:(f + 1) * HALF], ALU.add).then_inc(down_added, 1)

            def events(t):
                H = t // 4 - 1
                return (H, t % 4, 0) if H >= 0 else (7, t % 4, 1)

            def hcols(half):
                return slice(half * HALF, (half + 1) * HALF)

            def act_ffn(act, g, t, only_events=False):
                H, phase, back = events(t)
                u, half = H // 2, H % 2
                gg = g - back
                if not (isinstance(gg, int) and gg < 0):
                    if phase == 0:
                        act.wait_ge(gemm_halves, 2 * F0 + 8 * gg + H + 1)
                        if half == 0:
                            if not (isinstance(gg, int) and gg == 0 and H == 0):
                                act.wait_ge(f_conv, 24 * gg + 3 * H)
                            else:
                                act.wait_ge(f_pad, 1)
                        act.activation(fpre[:, 2 + half * HALF:2 + (half + 1) * HALF], gemm_bank[half],
                                       ACT.Copy).then_inc(f_read, 1)
                    if phase == 3:
                        act.wait_ge(f_conv, 24 * gg + 3 * H + 3)
                        if u % 2 == 0:
                            act.activation(gb[:, hcols(half)], gb[:, hcols(half)], ACT.Silu).then_inc(f_silu, 1)
                        else:
                            act.wait_ge(f_prod, 4 * gg + 2 * (u // 2) + half + 1)
                            if not (isinstance(gg, int) and gg == 0):
                                act.wait_ge(down, 16 * gg - 8 + 8 * half)
                            act.activation(a_hi[:, u // 2, hcols(half)], ub[:, hcols(half)], ACT.Copy).then_inc(f_hi, 1)
                if only_events:
                    return
                if t % 8 == 1:
                    u = t // 8 + 1
                    if not (isinstance(g, int) and g == GROUPS - 1 and u == 4):
                        split_hi(act, F0 + 4 * g + u, u % 2, 16 * (F0 // 2 + 2 * g + u // 2 + 1))
                if t == 20:
                    act.wait_ge(wd_landed, 16 * (g + 1))
                    if not (isinstance(g, int) and g == 0):
                        act.wait_ge(down, 16 * g)
                    act.activation(wd_hi[:, :, :], wd_raw[:, :, :], ACT.Copy).then_inc(wd_his, 1)

            def vec_ffn(v, g, t, only_events=False):
                H, phase, back = events(t)
                u, half = H // 2, H % 2
                gg = g - back
                if t >= 1 and t <= 16 and not (isinstance(g, int) and g == 0):
                    down_add(v, g - 1, t - 1)
                if not (isinstance(gg, int) and gg < 0):
                    buf = (gb if u % 2 == 0 else ub)[:, hcols(half)]
                    if phase < 3:
                        w = tapc[:, u % 2, u // 2, :]
                        x_j = fpre[:, 2 - phase + half * HALF:2 - phase + (half + 1) * HALF]
                        if phase == 0:
                            v.wait_ge(f_read, 8 * gg + H + 1)
                            if H == 0:
                                v.wait_ge(tap_in, 1 + gg)
                            if u % 2:
                                if not (isinstance(gg, int) and gg == 0 and u == 1):
                                    v.wait_ge(f_lo, 4 * gg + 2 * (u // 2) + half - 1)
                            v.tensor_scalar(buf, x_j, w[:, 2:3], None, ALU.mult).then_inc(f_conv, 1)
                        else:
                            v.wait_ge(f_conv, 24 * gg + 3 * H + phase)
                            v.scalar_tensor_tensor(out=buf, in0=x_j, scalar=w[:, 2 - phase:3 - phase], in1=buf,
                                                   op0=ALU.mult, op1=ALU.add).then_inc(f_conv, 1)
                    elif u % 2:
                        v.wait_ge(f_silu, 4 * gg + 2 * (u // 2) + half + 1)
                        v.wait_ge(f_conv, 24 * gg + 3 * H + 3)
                        v.tensor_tensor(buf, gb[:, hcols(half)], buf, ALU.mult).then_inc(f_prod, 1)
                if only_events:
                    return
                if t == 3:
                    v.tensor_copy(tapc[:, :, :, :], taps[:, :, bass.ds(2 * g, 2), :]).then_inc(tap_in, 1)

            def pool_ffn(pool, g, t, only_events=False):
                H, phase, back = events(t)
                u, half = H // 2, H % 2
                gg = g - back
                if not (isinstance(gg, int) and gg < 0) and phase == 3 and u % 2:
                    pool.wait_ge(f_hi, 4 * gg + 2 * (u // 2) + half + 1)
                    pool.tensor_tensor(a_lo[:, u // 2, hcols(half)], ub[:, hcols(half)],
                                       a_hi[:, u // 2, hcols(half)].bitcast(F32), ALU.subtract).then_inc(f_lo, 1)
                if only_events:
                    return
                if t % 8 == 1:
                    u = t // 8 + 1
                    if not (isinstance(g, int) and g == GROUPS - 1 and u == 4):
                        split_lo(pool, F0 + 4 * g + u, u % 2)
                if t == 20:
                    pool.wait_ge(wd_his, g + 1)
                    if not (isinstance(g, int) and g == 0):
                        pool.wait_ge(down, 16 * g)
                    pool.tensor_tensor(wd_lo[:, :, :], wd_raw[:, :, :], wd_hi[:, :, :].bitcast(F32),
                                       ALU.subtract).then_inc(wd_los, 1)

            def pe_ffn(pe, g, t):
                if t >= 1 and t <= 16 and not (isinstance(g, int) and g == 0):
                    down_output(pe, g - 1, t - 1)
                u, half, part = t // 8, t % 8 // 4, t % 4
                U = F0 + 4 * g + u
                if part == 0:
                    if half == 0:
                        pe.wait_ge(hi_split, U + 1)
                        pe.wait_ge(lo_split, U + 1)
                    if not (isinstance(g, int) and g == 0 and u == 0):
                        pe.wait_ge(f_read, 8 * g + 2 * u + half - 1)
                mm = unit_products(pe, u % 2, half, (2 * part, 2 * part + 1), n2_hi, n2_lo)
                if part == 3:
                    mm.then_inc(gemm_halves, 1)

            with nc.Block() as block:
                @block.sync
                def _(sp):
                    sp.dma_start(taps[:, :, :, :], ffn_conv.rearrange("p (s b) j -> p s b j", s=2)).then_inc(small_in, 16)
                    sp.dma_start(wf[:, :], norm_f.to_broadcast([P, D])).then_inc(small_in, 16)

                    def group(g, units):
                        for u in units:
                            src = w_up[bass.ds(2 * g + (u % 2 * FB + u // 2), 1)].rearrange("o p k n -> (o p) k n")
                            load_unit(sp, F0 + 4 * g + u, u % 2, src)
                        if not (isinstance(g, int) and g == 0):
                            sp.wait_ge(wd_los, g)
                        sp.dma_start(wd_raw[:, :, :], w_down[bass.ds(g, 1)].rearrange("o p k n -> (o p) k n")).then_inc(wd_landed, 16)

                    group(0, (2, 3))
                    with sp.Fori(1, GROUPS) as g:
                        group(g, range(4))

                @block.tensor
                def _(pe):
                    for g in (0, 1):
                        for t in range(FSLOTS):
                            pe_ffn(pe, g, t)
                    with pe.Fori(2, GROUPS) as g:
                        for t in range(FSLOTS):
                            pe_ffn(pe, g, t)
                    for n in range(2 * TB):
                        down_output(pe, GROUPS - 1, n)

                @block.scalar
                def _(act):
                    split_hi(act, F0, 0, 16 * (F0 // 2 + 1))
                    for t in range(FSLOTS):
                        act_ffn(act, 0, t)
                    with act.Fori(1, GROUPS - 1) as g:
                        for t in range(FSLOTS):
                            act_ffn(act, g, t)
                    for t in range(FSLOTS):
                        act_ffn(act, GROUPS - 1, t)
                    for t in range(4):
                        act_ffn(act, GROUPS, t, only_events=True)
                    for i in range(TB):
                        act.wait_ge(down_added, 16 * (GROUPS - 1) + 2 * i + 2)
                        if i >= 2:
                            act.wait_ge(e_out, i - 1)
                        act.activation(sqf[i % 2][:, :], x1[:, i, :], ACT.Square, accum_out=stdf[:, i:i + 1]).then_inc(e_ss, 1)
                        act.wait_ge(e_ss, i + 1)
                        act.activation(stdf[:, i:i + 1], stdf[:, i:i + 1], ACT.Sqrt, bias=eps[:, :], scale=1.0 / D).then_inc(e_std, 1)

                @block.gpsimd
                def _(pool):
                    split_lo(pool, F0, 0)
                    for t in range(FSLOTS):
                        pool_ffn(pool, 0, t)
                    with pool.Fori(1, GROUPS - 1) as g:
                        for t in range(FSLOTS):
                            pool_ffn(pool, g, t)
                    for t in range(FSLOTS):
                        pool_ffn(pool, GROUPS - 1, t)
                    for t in range(4):
                        pool_ffn(pool, GROUPS, t, only_events=True)

                @block.vector
                def _(v):
                    v.memset(fpre[:, 0:2], 0.0).then_inc(f_pad, 1)
                    v.wait_ge(small_in, 32)
                    for t in range(FSLOTS):
                        vec_ffn(v, 0, t)
                    with v.Fori(1, GROUPS) as g:
                        for t in range(FSLOTS):
                            vec_ffn(v, g, t)
                    def final(i):
                        v.wait_ge(e_std, i + 1)
                        v.reciprocal(stdf[:, i:i + 1], stdf[:, i:i + 1]).then_inc(e_rec, 1)
                        v.wait_ge(e_rec, i + 1)
                        v.scalar_tensor_tensor(out=x1[:, i, :], in0=x1[:, i, :], scalar=stdf[:, i:i + 1], in1=wf[:, :],
                                               op0=ALU.mult, op1=ALU.mult).then_inc(e_out, 1)
                    for t in range(4):
                        vec_ffn(v, GROUPS, t, only_events=True)
                    for n in range(3, 2 * TB):
                        down_add(v, GROUPS - 1, n)
                        if n % 2 and n >= 5:
                            final(n // 2 - 2)
                    final(TB - 2)
                    final(TB - 1)

            with nc.Block() as block:
                @block.sync
                def _(sp):
                    for i in range(TB):
                        sp.wait_ge(e_out, i + 1)
                        sp.dma_start(out[0, i * P:(i + 1) * P, :], x1[:, i, :]).then_inc(stored, 16)
                    sp.wait_ge(stored, 16 * TB)

def kernel(**inputs):
    import concourse.bacc as bacc
    from concourse.bass_utils import run_bass_kernel_spmd

    nc = bacc.Bacc("TRN2", target_bir_lowering=False, num_devices=1)
    arrays, args = {}, []
    for name, a in layout(inputs).items():
        arrays[name] = a
        args.append(nc.dram_tensor(name, a.shape, mybir.dt.from_np(a.dtype), kind="ExternalInput").ap())
    shape = inputs["x"].shape
    out = nc.dram_tensor("out", shape, F32, kind="ExternalOutput").ap()
    build(nc, *args, out)
    results = run_bass_kernel_spmd(nc, [arrays], core_ids=[0])
    return results.results[0]["out"]


def layout(inputs):
    def units(w):
        k, n = w.shape
        return np.ascontiguousarray(w.reshape(k // P, P, n // P, P).transpose(2, 1, 0, 3))

    def columns(v):
        return np.ascontiguousarray(v.reshape(-1, P).T)

    a = {k: np.asarray(v) for k, v in inputs.items()}
    w = a["w_in"][0]
    qkv = 3 * HEADS * P
    taps = a["dn_conv_w"][0]
    up_taps = a["ffn_conv_w"][0]
    return {
        "x_in": a["x"],
        "norm1": columns(a["norm1_w"][0]),
        "w_main": units(np.concatenate([w[:, :qkv], w[:, qkv + 2 * HEADS:]], axis=1)),
        "w_ab": np.ascontiguousarray(w[:, qkv:qkv + 2 * HEADS].reshape(-1, P, 2 * HEADS).transpose(1, 0, 2)),
        "conv": np.ascontiguousarray(taps.reshape(taps.shape[0], 3, HEADS, P).transpose(3, 2, 1, 0)),
        "a_log": a["dn_A_log"],
        "dt_bias": a["dn_dt_bias"],
        "dn_norm": columns(a["dn_norm_w"][0]),
        "proj_dn": units(a["w_proj_dn"][0]),
        "proj_sb": units(a["w_proj_sb"][0]),
        "w_out_u": np.ascontiguousarray(a["w_out"][0].reshape(-1, P, 2, HALF).transpose(2, 1, 0, 3)),
        "norm2": columns(a["norm2_w"][0]),
        "w_up": units(a["ffn_w_up"][0]),
        "ffn_conv": np.ascontiguousarray(up_taps.reshape(up_taps.shape[0], -1, P).transpose(2, 1, 0)),
        "w_down": np.ascontiguousarray(a["ffn_w_down"][0].reshape(-1, 2, P, a["x"].shape[-1]).transpose(0, 2, 1, 3)),
        "norm_f": a["norm_f_w"].reshape(1, -1),
    }
```

```python
from contextlib import ExitStack

import numpy as np

import concourse.bass as bass
from concourse import mybir

P = 128
F32 = mybir.dt.float32
F32R = mybir.dt.float32r
BF16 = mybir.dt.bfloat16
ALU = mybir.AluOpType
ACT = mybir.ActivationFunctionType

EPS = 1e-6
BIG = 1e30
HEADS = 8
HALF = 512
SLOTS = 64
LEVELS = 7
UNITS = 8


def numbered(names):
    return {name: i + 1 for i, name in enumerate(names)}


def delta_steps():
    two = (0, 1)
    pe = [f"{s}{i}" for s in ("k", "q", "gk", "gq", "v", "kk", "qk", "y") for i in two]
    act = ["sqk", "lnk", "sqq", "lnq", "rk", "ck", "kd0", "kd1", "eg", "eD", "eT", "vb0", "vb1", "cg", "y0", "y1"]
    dve = ["tab", "cw", "gk", "gc", "D0", "D1", "gq", "nb", "T0", "T1", "L0", "L1", "at0", "at1", "cq", "x"]
    pool = [f"C{level}" for level in range(LEVELS)]
    for level in range(1, LEVELS):
        pe += [f"P{level}"] + [f"X{level}{i}" for i in two if level > 1] + [f"Y{level}"]
        act += [f"P{level}"]
        dve += [f"X{level}{i}" for i in two if level > 1] + [f"Y{level}"]
    for n in range(8):
        pe += [f"ks{n}", f"vn{n}", f"ds{n}"]
        dve += ["s_init"] * (n == 0) + [f"r{n}", f"s{n}"]
        act += [f"vn{n}"] + ([f"o{n // 4}"] if n % 4 == 3 else []) + ["sqo0"] * (n == 4)
    pe += ["to0", "to1"]
    act += ["sqo1", "lno", "ero"]
    dve += ["no", "fo0", "fo1"]
    return numbered(pe), numbered(act), numbered(dve), numbered(pool)


D_PE, D_ACT, D_DVE, D_POOL = delta_steps()


TAB_DVE = numbered(["ab0", "ab1", "y", "neg", "negabs", "softplus", "step", "G", "left", "nbeg"])
TAB_ACT = numbered(["exp", "ea", "ln", "eg", "egl", "eglast", "beta"])


def attn_steps():
    pe, act, dve = ["v0", "v1"], ["v0", "v1"], []
    for i in range(8):
        rounds = 1 + (i >= 4)
        pe += [f"z{i}"] + [f"t{i}{r}" for r in range(rounds)] + [f"o{i}"]
        act += [f"keep{i}", f"beta{i}"] + ([f"o{i // 4}"] if i % 4 == 3 else [])
        dve += [f"scan{i}", f"a{i}"] + [f"t{i}{r}" for r in range(rounds)]
    return numbered(pe), numbered(act), numbered(dve)


A_PE, A_ACT, A_DVE = attn_steps()

GATE_A, SB_V, DN_V, DN_Q, DN_K, DN_G, SB_Q, SB_K = range(UNITS)
CONVOLVED = (DN_V, DN_Q, DN_K)
SILU = (DN_V, DN_Q, DN_K, DN_G)


LEVEL_SLOT = 14
CHUNK_SLOT = 27
NORM_SLOT = 54


def z_slot(i):
    return 10 + 5 * i


def build(nc, x, norm1, w_main, w_ab, conv, a_log, dt_bias, dn_norm, w_proj_dn, w_proj_sb,
          w_out, norm2, w_up, ffn_conv, w_down, norm_f, out):
    T, D = x.shape[1], x.shape[2]
    KB = D // P
    TB = T // P
    BLOCK = {kind: HEADS * i for i, kind in enumerate((DN_Q, DN_K, DN_V, DN_G, SB_Q, SB_K, SB_V, GATE_A))}
    GATE_B_BLOCK = BLOCK[GATE_A] + KB
    SCALE = float(P) ** -0.5

    gates_d = nc.dram_tensor("gates_d", (2 * KB, P, T), F32).ap()
    o_d = nc.dram_tensor("o_d", (2, HEADS, P, T), F32).ap()

    whole = ExitStack()
    with whole:
        def sem(name, ctx=whole):
            return ctx.enter_context(nc.semaphore(name))

        def sb(name, shape, dt=F32, ctx=whole):
            return ctx.enter_context(nc.sbuf_tensor(name, shape, dt))

        identf = sb("identf", [P, P])
        identb = sb("identb", [P, P], BF16)
        ones = sb("ones", [P, P])
        eps = sb("eps", [P, 1])
        eps_q = sb("eps_q", [P, 1])
        w_raw = [sb(f"w_raw{i}", [P, KB, P]) for i in (0, 1)]
        w_hi = [sb(f"w_hi{i}", [P, KB, P], F32R) for i in (0, 1)]
        w_lo = [sb(f"w_lo{i}", [P, KB, P], F32R) for i in (0, 1)]
        psum = whole.enter_context(nc.psum_tensor("psum", [P, 8, HALF], F32))
        gemm_bank = [psum[:, 0, :], psum[:, 1, :]]

        raw_landed = [sem(f"raw_landed{i}") for i in (0, 1)]
        hi_split = sem("hi_split")
        lo_split = sem("lo_split")
        gemm_halves = sem("gemm_halves")
        gemm_read = sem("gemm_read")

        def load_unit(eng, U, parity, src, raw_wait=True):
            if raw_wait:
                eng.wait_ge(hi_split, U - 1)
                eng.wait_ge(lo_split, U - 1)
            eng.dma_start(w_raw[parity][:, :, :], src).then_inc(raw_landed[parity], 16)

        def split_hi(act, U, parity, landed, free=True):
            act.wait_ge(raw_landed[parity], landed)
            if free:
                act.wait_ge(gemm_halves, 2 * U - 2)
            act.activation(w_hi[parity][:, :, :], w_raw[parity][:, :, :], ACT.Copy).then_inc(hi_split, 1)

        def split_lo(pool, U, parity, free=True):
            pool.wait_ge(hi_split, U + 1)
            if free:
                pool.wait_ge(gemm_halves, 2 * U - 2)
            pool.tensor_tensor(w_lo[parity][:, :, :], w_raw[parity][:, :, :],
                               w_hi[parity][:, :, :].bitcast(F32), ALU.subtract).then_inc(lo_split, 1)

        def unit_products(pe, parity, half, ks, hi, lo, bank=None):
            bank = gemm_bank[half] if bank is None else bank
            cols = slice(half * HALF, (half + 1) * HALF)
            for k in ks:
                for j, (w, a) in enumerate(((w_hi, hi), (w_hi, lo), (w_lo, hi))):
                    mm = pe.matmul(bank, w[parity][:, k, :], a[:, k, cols],
                                   start=(k == 0 and j == 0), stop=(k == KB - 1 and j == 2))
            return mm

        nq, nk, nv = (sb(n, [P, T]) for n in ("nq", "nk", "nv"))
        sig = sb("sig", [P, T])
        M0 = UNITS * (HEADS + 1)
        gate_stored = [sem(f"gate_stored{i}") for i in (0, 1)]
        early_landed = [sem(f"early_landed{i}") for i in range(3)]

        head_ctx = ExitStack()
        with head_ctx:
            def hsb(name, shape, dt=F32):
                return sb(name, shape, dt, head_ctx)

            n1_hi = hsb("n1_hi", [P, KB, T], F32R)
            n1_lo = hsb("n1_lo", [P, KB, T], F32R)
            ng, nsq, nsk, nsv = hsb("ng", [P, T]), hsb("nsq", [P, T]), hsb("nsk", [P, T]), hsb("nsv", [P, T])
            cq, ck, cg = hsb("cq", [P, T]), hsb("ck", [P, T]), hsb("cg", [P, T])
            sums = hsb("sums", [P, 3, TB])
            logs = hsb("logs", [P, 3, TB])
            rows = hsb("rows", [P, 3, TB])
            inv = hsb("inv", [P, 2, TB])
            dec, decT = hsb("dec", [P, T]), hsb("decT", [P, T])
            X, Y, R = hsb("X", [P, T]), hsb("Y", [P, T]), hsb("R", [P, T])
            Cs = [hsb("C0", [P, T]), hsb("C1", [P, T])]
            vb, kd = hsb("vb", [P, T]), hsb("kd", [P, T])
            ob = hsb("ob", [P, T])
            S = hsb("S", [P, P])
            rr, vnew = hsb("rr", [P, P]), hsb("vnew", [P, P])
            keep, beta, aT = hsb("keep", [P, T]), hsb("beta", [P, T]), hsb("aT", [P, TB, P])
            sv = hsb("sv", [P, TB, P])
            ao = hsb("ao", [P, HALF])
            pre = hsb("pre", [P, 3 + T])
            G, BETA, NBEG, EGL, EGLAST = range(5)
            tab = hsb("tab", [P, HEADS, 5, TB])
            cur = hsb("cur", [P, 5, TB])
            cwt = hsb("cwt", [P, HEADS, 3, 4])
            cwc = hsb("cwc", [P, 3, 4])
            dnw = hsb("dnw", [P, 1])
            tri = hsb("tri", [P, P])
            pos_mask, neg_mask = hsb("pos_mask", [P, P]), hsb("neg_mask", [P, P])
            z_mask = hsb("z_mask", [P, P], BF16)
            level_mask = hsb("level_mask", [P, LEVELS, P], BF16)

            dbank = [psum[:, 6, :], psum[:, 7, :]]
            z_bank = psum[:, 2:4, :].rearrange("p b n -> p (b n)")
            z_pair = [psum[:, 2, :], psum[:, 3, :]]
            t_bank, ao_bank = psum[:, 4, :], psum[:, 5, :]
            side_bank = [t_bank, ao_bank]

            def conv_tap(v, y, w, half, j, counter, before):
                x_j = pre[:, 3 - j + half * HALF:3 - j + (half + 1) * HALF]
                if j == 0:
                    v.tensor_scalar(y, x_j, w[:, 3:4], None, ALU.mult).then_inc(counter, 1)
                else:
                    v.wait_ge(counter, before)
                    v.scalar_tensor_tensor(out=y, in0=x_j, scalar=w[:, 3 - j:4 - j], in1=y,
                                           op0=ALU.mult, op1=ALU.add).then_inc(counter, 1)

            first = ExitStack()
            with first:
                xs = [X, Y, Cs[0], R, dec, decT, vb, kd]
                wab_hi = sb("wab_hi", [P, KB, 2 * HEADS], F32R, first)
                wab_lo = sb("wab_lo", [P, KB, 2 * HEADS], F32R, first)
                abT = beta[0:2 * HEADS, :]
                wab = nsq[:, 0:KB * 2 * HEADS].rearrange("p (k n) -> p k n", k=KB)
                dt_b = nsq[:, 512:520]
                al_b = nsq[:, 520:528]
                y_ab = nsk[:, 0:64].rearrange("p (h n) -> p h n", h=HEADS)
                t1 = nsk[:, 64:128].rearrange("p (h n) -> p h n", h=HEADS)
                t2 = nsk[:, 128:192].rearrange("p (h n) -> p h n", h=HEADS)
                t3 = nsk[:, 192:256].rearrange("p (h n) -> p h n", h=HEADS)
                gstep = nsk[:, 256:320]
                ea = nsk[:, 320:328]
                n1w = nsk[:, 336:344]
                ss = nsk[:, 344:352]
                rstd = nsk[:, 352:360]
                std = nsk[:, 360:368]
                junk = keep
                LATE_ROWS = TB - 3

                c_small = sem("c_small", first)
                x_landed = [sem(f"x_landed{i}", first) for i in range(TB)]
                masks = sem("masks", first)
                x_ss = sem("x_ss", first)
                x_std = sem("x_std", first)
                x_rstd = sem("x_rstd", first)
                x_norm = sem("x_norm", first)
                x_turned = sem("x_turned", first)
                n_hi = sem("n_hi", first)
                n_lo = sem("n_lo", first)
                ab_hi = sem("ab_hi", first)
                ab_lo = sem("ab_lo", first)
                ab_sum = sem("ab_sum", first)
                tab_act = sem("tab_act", first)
                tab_dve = sem("tab_dve", first)
                pad = sem("pad", first)
                gate_out = sem("gate_out0", first)
                conv0 = sem("conv0", first)
                sig0 = sem("sig0", first)
                silu0 = sem("silu0", first)

                with nc.Block() as block:
                    @block.sync
                    def _(sp):
                        def load_x(i):
                            sp.dma_start(xs[i][:, :], x[0, i * P:(i + 1) * P, :]).then_inc(x_landed[i], 16)

                        for i in range(4):
                            load_x(i)
                        sp.dma_start(n1w, norm1).then_inc(c_small, 16)
                        sp.dma_start(wab, w_ab).then_inc(c_small, 16)
                        sp.dma_start(dt_b, dt_bias[0:1, :].to_broadcast([P, HEADS])).then_inc(c_small, 16)
                        sp.dma_start(al_b, a_log[0:1, :].to_broadcast([P, HEADS])).then_inc(c_small, 16)
                        sp.dma_start(dnw[:, :], dn_norm).then_inc(c_small, 16)
                        sp.dma_start(cwt[:, :, :, :], conv).then_inc(c_small, 16)
                        load_unit(sp, 0, 0, w_main[BLOCK[0]], raw_wait=False)
                        for i in range(4, TB):
                            load_x(i)
                        load_unit(sp, 1, 1, w_main[BLOCK[1]], raw_wait=False)
                        for U in range(2, UNITS):
                            load_unit(sp, U, U % 2, w_main[BLOCK[U]])
                            if U == 3:
                                for half in (0, 1):
                                    sp.wait_ge(gemm_read, half + 1)
                                    sp.dma_start(gates_d[0][:, half * HALF:(half + 1) * HALF],
                                                 sig[:, half * HALF:(half + 1) * HALF]).then_inc(gate_out, 16)
                        load_unit(sp, UNITS, 0, w_main[BLOCK[0] + 1])
                        sp.wait_ge(gate_out, 32)

                    @block.gpsimd
                    def _(pool):
                        count = [0]

                        def done(ins):
                            count[0] += 1
                            ins.then_inc(masks, 1)
                            pool.wait_ge(masks, count[0])

                        g = nc.gpsimd
                        done(g.memset(identf[:, :], 0.0))
                        done(g.affine_select(out=identf[:, :], in_=identf[:, :], compare_op=ALU.not_equal,
                                             fill=1.0, base=0, pattern=[[-1, P]], channel_multiplier=1))
                        done(g.memset(ones[:, :], 1.0))
                        done(g.memset(eps[:, :], EPS))
                        done(g.memset(eps_q[:, :], EPS * P))
                        done(g.affine_select(out=tri[:, :], in_=ones[:, :], compare_op=ALU.is_ge,
                                             fill=0.0, base=0, pattern=[[1, P]], channel_multiplier=-1))
                        done(g.memset(pos_mask[:, :], 0.0))
                        done(g.affine_select(out=pos_mask[:, :], in_=pos_mask[:, :], compare_op=ALU.is_gt,
                                             fill=BIG, base=0, pattern=[[-1, P]], channel_multiplier=1))
                        done(g.memset(neg_mask[:, :], 0.0))
                        done(g.affine_select(out=neg_mask[:, :], in_=neg_mask[:, :], compare_op=ALU.is_ge,
                                             fill=-BIG, base=0, pattern=[[1, P]], channel_multiplier=-1))
                        done(g.tensor_copy(identb[:, :], identf[:, :]))
                        done(g.memset(z_mask[:, :], 0.0))
                        done(g.affine_select(out=z_mask[:, :], in_=z_mask[:, :], compare_op=ALU.is_gt,
                                             fill=-BIG, base=0, pattern=[[-1, P]], channel_multiplier=1))
                        split_lo(pool, 0, 0, free=False)
                        for level in range(LEVELS):
                            s = 1 << level
                            m = level_mask[:, level, :].rearrange("p (b r) -> p b r", r=2 * s)
                            nb = P // (2 * s)
                            one = ones[:, :].rearrange("p (b r) -> p b r", r=2 * s)
                            done(g.affine_select(out=m, in_=one, compare_op=ALU.is_ge, fill=0.0, base=s - 1,
                                                 pattern=[[0, nb], [-1, 2 * s]], channel_multiplier=0))
                            done(g.affine_select(out=m, in_=m, compare_op=ALU.is_ge, fill=0.0, base=-s,
                                                 pattern=[[-2 * s, nb], [0, 2 * s]], channel_multiplier=1))
                            done(g.affine_select(out=m, in_=m, compare_op=ALU.is_ge, fill=0.0, base=2 * s - 1,
                                                 pattern=[[2 * s, nb], [0, 2 * s]], channel_multiplier=-1))
                        for U in range(UNITS + 1):
                            if U:
                                split_lo(pool, U, U % 2, free=U >= 2)
                            for half in (0, 1):
                                n = 2 * (U - 2) + half
                                if U - 2 in SILU:
                                    y = {DN_V: nv, DN_Q: nq, DN_K: nk, DN_G: ng}[U - 2][:, half * HALF:(half + 1) * HALF]
                                    pool.wait_ge(sig0, 2 * (U - 2 - DN_V) + half + 1)
                                    pool.tensor_tensor(y, y, sig[:, half * HALF:(half + 1) * HALF],
                                                       ALU.mult).then_inc(silu0, 1)

                    @block.tensor
                    def _(pe):
                        def turn_rows(i2, k):
                            n = KB * i2 + k
                            if k == 0:
                                pe.wait_ge(x_norm, 4 * i2 + 4)
                            if n >= 4:
                                pe.wait_ge(n_lo, n - 3)
                            for i in range(4):
                                tr = pe.transpose(psum[:, 2 + k % 4, i * P:(i + 1) * P],
                                                  xs[4 * i2 + i][:, k * P:(k + 1) * P], identf[:, :])
                            tr.then_inc(x_turned, 1)

                        def logits(half, k):
                            if k == 0:
                                pe.wait_ge(ab_lo, 1)
                            for j, (w, a) in enumerate(((wab_hi, n1_hi), (wab_hi, n1_lo), (wab_lo, n1_hi))):
                                mm = pe.matmul(psum[0:2 * HEADS, 6 + half, :], w[:, k, :],
                                               a[:, k, half * HALF:(half + 1) * HALF],
                                               start=(k == 0 and j == 0), stop=(k == KB - 1 and j == 2))
                            if k == KB - 1:
                                mm.then_inc(ab_sum, 1)

                        def unit_half(U, half, k):
                            if k == 0 and half == 0:
                                pe.wait_ge(hi_split, U + 1)
                                pe.wait_ge(lo_split, U + 1)
                            if k == 0 and U:
                                pe.wait_ge(gemm_read, 2 * U + half - 1)
                            mm = unit_products(pe, U % 2, half, (k,), n1_hi, n1_lo)
                            if k == KB - 1:
                                mm.then_inc(gemm_halves, 1)

                        pe.wait_ge(masks, 2)
                        for k in range(KB + 2):
                            if k < KB:
                                turn_rows(0, k)
                            if k >= 2:
                                pe.wait_ge(n_lo, k - 1)
                                unit_half(0, 0, k - 2)
                        for k in range(KB):
                            turn_rows(1, k)
                            logits(0, k)
                        for k in range(KB):
                            pe.wait_ge(n_lo, KB + k + 1)
                            unit_half(0, 1, k)
                        for k in range(KB):
                            logits(1, k)
                        for U in range(1, UNITS):
                            for half in (0, 1):
                                for k in range(KB):
                                    unit_half(U, half, k)
                            if U == 1:
                                pe.wait_ge(tab_dve, TAB_DVE["ab1"])
                                for i in range(TB):
                                    tr = pe.transpose(psum[:, 5, 16 * i:16 * i + 16], abT[:, i * P:(i + 1) * P],
                                                      identf[0:2 * HEADS, 0:2 * HEADS])
                                tr.then_inc(ab_sum, 1)
                            if U == 2:
                                pe.wait_ge(tab_dve, TAB_DVE["step"])
                                pe.wait_ge(masks, 6)
                                pe.matmul(psum[:, 4, 0:64], tri[:, :], gstep, start=True, stop=True)
                                pe.matmul(psum[:, 4, 64:128], ones[:, :], gstep, start=True, stop=True).then_inc(ab_sum, 1)

                    @block.scalar
                    def _(act):
                        def row_norm(i):
                            act.wait_ge(x_landed[i], 16)
                            if i:
                                act.wait_ge(x_ss, i)
                            act.activation(junk[:, :], xs[i][:, :], ACT.Square,
                                           accum_out=ss[:, i:i + 1]).then_inc(x_ss, 1)
                            if i == 0:
                                act.wait_ge(masks, 4)
                            act.wait_ge(x_ss, i + 1)
                            act.activation(std[:, i:i + 1], ss[:, i:i + 1], ACT.Sqrt, bias=eps[:, :],
                                           scale=1.0 / D).then_inc(x_std, 1)

                        def high_part(n):
                            k, half = n % KB, n // KB
                            act.wait_ge(x_turned, n + 1)
                            act.activation(n1_hi[:, k, half * HALF:(half + 1) * HALF], psum[:, 2 + k % 4, :],
                                           ACT.Copy, scale=n1w[:, k:k + 1]).then_inc(n_hi, 1)

                        for i in range(TB // 2):
                            row_norm(i)
                        act.wait_ge(c_small, 16 * 6)
                        act.activation(wab_hi[:, :, :], wab, ACT.Copy).then_inc(ab_hi, 1)
                        split_hi(act, 0, 0, 16, free=False)
                        for n in range(2 * KB):
                            if n == KB:
                                row_norm(TB - 1)
                            high_part(n)
                            if LATE_ROWS <= n < KB:
                                row_norm(n - 1)
                        split_hi(act, 1, 1, 16, free=False)

                        def softplus():
                            act.wait_ge(tab_dve, TAB_DVE["negabs"])
                            act.activation(t2, t1, ACT.Exp).then_inc(tab_act, 1)
                            act.activation(ea, al_b, ACT.Exp).then_inc(tab_act, 1)
                            act.wait_ge(tab_act, TAB_ACT["exp"])
                            act.wait_ge(masks, 3)
                            act.activation(t3, t2, ACT.Ln, bias=ones[:, 0:1]).then_inc(tab_act, 1)

                        def decays():
                            act.wait_ge(tab_dve, TAB_DVE["left"])
                            act.activation(t2, tab[:, :, G, :], ACT.Exp).then_inc(tab_act, 1)
                            act.activation(tab[:, :, EGL, :], t1, ACT.Exp).then_inc(tab_act, 1)
                            act.activation(tab[:, :, EGLAST, :],
                                           psum[:, 4, 64:128].rearrange("p (h n) -> p h n", h=HEADS),
                                           ACT.Exp).then_inc(tab_act, 1)
                            act.activation(tab[:, :, BETA, :],
                                           psum[:, 5, 0:128].rearrange("p (n c) -> p c n", n=TB)[:, HEADS:, :],
                                           ACT.Sigmoid).then_inc(tab_act, 1)

                        for U in range(UNITS):
                            if U >= 1:
                                split_hi(act, U + 1, (U + 1) % 2, 16 * ((U + 1) // 2 + 1))
                            if U == 2:
                                softplus()
                            for half in (0, 1):
                                cols = slice(half * HALF, (half + 1) * HALF)
                                act.wait_ge(gemm_halves, 2 * U + half + 1)
                                if (U, half) == (SB_K, 1):
                                    continue
                                if U == GATE_A:
                                    act.activation(sig[:, cols], gemm_bank[half], ACT.Sigmoid).then_inc(gemm_read, 1)
                                elif U in CONVOLVED:
                                    if U > DN_V:
                                        act.wait_ge(conv0, 8 * (U - DN_V))
                                    else:
                                        act.wait_ge(pad, 1)
                                    act.activation(pre[:, 3 + half * HALF:3 + (half + 1) * HALF], gemm_bank[half],
                                                   ACT.Copy).then_inc(gemm_read, 1)
                                else:
                                    dst = {SB_V: nsv, SB_Q: nsq, SB_K: nsk, DN_G: ng}[U]
                                    if U in (SB_Q, SB_K):
                                        act.wait_ge(tab_act, len(TAB_ACT))
                                        act.wait_ge(tab_dve, len(TAB_DVE))
                                    act.activation(dst[:, cols], gemm_bank[half], ACT.Copy).then_inc(gemm_read, 1)
                            if U in SILU:
                                for half in (0, 1):
                                    cols = slice(half * HALF, (half + 1) * HALF)
                                    y = {DN_V: nv, DN_Q: nq, DN_K: nk, DN_G: ng}[U]
                                    if U == DN_V:
                                        act.wait_ge(gate_out, 32)
                                    else:
                                        act.wait_ge(silu0, 2 * (U - DN_V - 1) + half + 1)
                                    if U in CONVOLVED:
                                        act.wait_ge(conv0, 8 * (U - DN_V) + 4 * half + 4)
                                    else:
                                        act.wait_ge(gemm_read, 2 * U + half + 1)
                                    act.activation(sig[:, cols], y[:, cols], ACT.Sigmoid).then_inc(sig0, 1)
                            if U == 2:
                                decays()

                    @block.vector
                    def _(v):
                        v.memset(pre[:, 0:3], 0.0).then_inc(pad, 1)
                        def scale_rows(i):
                            v.wait_ge(x_std, i + 1)
                            v.reciprocal(rstd[:, i:i + 1], std[:, i:i + 1]).then_inc(x_rstd, 1)
                            v.wait_ge(x_rstd, i + 1)
                            v.tensor_scalar(xs[i][:, :], xs[i][:, :], rstd[:, i:i + 1], None, ALU.mult).then_inc(x_norm, 1)

                        def low_part(n):
                            k, cols = n % KB, slice((n // KB) * HALF, (n // KB + 1) * HALF)
                            v.wait_ge(n_hi, n + 1)
                            v.scalar_tensor_tensor(out=n1_lo[:, k, cols], in0=psum[:, 2 + k % 4, :],
                                                   scalar=n1w[:, k:k + 1], in1=n1_hi[:, k, cols].bitcast(F32),
                                                   op0=ALU.mult, op1=ALU.subtract).then_inc(n_lo, 1)

                        for i in range(TB // 2):
                            scale_rows(i)
                        v.wait_ge(ab_hi, 1)
                        v.tensor_tensor(wab_lo[:, :, :], wab, wab_hi[:, :, :].bitcast(F32), ALU.subtract).then_inc(ab_lo, 1)
                        for n in range(2 * KB):
                            if n == KB:
                                scale_rows(TB - 1)
                            low_part(n)
                            if LATE_ROWS <= n < KB:
                                scale_rows(n - 1)
                        for half in (0, 1):
                            v.wait_ge(ab_sum, half + 1)
                            v.tensor_copy(abT[:, half * HALF:(half + 1) * HALF], psum[0:2 * HEADS, 6 + half, :]).then_inc(tab_dve, 1)
                        ab = psum[:, 5, 0:128].rearrange("p (n c) -> p c n", n=TB)
                        v.wait_ge(ab_sum, 3)
                        v.tensor_tensor(y_ab, ab[:, 0:HEADS, :], dt_b.unsqueeze(2).to_broadcast([P, HEADS, TB]),
                                        ALU.add).then_inc(tab_dve, 1)
                        v.wait_ge(tab_dve, TAB_DVE["y"])
                        v.tensor_scalar(t1, y_ab, -1.0, None, ALU.mult).then_inc(tab_dve, 1)
                        v.wait_ge(tab_dve, TAB_DVE["neg"])
                        v.tensor_tensor(t1, t1, y_ab, ALU.min).then_inc(tab_dve, 1)
                        v.wait_ge(tab_act, TAB_ACT["ln"])
                        v.scalar_tensor_tensor(out=y_ab, in0=y_ab, scalar=0.0, in1=t3, op0=ALU.max,
                                               op1=ALU.add).then_inc(tab_dve, 1)
                        v.wait_ge(tab_dve, TAB_DVE["softplus"])
                        v.scalar_tensor_tensor(out=gstep.rearrange("p (h n) -> p h n", h=HEADS), in0=y_ab, scalar=-1.0,
                                               in1=ea.unsqueeze(2).to_broadcast([P, HEADS, TB]), op0=ALU.mult,
                                               op1=ALU.mult).then_inc(tab_dve, 1)

                        def taps_of(u):
                            for half in (0, 1):
                                v.wait_ge(gemm_read, 2 * u + half + 1)
                                y = {DN_V: nv, DN_Q: nq, DN_K: nk}[u][:, half * HALF:(half + 1) * HALF]
                                w = cwt[:, 0, {DN_Q: 0, DN_K: 1, DN_V: 2}[u], :]
                                for j in range(4):
                                    conv_tap(v, y, w, half, j, conv0, (8 * (u - DN_V) + 4 * half + j) if j else None)

                        taps_of(DN_V)
                        v.wait_ge(ab_sum, 4)
                        v.tensor_copy(tab[:, :, G, :], psum[:, 4, 0:64].rearrange("p (h n) -> p h n", h=HEADS)).then_inc(tab_dve, 1)
                        v.wait_ge(tab_dve, TAB_DVE["G"])
                        v.tensor_tensor(t1, psum[:, 4, 64:128].rearrange("p (h n) -> p h n", h=HEADS),
                                        tab[:, :, G, :], ALU.subtract).then_inc(tab_dve, 1)
                        taps_of(DN_Q)
                        v.wait_ge(tab_act, TAB_ACT["beta"])
                        v.scalar_tensor_tensor(out=tab[:, :, NBEG, :], in0=tab[:, :, BETA, :], scalar=-1.0, in1=t2,
                                               op0=ALU.mult, op1=ALU.mult).then_inc(tab_dve, 1)
                        taps_of(DN_K)

            loop = ExitStack()
            with loop:
                delta_products = sem("delta_products", loop)
                delta_act = sem("delta_act", loop)
                delta_vec = sem("delta_vec", loop)
                delta_pool = sem("delta_pool", loop)
                attn_products = sem("attn_products", loop)
                attn_act = sem("attn_act", loop)
                attn_vec = sem("attn_vec", loop)
                conv_taps = sem("conv_taps", loop)
                sigmoids = sem("sigmoids", loop)
                silus = sem("silus", loop)
                gate_done = sem("gate_done", loop)
                ao_stored = sem("ao_stored", loop)
                ob_stored = sem("ob_stored", loop)

                def d(h, table, step):
                    return h * len(table) + table[step]

                def chunk(n):
                    return slice(n * P, (n + 1) * P)

                def halves(i):
                    return slice(i * HALF, (i + 1) * HALF)

                def blocks(tile, level):
                    return tile[:, :].rearrange("p (b r s) -> p b r s", r=2, s=1 << level)

                def live_rows(level):
                    return slice(0, P // 2) if level == LEVELS - 1 else slice(0, P)

                def packed(bank, level):
                    return bank.rearrange("p (b s) -> p b s", s=1 << level)

                def col(table, n):
                    return cur[:, table, n:n + 1]

                def pe_delta(pe, h, t):
                    def four(i, bank, lhs, rhs):
                        for q in range(4):
                            mm = pe.matmul(bank[:, chunk(q)], lhs[:, chunk(4 * i + q)], rhs[:, chunk(4 * i + q)],
                                           start=True, stop=True)
                        mm.then_inc(delta_products, 1)

                    def turn(i, bank, src):
                        for q in range(4):
                            tr = pe.transpose(bank[:, chunk(q)], src[:, chunk(4 * i + q)], identf[:, :])
                        tr.then_inc(delta_products, 1)

                    def as_rows(i, bank, table):
                        for q in range(4):
                            tr = pe.transpose(bank[:, chunk(q)], table[:, 4 * i + q:4 * i + q + 1].to_broadcast([P, P]),
                                              identf[:, :])
                        tr.then_inc(delta_products, 1)

                    def changed(bank, level, lhs, rhs):
                        for n in range(TB):
                            rows_ = live_rows(level) if n else slice(0, P)
                            k_rows = rows_ if lhs is X else slice(0, P)
                            mm = pe.matmul(dbank[bank][rows_, n * P // 2:(n + 1) * P // 2],
                                           lhs[k_rows, n * P:n * P + rows_.stop],
                                           rhs[k_rows, chunk(n)].rearrange("p (b r s) -> p b r s", r=2, s=1 << level)[:, :, 1, :],
                                           start=True, stop=True)
                        mm.then_inc(delta_products, 1)

                    if t == 1:
                        pe.wait_ge(delta_vec, d(h, D_DVE, "tab"))
                        pe.wait_ge(gemm_read, 2 * (h * UNITS + UNITS))
                        for i in (0, 1):
                            turn(i, side_bank[i], nk)
                    if t == 2:
                        for i in (0, 1):
                            turn(i, dbank[i], nq)
                    if t == 4:
                        pe.wait_ge(delta_vec, d(h, D_DVE, "gk"))
                        for i in (0, 1):
                            as_rows(i, z_pair[i], rows[:, 1, :])
                    if t == 6:
                        pe.wait_ge(delta_vec, d(h, D_DVE, "gq"))
                        for i in (0, 1):
                            as_rows(i, dbank[i], rows[:, 0, :])
                    if t == 7:
                        for i in (0, 1):
                            pe.wait_ge(delta_act, d(h, D_ACT, f"kd{i}"))
                            turn(i, side_bank[i], nv)
                    if t == 8:
                        for i in (0, 1):
                            pe.wait_ge(delta_vec, d(h, D_DVE, f"D{i}"))
                            four(i, z_pair[i], ck, ck)
                    if t == 9:
                        pe.wait_ge(delta_act, d(h, D_ACT, "eg"))
                        for i in (0, 1):
                            pe.wait_ge(delta_vec, d(h, D_DVE, f"T{i}"))
                            four(i, dbank[i], ck, nq)
                    if t == 12:
                        pe.wait_ge(delta_vec, d(h, D_DVE, "x"))
                        for i in (0, 1):
                            turn(i, dbank[i], X)
                    if LEVEL_SLOT <= t < LEVEL_SLOT + 2 * (LEVELS - 1):
                        level, part = 1 + (t - LEVEL_SLOT) // 2, (t - LEVEL_SLOT) % 2
                        if part == 0:
                            if level == 1:
                                pe.wait_ge(delta_act, d(h, D_ACT, "y1"))
                            else:
                                pe.wait_ge(delta_vec, d(h, D_DVE, f"Y{level - 1}"))
                            pe.wait_ge(delta_pool, d(h, D_POOL, f"C{level}"))
                            changed(0, level, Cs[level % 2], Y)
                            if level > 1:
                                for i, bank in ((0, dbank[1]), (1, z_pair[1])):
                                    turn(i, bank, Y)
                        else:
                            pe.wait_ge(delta_act, d(h, D_ACT, f"P{level}"))
                            if level > 1:
                                pe.wait_ge(delta_vec, d(h, D_DVE, f"X{level}1"))
                            changed(1, level, X, R)
                    if CHUNK_SLOT <= t < CHUNK_SLOT + 24:
                        n, part = (t - CHUNK_SLOT) // 3, (t - CHUNK_SLOT) % 3
                        if part == 0:
                            pe.wait_ge(delta_vec, d(h, D_DVE, f"s{n - 1}" if n else "s_init"))
                            pe.matmul(dbank[1][:, chunk(0)], ck[:, chunk(n)], S[:, :], start=True,
                                      stop=True).then_inc(delta_products, 1)
                        if part == 1:
                            pe.wait_ge(delta_vec, d(h, D_DVE, f"r{n}"))
                            pe.matmul(dbank[1][:, chunk(1)], Y[:, chunk(n)], rr[:, :], start=True,
                                      stop=True).then_inc(delta_products, 1)
                        if part == 2:
                            pe.wait_ge(delta_act, d(h, D_ACT, f"vn{n}"))
                            if n == 4:
                                pe.wait_ge(delta_act, d(h, D_ACT, "o0"))
                            bank = dbank[0][:, chunk(n % 4)]
                            pe.matmul(bank, cq[:, chunk(n)], S[:, :], start=True, stop=False)
                            pe.matmul(bank, decT[:, chunk(n)], vnew[:, :], start=False, stop=True)
                            pe.matmul(dbank[1][:, chunk(2)], kd[:, chunk(n)], vnew[:, :], start=True,
                                      stop=True).then_inc(delta_products, 1)
                    if t == NORM_SLOT + 2:
                        pe.wait_ge(delta_vec, d(h, D_DVE, "no"))
                        for i in (0, 1):
                            turn(i, dbank[i], ob)

                def pe_attn(pe, h, t):
                    if t in (9, 10):
                        i = t - 9
                        pe.wait_ge(delta_act, d(h, D_ACT, f"vb{i}"))
                        for q in range(4):
                            tr = pe.transpose(side_bank[i][:, chunk(q)], nsv[:, chunk(4 * i + q)], identf[:, :])
                        tr.then_inc(attn_products, 1)
                    for i in range(TB):
                        w = (i + 1) * P
                        if t == z_slot(i):
                            if i:
                                pe.wait_ge(attn_act, d(h, A_ACT, f"beta{i - 1}"))
                            else:
                                pe.wait_ge(delta_vec, d(h, D_DVE, "L1"))
                            for lo in range(0, w, HALF):
                                hi = min(w, lo + HALF)
                                pe.matmul(z_bank[:, lo:hi], nsq[:, chunk(i)], nsk[:, lo:hi], start=True, stop=True)
                            pe.matmul(z_bank[:, w - P:w], identb[:, :], z_mask[:, :], start=False, stop=True,
                                      skip_group_check=True).then_inc(attn_products, 1)
                        for r in range(1 + (i >= 4)):
                            if t == z_slot(i) + 3 + r:
                                pe.wait_ge(attn_vec, d(h, A_DVE, f"a{i}"))
                                if r:
                                    pe.wait_ge(attn_vec, d(h, A_DVE, f"t{i}0"))
                                for j in range(4 * r, min(4 * r + 4, i + 1)):
                                    tr = pe.transpose(t_bank[:, chunk(j % 4)], beta[:, chunk(j)], identf[:, :])
                                tr.then_inc(attn_products, 1)
                        if t == z_slot(i) + 5:
                            pe.wait_ge(attn_vec, d(h, A_DVE, f"t{i}{int(i >= 4)}"))
                            if i == 4:
                                pe.wait_ge(attn_act, d(h, A_ACT, "o0"))
                            for j in range(i + 1):
                                mm = pe.matmul(ao_bank[:, chunk(i % 4)], sv[:, j, :], aT[:, j, :],
                                               start=(j == 0), stop=(j == i))
                            mm.then_inc(attn_products, 1)

                def pe_gemm(pe, h, t):
                    u, half, part = t // 8, t % 8 // 4, t % 4
                    U = h * UNITS + UNITS + u
                    if part == 0:
                        pe.wait_ge(gemm_read, 2 * U + half - 1)
                        if half == 0:
                            pe.wait_ge(hi_split, U + 1)
                            pe.wait_ge(lo_split, U + 1)
                    mm = unit_products(pe, u % 2, half, (2 * part, 2 * part + 1), n1_hi, n1_lo)
                    if part == 3:
                        mm.then_inc(gemm_halves, 1)

                def act_delta(act, h, t):
                    def out(dst, src, func=ACT.Copy, **kw):
                        return act.activation(dst, src, func, **kw)

                    def squares(src, junk, log, chunks):
                        for n in chunks:
                            last = out(junk[:, chunk(n)], src(n), ACT.Square, accum_out=sums[:, log, n:n + 1])
                        last.then_inc(delta_act, 1)

                    if t == 1:
                        act.wait_ge(delta_products, d(h, D_PE, "k1"))
                        squares(lambda n: side_bank[n // 4][:, chunk(n % 4)], X, 1, range(TB))
                        act.wait_ge(delta_act, d(h, D_ACT, "sqk"))
                        out(logs[:, 1, :], sums[:, 1, :], ACT.Ln, bias=eps[:, :]).then_inc(delta_act, 1)
                    if t == 2:
                        act.wait_ge(delta_products, d(h, D_PE, "q1"))
                        squares(lambda n: dbank[n // 4][:, chunk(n % 4)], Y, 0, range(TB))
                        act.wait_ge(delta_act, d(h, D_ACT, "sqq"))
                        out(logs[:, 0, :], sums[:, 0, :], ACT.Ln, bias=eps_q[:, :], scale=float(P)).then_inc(delta_act, 1)
                        act.wait_ge(delta_act, d(h, D_ACT, "lnk"))
                        out(inv[:, 0, :], logs[:, 1, :], ACT.Exp, scale=-0.5).then_inc(delta_act, 1)
                    if t == 4:
                        out(ck[:, :], nk[:, :]).then_inc(delta_act, 1)
                        act.wait_ge(delta_vec, d(h, D_DVE, "nb"))
                        for i in (0, 1):
                            for q in range(4):
                                n = 4 * i + q
                                last = out(kd[:, chunk(n)], side_bank[i][:, chunk(q)], scale=col(EGL, n))
                            last.then_inc(delta_act, 1)
                    if t == 6:
                        act.wait_ge(delta_products, d(h, D_PE, "gq1"))
                        out(R[:, :], psum[:, 6:8, :].rearrange("p b n -> p (b n)"), ACT.Exp).then_inc(delta_act, 1)
                        act.wait_ge(delta_vec, d(h, D_DVE, "D1"))
                        out(dec[:, :], dec[:, :], ACT.Exp, scale=-1.0).then_inc(delta_act, 1)
                    if t == 7:
                        act.wait_ge(delta_vec, d(h, D_DVE, "T1"))
                        out(decT[:, :], decT[:, :], ACT.Exp).then_inc(delta_act, 1)
                        for i in (0, 1):
                            act.wait_ge(delta_products, d(h, D_PE, f"v{i}"))
                            for q in range(4):
                                n = 4 * i + q
                                last = out(vb[:, chunk(n)], side_bank[i][:, chunk(q)], scale=col(BETA, n))
                            last.then_inc(delta_act, 1)
                    if t == 10:
                        out(cg[:, :], ng[:, :]).then_inc(delta_act, 1)
                    if t == 12:
                        for i in (0, 1):
                            act.wait_ge(delta_products, d(h, D_PE, f"y{i}"))
                            out(Y[:, halves(i)], dbank[i]).then_inc(delta_act, 1)
                    if LEVEL_SLOT <= t < LEVEL_SLOT + 2 * (LEVELS - 1) and (t - LEVEL_SLOT) % 2 == 0:
                        level = 1 + (t - LEVEL_SLOT) // 2
                        act.wait_ge(delta_products, d(h, D_PE, f"P{level}"))
                        if level == 1:
                            act.wait_ge(delta_vec, d(h, D_DVE, "cq"))
                        live = live_rows(level)
                        out(blocks(R, level)[live, :, 1, :], packed(dbank[0], level)[live]).then_inc(delta_act, 1)
                    if CHUNK_SLOT <= t < CHUNK_SLOT + 24:
                        n, part = (t - CHUNK_SLOT) // 3, (t - CHUNK_SLOT) % 3
                        if part == 1:
                            act.wait_ge(delta_products, d(h, D_PE, f"vn{n}"))
                            out(vnew[:, :], dbank[1][:, chunk(1)]).then_inc(delta_act, 1)
                        if part == 2 and n % 4 == 3:
                            act.wait_ge(delta_products, d(h, D_PE, f"ds{n}"))
                            if n == 3:
                                act.wait_ge(ob_stored, h * 32)
                            out(ob[:, halves(n // 4)], dbank[0]).then_inc(delta_act, 1)
                        if part == 2 and n == 4:
                            act.wait_ge(delta_act, d(h, D_ACT, "o0"))
                            squares(lambda n: ob[:, chunk(n)], R, 2, range(4))
                    if t == NORM_SLOT - 2:
                        act.wait_ge(delta_act, d(h, D_ACT, "o1"))
                        squares(lambda n: ob[:, chunk(n)], R, 2, range(4, TB))
                    if t == NORM_SLOT:
                        act.wait_ge(delta_act, d(h, D_ACT, "sqo1"))
                        out(logs[:, 2, :], sums[:, 2, :], ACT.Ln, bias=eps[:, :], scale=1.0 / P).then_inc(delta_act, 1)
                        act.wait_ge(delta_act, d(h, D_ACT, "lno"))
                        out(inv[:, 1, :], logs[:, 2, :], ACT.Exp, scale=-0.5).then_inc(delta_act, 1)
                    if t == 61:
                        for i in (0, 1):
                            act.wait_ge(delta_vec, d(h, D_DVE, f"fo{i}"))
                            act.dma_start(o_d[0][bass.ds(h, 1), :, halves(i)].rearrange("o p n -> (o p) n"),
                                          ob[:, halves(i)]).then_inc(ob_stored, 16)

                def act_attn(act, h, t):
                    if t in (9, 10):
                        i = t - 9
                        act.wait_ge(attn_products, d(h, A_PE, f"v{i}"))
                        act.activation(sv[:, 4 * i:4 * i + 4, :], side_bank[i], ACT.Copy).then_inc(attn_act, 1)
                    for i in range(TB):
                        w = (i + 1) * P
                        if t == z_slot(i):
                            act.wait_ge(attn_products, d(h, A_PE, f"z{i}"))
                            if i:
                                act.wait_ge(attn_products, d(h, A_PE, f"t{i - 1}{int(i > 4)}"))
                            act.activation(keep[:, 0:w], z_bank[:, 0:w], ACT.Sigmoid, scale=-SCALE).then_inc(attn_act, 1)
                            act.activation(beta[:, 0:w], z_bank[:, 0:w], ACT.Sigmoid, scale=SCALE).then_inc(attn_act, 1)
                        if t == z_slot(i) + 5 and i % 4 == 3:
                            act.wait_ge(attn_products, d(h, A_PE, f"o{i}"))
                            act.wait_ge(ao_stored, h * 32 + (i // 4) * 16)
                            act.activation(ao[:, :], ao_bank, ACT.Copy).then_inc(attn_act, 1)
                            act.wait_ge(attn_act, d(h, A_ACT, f"o{i // 4}"))
                            act.dma_start(o_d[1][bass.ds(h, 1), :, halves(i // 4)].rearrange("o p n -> (o p) n"),
                                          ao[:, :]).then_inc(ao_stored, 16)

                def half_before(t, slots):
                    return (t - slots) // 4 // 2, (t - slots) // 4 % 2

                def act_gemm(act, h, t, last):
                    U0 = h * UNITS + UNITS
                    if t % 4 == 0:
                        u, half = half_before(t, 4) if t else (SB_K, 1)
                        act.wait_ge(gemm_halves, 2 * U0 + t // 4)
                        if last and t:
                            gate_b(act, u, half)
                        elif u == GATE_A:
                            gate_a(act, half, h)
                        elif u in CONVOLVED:
                            if half == 0:
                                act.wait_ge(conv_taps, h * 24 + 8 * (u - DN_V))
                            act.activation(pre[:, 3 + half * HALF:3 + (half + 1) * HALF], gemm_bank[half],
                                           ACT.Copy).then_inc(gemm_read, 1)
                        else:
                            dst = {SB_V: nsv, SB_Q: nsq, SB_K: nsk, DN_G: ng}[u]
                            if u == SB_V:
                                act.wait_ge(attn_products, d(h, A_PE, "v1"))
                            if u == DN_G:
                                act.wait_ge(delta_act, d(h, D_ACT, "cg"))
                            if u == SB_Q:
                                act.wait_ge(attn_products, d(h, A_PE, "z7"))
                            act.activation(dst[:, halves(half)], gemm_bank[half], ACT.Copy).then_inc(gemm_read, 1)
                    if t % 8 == 1 and not (last and t // 8 == UNITS - 1):
                        u = t // 8 + 1
                        split_hi(act, U0 + u, u % 2, 16 * (4 * h + 4 + u // 2 + 1))
                    if t % 4 == 2 and t >= 6 and not last:
                        u, half = half_before(t, 8) if t >= 8 else (0, 0)
                        if t >= 8 and u in SILU:
                            n = 2 * (u - DN_V) + half
                            if u in CONVOLVED:
                                act.wait_ge(conv_taps, h * 24 + 4 * n + 4)
                            else:
                                act.wait_ge(gemm_read, 2 * (U0 + u) + half + 1)
                            if n >= 2:
                                act.wait_ge(silus, h * 8 + n - 1)
                            else:
                                act.wait_ge(gate_stored[half], h * 16 + 16)
                            y = {DN_V: nv, DN_Q: nq, DN_K: nk, DN_G: ng}[u]
                            act.activation(sig[:, halves(half)], y[:, halves(half)], ACT.Sigmoid).then_inc(sigmoids, 1)

                def gate_a(act, half, h):
                    if half == 0:
                        act.wait_ge(silus, h * 8)
                    act.activation(sig[:, halves(half)], gemm_bank[half],
                                   ACT.Sigmoid if half else ACT.Copy).then_inc(gemm_read, 1)
                    if half:
                        act.wait_ge(gemm_read, 2 * (h * UNITS + UNITS) + 1)
                        act.activation(sig[:, halves(0)], sig[:, halves(0)], ACT.Sigmoid).then_inc(gate_done, 1)
                        act.wait_ge(gemm_read, 2 * (h * UNITS + UNITS) + 2)
                        act.wait_ge(gate_done, h + 1)
                        for i in (0, 1):
                            act.dma_start(gates_d[bass.ds(h + 1, 1), :, halves(i)].rearrange("o p n -> (o p) n"),
                                          sig[:, halves(i)]).then_inc(gate_stored[i], 16)

                def gate_b(act, u, half):
                    act.wait_ge(gate_stored[half], 16 * (HEADS - 1 + u))
                    act.activation(sig[:, halves(half)], gemm_bank[half], ACT.Sigmoid).then_inc(gemm_read, 1)
                    act.wait_ge(gemm_read, 2 * (HEADS * UNITS + u) + half + 1)
                    act.dma_start(gates_d[KB + u][:, halves(half)], sig[:, halves(half)]).then_inc(gate_stored[half], 16)

                def vec_delta(v, h, t):
                    if t == 0:
                        v.tensor_copy(cur[:, :, :], tab[:, bass.ds(h, 1), :, :].rearrange("p o a n -> p (o a) n")).then_inc(delta_vec, 1)
                        v.tensor_copy(cwc[:, :, :], cwt[:, bass.ds(cw_head(h), 1), :, :].rearrange("p o a n -> p (o a) n")).then_inc(delta_vec, 1)
                    def with_norm(row, log, factor):
                        v.scalar_tensor_tensor(out=rows[:, row, :], in0=logs[:, log, :], scalar=factor,
                                               in1=cur[:, G, :], op0=ALU.mult, op1=ALU.add).then_inc(delta_vec, 1)

                    if t == 2:
                        v.wait_ge(delta_act, d(h, D_ACT, "lnk"))
                        with_norm(1, 1, 0.5)
                        with_norm(2, 1, -0.5)
                    if t == 4:
                        for i in (0, 1):
                            v.wait_ge(delta_products, d(h, D_PE, f"gk{i}"))
                            if i == 0:
                                v.wait_ge(delta_vec, d(h, D_DVE, "gc"))
                            for q in range(4):
                                n = 4 * i + q
                                last = v.scalar_tensor_tensor(out=dec[:, chunk(n)], in0=z_pair[i][:, chunk(q)],
                                                              scalar=rows[:, 2, n:n + 1], in1=pos_mask[:, :],
                                                              op0=ALU.subtract, op1=ALU.max)
                            last.then_inc(delta_vec, 1)
                    if t == 5:
                        v.wait_ge(delta_act, d(h, D_ACT, "lnq"))
                        with_norm(0, 0, -0.5)
                        v.wait_ge(delta_act, d(h, D_ACT, "rk"))
                        v.tensor_tensor(cur[:, NBEG:EGL + 1, :], cur[:, NBEG:EGL + 1, :],
                                        inv[:, 0:1, :].to_broadcast([P, 2, TB]), ALU.mult).then_inc(delta_vec, 1)
                    if t == 6:
                        for i in (0, 1):
                            if i == 0:
                                v.wait_ge(delta_act, d(h, D_ACT, "eg"))
                            for q in range(4):
                                n = 4 * i + q
                                last = v.scalar_tensor_tensor(out=decT[:, chunk(n)], in0=dbank[i][:, chunk(q)],
                                                              scalar=rows[:, 1, n:n + 1], in1=neg_mask[:, :],
                                                              op0=ALU.subtract, op1=ALU.min)
                            last.then_inc(delta_vec, 1)
                    if t == 8:
                        v.wait_ge(delta_act, d(h, D_ACT, "eD"))
                        for i in (0, 1):
                            v.wait_ge(delta_products, d(h, D_PE, f"kk{i}"))
                            for q in range(4):
                                n = 4 * i + q
                                last = v.scalar_tensor_tensor(out=dec[:, chunk(n)], in0=z_pair[i][:, chunk(q)], scalar=col(BETA, n),
                                                              in1=dec[:, chunk(n)], op0=ALU.mult, op1=ALU.mult)
                            last.then_inc(delta_vec, 1)
                    if t == 9:
                        v.wait_ge(delta_act, d(h, D_ACT, "eT"))
                        for i in (0, 1):
                            v.wait_ge(delta_products, d(h, D_PE, f"qk{i}"))
                            v.tensor_tensor(decT[:, halves(i)], dbank[i], decT[:, halves(i)], ALU.mult).then_inc(delta_vec, 1)
                    if t == 10:
                        v.tensor_tensor(cq[:, :], nq[:, :], R[:, :], ALU.mult).then_inc(delta_vec, 1)
                    if t == 11:
                        v.wait_ge(delta_pool, d(h, D_POOL, "C0"))
                        v.tensor_tensor(X[:, :].rearrange("p (n c) -> p n c", n=TB),
                                        identf[:, :].unsqueeze(1).to_broadcast([P, TB, P]),
                                        Cs[0][:, :].rearrange("p (n c) -> p n c", n=TB), ALU.subtract).then_inc(delta_vec, 1)
                    if LEVEL_SLOT < t < LEVEL_SLOT + 2 * (LEVELS - 1) and (t - LEVEL_SLOT) % 2 == 0:
                        level = 1 + (t - LEVEL_SLOT) // 2
                        for i, bank in ((0, dbank[1]), (1, z_pair[1])):
                            v.wait_ge(delta_products, d(h, D_PE, f"X{level}{i}"))
                            v.tensor_copy(X[:, halves(i)], bank).then_inc(delta_vec, 1)
                    if LEVEL_SLOT <= t < LEVEL_SLOT + 2 * (LEVELS - 1) and (t - LEVEL_SLOT) % 2:
                        level = 1 + (t - LEVEL_SLOT) // 2
                        v.wait_ge(delta_products, d(h, D_PE, f"Y{level}"))
                        live = live_rows(level)
                        cols = blocks(Y, level)[live, :, 1, :]
                        v.tensor_tensor(cols, cols, packed(dbank[1], level)[live], ALU.subtract).then_inc(delta_vec, 1)
                    if CHUNK_SLOT <= t < CHUNK_SLOT + 24:
                        n, part = (t - CHUNK_SLOT) // 3, (t - CHUNK_SLOT) % 3
                        if part == 0:
                            if n == 0:
                                v.memset(S[:, :], 0.0).then_inc(delta_vec, 1)
                            v.wait_ge(delta_products, d(h, D_PE, f"ks{n}"))
                            v.scalar_tensor_tensor(out=rr[:, :], in0=dbank[1][:, chunk(0)], scalar=col(NBEG, n),
                                                   in1=vb[:, chunk(n)], op0=ALU.mult, op1=ALU.add).then_inc(delta_vec, 1)
                        if part == 2:
                            v.wait_ge(delta_products, d(h, D_PE, f"ds{n}"))
                            v.scalar_tensor_tensor(out=S[:, :], in0=S[:, :], scalar=col(EGLAST, n),
                                                   in1=dbank[1][:, chunk(2)], op0=ALU.mult, op1=ALU.add).then_inc(delta_vec, 1)
                    if t == NORM_SLOT + 1:
                        v.wait_ge(delta_act, d(h, D_ACT, "ero"))
                        v.tensor_tensor(ob[:, :].rearrange("p (n c) -> p n c", n=TB),
                                        ob[:, :].rearrange("p (n c) -> p n c", n=TB),
                                        inv[:, 1, :].unsqueeze(2).to_broadcast([P, TB, P]), ALU.mult).then_inc(delta_vec, 1)
                    if t in (NORM_SLOT + 3, NORM_SLOT + 4):
                        i = t - NORM_SLOT - 3
                        v.wait_ge(delta_products, d(h, D_PE, f"to{i}"))
                        v.scalar_tensor_tensor(out=ob[:, halves(i)], in0=dbank[i], scalar=dnw[:, :],
                                               in1=cg[:, halves(i)], op0=ALU.mult, op1=ALU.mult).then_inc(delta_vec, 1)

                def vec_attn(v, h, t):
                    for i in range(TB):
                        w = (i + 1) * P
                        if t == z_slot(i) + 1:
                            v.wait_ge(attn_act, d(h, A_ACT, f"keep{i}"))
                            v.tensor_tensor_scan(keep[:, w - 1::-1], keep[:, w - 1::-1], keep[:, w - 1::-1], 1.0,
                                                 ALU.mult, ALU.bypass).then_inc(attn_vec, 1)
                        if t == z_slot(i) + 2:
                            v.wait_ge(attn_act, d(h, A_ACT, f"beta{i}"))
                            v.wait_ge(attn_vec, d(h, A_DVE, f"scan{i}"))
                            v.tensor_tensor(beta[:, 0:w - 1], beta[:, 0:w - 1], keep[:, 1:w], ALU.mult).then_inc(attn_vec, 1)
                        for r in range(1 + (i >= 4)):
                            if t == z_slot(i) + 3 + r:
                                v.wait_ge(attn_products, d(h, A_PE, f"t{i}{r}"))
                                if i and r == 0:
                                    v.wait_ge(attn_products, d(h, A_PE, f"o{i - 1}"))
                                n = min(4, i + 1 - 4 * r)
                                v.tensor_copy(aT[:, 4 * r:4 * r + n, :], t_bank[:, 0:n * P]).then_inc(attn_vec, 1)

                def vec_gemm(v, h, t, last):
                    if last or t < 4:
                        return
                    u, half = half_before(t, 4)
                    if u in CONVOLVED:
                        n = 2 * (u - DN_V) + half
                        j = t % 4
                        if j == 0:
                            v.wait_ge(gemm_read, 2 * (h * UNITS + UNITS + u) + half + 1)
                            if half == 0:
                                used = {DN_V: (delta_products, d(h, D_PE, "v1")),
                                        DN_Q: (delta_products, d(h, D_PE, "qk1")),
                                        DN_K: (delta_act, d(h, D_ACT, "ck"))}[u]
                                v.wait_ge(*used)
                        y = {DN_V: nv, DN_Q: nq, DN_K: nk}[u][:, halves(half)]
                        w = cwc[:, {DN_Q: 0, DN_K: 1, DN_V: 2}[u], :]
                        conv_tap(v, y, w, half, j, conv_taps, h * 24 + 4 * n + j)

                def pool_delta(pool, h, t):
                    g = nc.gpsimd
                    slot = [8, 8, 12] + [LEVEL_SLOT + 2 * n - 5 for n in range(3, LEVELS)]
                    for level in [n for n in range(LEVELS) if slot[n] == t]:
                        if level == 0:
                            pool.wait_ge(delta_vec, d(h, D_DVE, "L1"))
                        elif level == 2:
                            pool.wait_ge(delta_vec, d(h, D_DVE, "x"))
                        elif level > 2:
                            pool.wait_ge(delta_products, d(h, D_PE, f"P{level - 2}"))
                        g.tensor_tensor(Cs[level % 2][:, :].rearrange("p (n c) -> p n c", n=TB),
                                        dec[:, :].rearrange("p (n c) -> p n c", n=TB),
                                        level_mask[:, level, :].unsqueeze(1).to_broadcast([P, TB, P]),
                                        ALU.mult).then_inc(delta_pool, 1)

                def pool_gemm(pool, h, t, last):
                    U0 = h * UNITS + UNITS
                    if t % 8 == 1 and not (last and t // 8 == UNITS - 1):
                        u = t // 8 + 1
                        split_lo(pool, U0 + u, u % 2)
                    if t % 4 == 2 and t >= 8 and not last:
                        u, half = half_before(t, 8)
                        if u in SILU:
                            n = 2 * (u - DN_V) + half
                            y = {DN_V: nv, DN_Q: nq, DN_K: nk, DN_G: ng}[u][:, halves(half)]
                            pool.wait_ge(sigmoids, h * 8 + n + 1)
                            pool.tensor_tensor(y, y, sig[:, halves(half)], ALU.mult).then_inc(silus, 1)

                def cw_head(h):
                    return h + 1 if not isinstance(h, int) or h < HEADS - 1 else HEADS - 1

                with nc.Block() as block:
                    @block.sync
                    def _(sp):
                        with sp.Fori(0, HEADS - 1) as h:
                            for u in range(1, UNITS + 1):
                                load_unit(sp, h * UNITS + UNITS + u, u % 2,
                                          w_main[bass.ds(h + (BLOCK[u % UNITS] + 1 + u // UNITS), 1)].rearrange("o p k n -> (o p) k n"))
                        for u in range(1, KB):
                            load_unit(sp, HEADS * UNITS + u, u % 2,
                                      w_main[GATE_B_BLOCK + u])
                            if u == 4:
                                sp.wait_ge(ob_stored, 32 * (HEADS - 1))
                                for i, (row, used) in enumerate((
                                        (nq, (delta_vec, d(HEADS - 1, D_DVE, "cq"))),
                                        (nk, (delta_act, d(HEADS - 1, D_ACT, "ck"))),
                                        (nv, (delta_products, d(HEADS - 1, D_PE, "v1"))))):
                                    sp.wait_ge(*used)
                                    sp.dma_start(row[:, :], o_d[0][i]).then_inc(early_landed[i], 16)
                        for u in (0, 1):
                            load_unit(sp, M0 + u, u, w_proj_dn[u])

                    @block.tensor
                    def _(pe):
                        def head(h):
                            for t in range(SLOTS):
                                pe_delta(pe, h, t)
                                pe_attn(pe, h, t)
                                pe_gemm(pe, h, t)

                        with pe.Fori(0, HEADS - 1) as h:
                            head(h)
                        head(HEADS - 1)

                    @block.scalar
                    def _(act):
                        def head(h, last):
                            for t in range(SLOTS):
                                if t == 0:
                                    act_gemm(act, h, t, last)
                                act_delta(act, h, t)
                                act_attn(act, h, t)
                                if t:
                                    act_gemm(act, h, t, last)

                        with act.Fori(0, HEADS - 1) as h:
                            head(h, False)
                        head(HEADS - 1, True)
                        split_hi(act, M0, 0, 16 * (M0 // 2 + 1))
                        act.wait_ge(gemm_halves, 2 * UNITS * (HEADS + 1))
                        gate_b(act, KB - 1, 1)
                        act.wait_ge(ao_stored, 32 * HEADS)
                        act.wait_ge(ob_stored, 32 * HEADS)

                    @block.vector
                    def _(v):
                        def head(h, last):
                            for t in range(SLOTS):
                                vec_delta(v, h, t)
                                vec_attn(v, h, t)
                                vec_gemm(v, h, t, last)

                        with v.Fori(0, HEADS - 1) as h:
                            head(h, False)
                        head(HEADS - 1, True)

                    @block.gpsimd
                    def _(pool):
                        def head(h, last):
                            for t in range(SLOTS):
                                pool_gemm(pool, h, t, last)
                                pool_delta(pool, h, t)

                        with pool.Fori(0, HEADS - 1) as h:
                            head(h, False)
                        head(HEADS - 1, True)
                        split_lo(pool, M0, 0)

        O0 = M0 + 2 * KB
        F0 = O0 + KB
        FB = w_up.shape[0] // 2
        tail = ExitStack()
        with tail:
            x1 = sb("x1", [P, TB, D], F32, tail)
            n2_hi = sb("n2_hi", [P, KB, T], F32R, tail)
            n2_lo = sb("n2_lo", [P, KB, T], F32R, tail)
            n2w = sb("n2w", [P, KB], F32, tail)
            ss2 = sb("ss2", [P, 2, TB], F32, tail)
            std2 = sb("std2", [P, TB], F32, tail)
            rstd2 = sb("rstd2", [P, TB], F32, tail)
            n2w_in = sem("n2w_in", tail)
            r_ss = sem("r_ss", tail)
            r_sum = sem("r_sum", tail)
            r_std = sem("r_std", tail)
            r_rec = sem("r_rec", tail)
            r_norm = sem("r_norm", tail)
            EARLY = 3

            def root(act, i, n):
                act.activation(std2[:, i:i + n], std2[:, i:i + n], ACT.Sqrt, bias=eps[:, :], scale=1.0 / D).then_inc(r_std, 1)

            def add_halves(v, i, n):
                v.tensor_tensor(std2[:, i:i + n], ss2[:, 0, i:i + n], ss2[:, 1, i:i + n], ALU.add).then_inc(r_sum, 1)

            def scale_row(v, row, i):
                v.tensor_scalar(row, x1[:, i, :], rstd2[:, i:i + 1], None, ALU.mult).then_inc(r_norm, 1)

            merge = ExitStack()
            with merge:
                mix_hi = sb("mix_hi", [P, KB, T], F32R, merge)
                mix_lo = sb("mix_lo", [P, KB, T], F32R, merge)
                gbuf = [sb(f"gbuf{i}", [P, HALF], F32, merge) for i in range(3)]
                stage = [nq, nk, nv]
                so_hi, so_lo = n2_hi, n2_lo
                mixa = x1

                o_landed = early_landed
                g_landed = [sem(f"g_landed{i}", merge) for i in range(3)]
                o_hi = sem("o_hi", merge)
                o_lo = sem("o_lo", merge)
                gated = sem("gated", merge)
                summed = sem("summed", merge)
                m_hi = sem("m_hi", merge)
                m_lo = sem("m_lo", merge)
                x_in = [sem(f"x_in{i}", merge) for i in range(TB)]
                out_rows = sem("out_rows", merge)
                added = sem("added", merge)

                OUT_CHUNKS = KB // 2
                OUT_BANK = [2, 3, 4, 5, 6, 7, 0, 1]

                def merge_bank(m, half):
                    return psum[:, 2 * (m == 1) + half, :]

                def halfcols(half):
                    return slice(half * HALF, (half + 1) * HALF)

                with nc.Block() as block:
                    @block.sync
                    def _(sp):
                        def source(m):
                            if m < 2 * KB:
                                return (w_proj_dn if m < KB else w_proj_sb)[m % KB]
                            if m < 3 * KB:
                                f, c = (m - 2 * KB) // OUT_CHUNKS, (m - 2 * KB) % OUT_CHUNKS
                                return w_out[f][:, 2 * c:2 * c + 2, :].rearrange("p k (a n) -> p (k a) n", n=P)
                            return w_up[0 if m == 3 * KB else FB]

                        def load_o(n):
                            sp.wait_ge(o_lo, n - 2)
                            sp.dma_start(stage[n % 3][:, :], o_d[n // HEADS][n % HEADS]).then_inc(o_landed[n % 3], 16)

                        def load_gate(g):
                            if g >= 3:
                                sp.wait_ge(gated, g - 2)
                                if g - 3 >= 2 * KB:
                                    sp.wait_ge(summed, g - 2 - 2 * KB)
                            sp.dma_start(gbuf[g % 3][:, :], gates_d[g // 2][:, halfcols(g % 2)]).then_inc(g_landed[g % 3], 16)

                        for n in (3, 4):
                            load_o(n)
                        load_unit(sp, M0 + 2, 0, source(2))
                        for n in (5, 6, 7):
                            load_o(n)
                        for half in (0, 1):
                            sp.wait_ge(gate_stored[half], 16 * (HEADS - 1 + KB))
                        for g in range(3):
                            load_gate(g)
                        for n in (0, 1, 2):
                            load_o(HEADS + n)
                        sp.dma_start(n2w[:, :], norm2).then_inc(n2w_in, 16)
                        for m in range(2, 3 * KB + 1):
                            load_unit(sp, M0 + m + 1, (m + 1) % 2, source(m + 1))
                            for g in (2 * m - 1, 2 * m):
                                if g < 4 * KB:
                                    load_gate(g)
                            if m + 1 < HEADS:
                                load_o(HEADS + m + 1)
                            i = m - KB - 3
                            if 0 <= i < TB:
                                sp.wait_ge(m_lo, 2 * i + 2)
                                sp.dma_start(x1[:, i, :], x[0, i * P:(i + 1) * P, :]).then_inc(x_in[i], 16)

                    @block.scalar
                    def _(act):
                        def split_o(n):
                            act.wait_ge(o_landed[n % 3], 16 * (n // 3 + 1))
                            act.activation((mix_hi if n < HEADS else so_hi)[:, n % HEADS, :], stage[n % 3][:, :],
                                           ACT.Copy).then_inc(o_hi, 1)

                        def square(f, i):
                            n = TB * f + i
                            act.wait_ge(added, n + 1)
                            if n >= 2:
                                act.wait_ge(r_ss, n - 1)
                            act.activation(gbuf[n % 2][:, :], x1[:, i, halfcols(f)], ACT.Square,
                                           accum_out=ss2[:, f, i:i + 1]).then_inc(r_ss, 1)

                        split_o(0)
                        split_hi(act, M0 + 1, 1, 16 * (M0 // 2 + 1))
                        for n in range(1, HEADS):
                            split_o(n)
                        for m in range(2, 3 * KB + 1):
                            split_hi(act, M0 + m, m % 2, 16 * ((M0 + m) // 2 + 1))
                            for n in {2: (0, 1)}.get(m, (m - 1,)):
                                if n < HEADS:
                                    split_o(HEADS + n)
                            if KB <= m - 2 < 2 * KB:
                                for half in (0, 1):
                                    act.wait_ge(summed, 2 * (m - 2 - KB) + half + 1)
                                    act.activation(mix_hi[:, m - 2 - KB, halfcols(half)], mixa[:, m - 2 - KB, halfcols(half)],
                                                   ACT.Copy).then_inc(m_hi, 1)
                            if m == 3 * KB - 2:
                                for i in range(TB):
                                    square(0, i)
                        for i in range(TB - 1):
                            square(1, i)
                            if 1 <= i <= EARLY:
                                act.wait_ge(r_sum, i)
                                root(act, i - 1, 1)

                    @block.gpsimd
                    def _(pool):
                        split_lo(pool, M0 + 1, 1)
                        for m in range(2, 3 * KB + 1):
                            split_lo(pool, M0 + m, m % 2)
                            if KB <= m - 2 < 2 * KB:
                                for half in (0, 1):
                                    pool.wait_ge(m_hi, 2 * (m - 2 - KB) + half + 1)
                                    pool.tensor_tensor(mix_lo[:, m - 2 - KB, halfcols(half)],
                                                       mixa[:, m - 2 - KB, halfcols(half)],
                                                       mix_hi[:, m - 2 - KB, halfcols(half)].bitcast(F32),
                                                       ALU.subtract).then_inc(m_lo, 1)

                    @block.vector
                    def _(v):
                        def low_o(n):
                            v.wait_ge(o_hi, n + 1)
                            hi, lo = (mix_hi, mix_lo) if n < HEADS else (so_hi, so_lo)
                            v.tensor_tensor(lo[:, n % HEADS, :], stage[n % 3][:, :], hi[:, n % HEADS, :].bitcast(F32),
                                            ALU.subtract).then_inc(o_lo, 1)

                        for n in range(HEADS):
                            low_o(n)
                        for m in range(2 * KB):
                            for half in (0, 1):
                                g, cols = 2 * m + half, halfcols(half)
                                v.wait_ge(g_landed[g % 3], 16 * (g // 3 + 1))
                                v.wait_ge(gemm_halves, 2 * (M0 + m) + half + 1)
                                dst = mixa[:, m, cols] if m < KB else gbuf[g % 3][:, :]
                                v.tensor_tensor(dst, merge_bank(m, half), gbuf[g % 3][:, :], ALU.mult).then_inc(gated, 1)
                                if m >= KB:
                                    v.wait_ge(gated, g + 1)
                                    v.tensor_tensor(mixa[:, m - KB, cols], mixa[:, m - KB, cols], dst,
                                                    ALU.add).then_inc(summed, 1)
                            for n in {0: (0, 1)}.get(m, (m + 1,)):
                                if n < HEADS:
                                    low_o(HEADS + n)

                        def scaled(i):
                            v.wait_ge(r_ss, TB + i + 1)
                            add_halves(v, i, 1)
                            v.wait_ge(r_std, i + 1)
                            v.reciprocal(rstd2[:, i:i + 1], std2[:, i:i + 1]).then_inc(r_rec, 1)
                            v.wait_ge(r_rec, i + 1)
                            scale_row(v, stage[i][:, :], i)

                        for n in range(2 * TB):
                            f, i = n // TB, n % TB
                            if f == 0:
                                v.wait_ge(x_in[i], 16)
                            v.wait_ge(out_rows, n + 1)
                            v.tensor_tensor(x1[:, i, halfcols(f)], psum[:, OUT_BANK[i], :], x1[:, i, halfcols(f)],
                                            ALU.add).then_inc(added, 1)
                            if f and 2 <= i < 2 + EARLY:
                                scaled(i - 2)

                    @block.tensor
                    def _(pe):
                        for k in range(KB + 3):
                            for m, kk in ((0, k), (1, k - 3)):
                                if not 0 <= kk < KB:
                                    continue
                                if kk == 0:
                                    pe.wait_ge(hi_split, M0 + m + 1)
                                    pe.wait_ge(lo_split, M0 + m + 1)
                                if m == 0:
                                    pe.wait_ge(o_lo, k + 1)
                                for half in (0, 1):
                                    mm = unit_products(pe, m, half, (kk,), mix_hi, mix_lo, merge_bank(m, half))
                                    if kk == KB - 1:
                                        mm.then_inc(gemm_halves, 1)
                        for m in range(2, 2 * KB):
                            U = M0 + m
                            pe.wait_ge(hi_split, U + 1)
                            pe.wait_ge(lo_split, U + 1)
                            if m == KB:
                                pe.wait_ge(o_lo, 2 * HEADS)
                            for half in (0, 1):
                                pe.wait_ge(gated, 2 * m + half - 1 if m > 2 else half + 1)
                                hi, lo = (mix_hi, mix_lo) if m < KB else (so_hi, so_lo)
                                unit_products(pe, m % 2, half, range(KB), hi, lo).then_inc(gemm_halves, 1)
                        for n in range(KB):
                            f, c = n // OUT_CHUNKS, n % OUT_CHUNKS
                            pe.wait_ge(hi_split, O0 + n + 1)
                            pe.wait_ge(lo_split, O0 + n + 1)
                            if f == 0:
                                pe.wait_ge(m_lo, 4 * c + 4)
                            for i in range(TB):
                                if c == 0:
                                    if f:
                                        pe.wait_ge(added, i + 1)
                                    else:
                                        pe.wait_ge(gated, 4 * KB - 1 + (i == TB - 1))
                                for k in (0, 1):
                                    for j, (a, w) in enumerate(((mix_hi, w_hi), (mix_hi, w_lo), (mix_lo, w_hi))):
                                        mm = pe.matmul(psum[:, OUT_BANK[i], :], a[:, 2 * c + k, i * P:(i + 1) * P],
                                                       w[n % 2][:, 4 * k:4 * k + 4, :].rearrange("p a n -> p (a n)"),
                                                       start=(c == 0 and k == 0 and j == 0),
                                                       stop=(c == OUT_CHUNKS - 1 and k == 1 and j == 2))
                                        if f and c == 0 and i == 0 and k == 0 and j == 0:
                                            mm.then_inc(gemm_halves, 2)
                                if c == OUT_CHUNKS - 1:
                                    mm.then_inc(out_rows, 1)
                                elif i % (TB // 2) == TB // 2 - 1:
                                    mm.then_inc(gemm_halves, 1)

            GROUPS = FB // 2
            FSLOTS = 32
            gb, ub = sb("gb", [P, T], F32, tail), sb("ub", [P, T], F32, tail)
            fpre = sb("fpre", [P, 2 + T], F32, tail)
            a_hi = sb("a_hi", [P, 2, T], F32R, tail)
            a_lo = sb("a_lo", [P, 2, T], F32R, tail)
            wd_raw = sb("wd_raw", [P, 2, D], F32, tail)
            wd_hi = sb("wd_hi", [P, 2, D], F32R, tail)
            wd_lo = sb("wd_lo", [P, 2, D], F32R, tail)
            taps = sb("taps", [P, 2, FB, 3], F32, tail)
            tapc = sb("tapc", [P, 2, 2, 3], F32, tail)
            wf = sb("wf", [P, D], F32, tail)
            sqf = [sb(f"sqf{i}", [P, D], F32, tail) for i in (0, 1)]
            stdf = sb("stdf", [P, TB], F32, tail)
            small_in = sem("small_in", tail)
            wd_landed = sem("wd_landed", tail)
            wd_his = sem("wd_his", tail)
            wd_los = sem("wd_los", tail)
            f_read = sem("f_read", tail)
            f_pad = sem("f_pad", tail)
            tap_in = sem("tap_in", tail)
            f_conv = sem("f_conv", tail)
            f_silu = sem("f_silu", tail)
            f_prod = sem("f_prod", tail)
            f_hi = sem("f_hi", tail)
            f_lo = sem("f_lo", tail)
            down = sem("down", tail)
            down_added = sem("down_added", tail)
            r_turn = sem("r_turn", tail)
            r_hi = sem("r_hi", tail)
            r_lo = sem("r_lo", tail)
            r_late = sem("r_late", tail)
            xr = [nq, nk, nv, sqf[0], sqf[1], gb, ub, fpre[:, 2:2 + T]]
            e_ss, e_std, e_rec, e_out = (sem(n, tail) for n in ("e_ss", "e_std", "e_rec", "e_out"))
            stored = sem("stored", tail)

            def down_output(pe, g, n):
                i, f = n // 2, n % 2
                if n >= 4 or not (isinstance(g, int) and g == 0):
                    pe.wait_ge(down_added, 16 * g + n - 3)
                if n == 0:
                    pe.wait_ge(wd_los, g + 1)
                    pe.wait_ge(f_lo, 4 * g + 3)
                if n == 8:
                    pe.wait_ge(f_lo, 4 * g + 4)
                bank = psum[:, 2 + n % 4, :]
                for k in (0, 1):
                    for j, (a, w) in enumerate(((a_hi, wd_hi), (a_hi, wd_lo), (a_lo, wd_hi))):
                        mm = pe.matmul(bank, a[:, k, i * P:(i + 1) * P], w[:, k, f * HALF:(f + 1) * HALF],
                                       start=(k == 0 and j == 0), stop=(k == 1 and j == 2))
                mm.then_inc(down, 1)

            def down_add(v, g, n):
                i, f = n // 2, n % 2
                v.wait_ge(down, 16 * g + n + 1)
                v.tensor_tensor(x1[:, i, f * HALF:(f + 1) * HALF], psum[:, 2 + n % 4, :],
                                x1[:, i, f * HALF:(f + 1) * HALF], ALU.add).then_inc(down_added, 1)

            def events(t):
                H = t // 4 - 1
                return (H, t % 4, 0) if H >= 0 else (7, t % 4, 1)

            def hcols(half):
                return slice(half * HALF, (half + 1) * HALF)

            def act_ffn(act, g, t, only_events=False):
                H, phase, back = events(t)
                u, half = H // 2, H % 2
                gg = g - back
                if not (isinstance(gg, int) and gg < 0):
                    if phase == 0:
                        act.wait_ge(gemm_halves, 2 * F0 + 8 * gg + H + 1)
                        if half == 0:
                            if not (isinstance(gg, int) and gg == 0 and H == 0):
                                act.wait_ge(f_conv, 24 * gg + 3 * H)
                            else:
                                act.wait_ge(f_pad, 1)
                                act.wait_ge(r_turn, 2 * KB)
                        act.activation(fpre[:, 2 + half * HALF:2 + (half + 1) * HALF], gemm_bank[half],
                                       ACT.Copy).then_inc(f_read, 1)
                    if phase == 3:
                        act.wait_ge(f_conv, 24 * gg + 3 * H + 3)
                        if u % 2 == 0:
                            act.activation(gb[:, hcols(half)], gb[:, hcols(half)], ACT.Silu).then_inc(f_silu, 1)
                        else:
                            act.wait_ge(f_prod, 4 * gg + 2 * (u // 2) + half + 1)
                            if not (isinstance(gg, int) and gg == 0):
                                act.wait_ge(down, 16 * gg - 8 + 8 * half)
                            act.activation(a_hi[:, u // 2, hcols(half)], ub[:, hcols(half)], ACT.Copy).then_inc(f_hi, 1)
                if only_events:
                    return
                if t % 8 == 1:
                    u = t // 8 + 1
                    if not (isinstance(g, int) and (g == GROUPS - 1 and u == 4 or g == 0 and u == 1)):
                        split_hi(act, F0 + 4 * g + u, u % 2, 16 * (F0 // 2 + 2 * g + u // 2 + 1))
                if t == 20:
                    act.wait_ge(wd_landed, 16 * (g + 1))
                    if not (isinstance(g, int) and g == 0):
                        act.wait_ge(down, 16 * g)
                    act.activation(wd_hi[:, :, :], wd_raw[:, :, :], ACT.Copy).then_inc(wd_his, 1)

            def vec_ffn(v, g, t, only_events=False):
                H, phase, back = events(t)
                u, half = H // 2, H % 2
                gg = g - back
                if t >= 1 and t <= 16 and not (isinstance(g, int) and g == 0):
                    down_add(v, g - 1, t - 1)
                if not (isinstance(gg, int) and gg < 0):
                    buf = (gb if u % 2 == 0 else ub)[:, hcols(half)]
                    if phase < 3:
                        w = tapc[:, u % 2, u // 2, :]
                        x_j = fpre[:, 2 - phase + half * HALF:2 - phase + (half + 1) * HALF]
                        if phase == 0:
                            v.wait_ge(f_read, 8 * gg + H + 1)
                            if H == 0:
                                v.wait_ge(tap_in, 1 + gg)
                            if u % 2:
                                if not (isinstance(gg, int) and gg == 0 and u == 1):
                                    v.wait_ge(f_lo, 4 * gg + 2 * (u // 2) + half - 1)
                            v.tensor_scalar(buf, x_j, w[:, 2:3], None, ALU.mult).then_inc(f_conv, 1)
                        else:
                            v.wait_ge(f_conv, 24 * gg + 3 * H + phase)
                            v.scalar_tensor_tensor(out=buf, in0=x_j, scalar=w[:, 2 - phase:3 - phase], in1=buf,
                                                   op0=ALU.mult, op1=ALU.add).then_inc(f_conv, 1)
                    elif u % 2:
                        v.wait_ge(f_silu, 4 * gg + 2 * (u // 2) + half + 1)
                        v.wait_ge(f_conv, 24 * gg + 3 * H + 3)
                        v.tensor_tensor(buf, gb[:, hcols(half)], buf, ALU.mult).then_inc(f_prod, 1)
                if only_events:
                    return
                if t == 3:
                    v.tensor_copy(tapc[:, :, :, :], taps[:, :, bass.ds(2 * g, 2), :]).then_inc(tap_in, 1)

            def pool_ffn(pool, g, t, only_events=False):
                H, phase, back = events(t)
                u, half = H // 2, H % 2
                gg = g - back
                if not (isinstance(gg, int) and gg < 0) and phase == 3 and u % 2:
                    pool.wait_ge(f_hi, 4 * gg + 2 * (u // 2) + half + 1)
                    pool.tensor_tensor(a_lo[:, u // 2, hcols(half)], ub[:, hcols(half)],
                                       a_hi[:, u // 2, hcols(half)].bitcast(F32), ALU.subtract).then_inc(f_lo, 1)
                if only_events:
                    return
                if t % 8 == 1:
                    u = t // 8 + 1
                    if not (isinstance(g, int) and g == GROUPS - 1 and u == 4):
                        split_lo(pool, F0 + 4 * g + u, u % 2)
                if t == 20:
                    pool.wait_ge(wd_his, g + 1)
                    if not (isinstance(g, int) and g == 0):
                        pool.wait_ge(down, 16 * g)
                    pool.tensor_tensor(wd_lo[:, :, :], wd_raw[:, :, :], wd_hi[:, :, :].bitcast(F32),
                                       ALU.subtract).then_inc(wd_los, 1)

            def pe_ffn(pe, g, t):
                if t >= 1 and t <= 16 and not (isinstance(g, int) and g == 0):
                    down_output(pe, g - 1, t - 1)
                u, half, part = t // 8, t % 8 // 4, t % 4
                U = F0 + 4 * g + u
                if part == 0:
                    if half == 0:
                        pe.wait_ge(hi_split, U + 1)
                        pe.wait_ge(lo_split, U + 1)
                    if not (isinstance(g, int) and g == 0 and u == 0):
                        pe.wait_ge(f_read, 8 * g + 2 * u + half - 1)
                mm = unit_products(pe, u % 2, half, (2 * part, 2 * part + 1), n2_hi, n2_lo)
                if part == 3:
                    mm.then_inc(gemm_halves, 1)

            with nc.Block() as block:
                @block.sync
                def _(sp):
                    sp.dma_start(taps[:, :, :, :], ffn_conv.rearrange("p (s b) j -> p s b j", s=2)).then_inc(small_in, 16)
                    sp.dma_start(wf[:, :], norm_f.to_broadcast([P, D])).then_inc(small_in, 16)

                    def group(g, units):
                        for u in units:
                            src = w_up[bass.ds(2 * g + (u % 2 * FB + u // 2), 1)].rearrange("o p k n -> (o p) k n")
                            load_unit(sp, F0 + 4 * g + u, u % 2, src)
                        if not (isinstance(g, int) and g == 0):
                            sp.wait_ge(wd_los, g)
                        sp.dma_start(wd_raw[:, :, :], w_down[bass.ds(g, 1)].rearrange("o p k n -> (o p) k n")).then_inc(wd_landed, 16)

                    group(0, (2, 3))
                    with sp.Fori(1, GROUPS) as g:
                        group(g, range(4))
                    for i in range(TB):
                        sp.wait_ge(e_out, i + 1)
                        sp.dma_start(out[0, i * P:(i + 1) * P, :], x1[:, i, :]).then_inc(stored, 16)
                    sp.wait_ge(stored, 16 * TB)

                @block.tensor
                def _(pe):
                    def turn_rows(i2, k):
                        n = KB * i2 + k
                        if n >= 4:
                            pe.wait_ge(r_lo, n - 3)
                        if n == 0:
                            pe.wait_ge(r_norm, EARLY + 1)
                        if n == KB:
                            pe.wait_ge(r_late, 4)
                        for i in range(4):
                            tr = pe.transpose(psum[:, 2 + k % 4, i * P:(i + 1) * P],
                                              xr[4 * i2 + i][:, k * P:(k + 1) * P], identf[:, :])
                            if n == 0 and i == 0:
                                tr.then_inc(gemm_halves, 2)
                        tr.then_inc(r_turn, 1)

                    pe.wait_ge(hi_split, F0 + 1)
                    pe.wait_ge(lo_split, F0 + 1)
                    for half in (0, 1):
                        for k in range(KB + 2):
                            if k < KB:
                                turn_rows(half, k)
                            if k >= 2:
                                pe.wait_ge(r_lo, KB * half + k - 1)
                                mm = unit_products(pe, 0, half, (k - 2,), n2_hi, n2_lo)
                        mm.then_inc(gemm_halves, 1)
                    for g in (0, 1):
                        for t in range(0 if g else 8, FSLOTS):
                            pe_ffn(pe, g, t)
                    with pe.Fori(2, GROUPS) as g:
                        for t in range(FSLOTS):
                            pe_ffn(pe, g, t)
                    for n in range(2 * TB):
                        down_output(pe, GROUPS - 1, n)

                @block.scalar
                def _(act):
                    act.activation(sqf[1][:, 0:HALF], x1[:, TB - 1, HALF:D], ACT.Square,
                                   accum_out=ss2[:, 1, TB - 1:TB]).then_inc(r_ss, 1)
                    act.wait_ge(r_sum, EARLY + 1)
                    root(act, EARLY, TB - EARLY)
                    act.wait_ge(n2w_in, 16)
                    for n in range(2 * KB):
                        k = n % KB
                        act.wait_ge(r_turn, n + 1)
                        act.activation(n2_hi[:, k, hcols(n // KB)], psum[:, 2 + k % 4, :], ACT.Copy,
                                       scale=n2w[:, k:k + 1]).then_inc(r_hi, 1)
                        if n == KB:
                            split_hi(act, F0 + 1, 1, 16 * (F0 // 2 + 1))
                        if n == 3:
                            act.activation(xr[TB - 1], x1[:, TB - 1, :], ACT.Copy,
                                           scale=rstd2[:, TB - 1:TB]).then_inc(r_late, 1)
                    for t in range(FSLOTS):
                        act_ffn(act, 0, t)
                    with act.Fori(1, GROUPS - 1) as g:
                        for t in range(FSLOTS):
                            act_ffn(act, g, t)
                    for t in range(FSLOTS):
                        act_ffn(act, GROUPS - 1, t)
                    for t in range(4):
                        act_ffn(act, GROUPS, t, only_events=True)
                    for i in range(TB):
                        act.wait_ge(down_added, 16 * (GROUPS - 1) + 2 * i + 2)
                        if i >= 2:
                            act.wait_ge(e_out, i - 1)
                        act.activation(sqf[i % 2][:, :], x1[:, i, :], ACT.Square, accum_out=stdf[:, i:i + 1]).then_inc(e_ss, 1)
                        act.wait_ge(e_ss, i + 1)
                        act.activation(stdf[:, i:i + 1], stdf[:, i:i + 1], ACT.Sqrt, bias=eps[:, :], scale=1.0 / D).then_inc(e_std, 1)

                @block.gpsimd
                def _(pool):
                    pool.wait_ge(r_rec, EARLY + 1)
                    for i in range(4, TB - 1):
                        pool.tensor_tensor(xr[i][:, :], x1[:, i, :], rstd2[:, i:i + 1].to_broadcast([P, D]),
                                           ALU.mult).then_inc(r_late, 1)
                    for t in range(FSLOTS):
                        pool_ffn(pool, 0, t)
                    with pool.Fori(1, GROUPS - 1) as g:
                        for t in range(FSLOTS):
                            pool_ffn(pool, g, t)
                    for t in range(FSLOTS):
                        pool_ffn(pool, GROUPS - 1, t)
                    for t in range(4):
                        pool_ffn(pool, GROUPS, t, only_events=True)

                @block.vector
                def _(v):
                    v.memset(fpre[:, 0:2], 0.0).then_inc(f_pad, 1)
                    v.wait_ge(r_ss, 2 * TB)
                    add_halves(v, EARLY, TB - EARLY)
                    v.wait_ge(r_std, EARLY + 1)
                    v.reciprocal(rstd2[:, EARLY:TB], std2[:, EARLY:TB]).then_inc(r_rec, 1)
                    v.wait_ge(r_rec, EARLY + 1)
                    scale_row(v, xr[EARLY][:, :], EARLY)
                    for n in range(2 * KB):
                        k, cols = n % KB, hcols(n // KB)
                        v.wait_ge(r_hi, n + 1)
                        v.scalar_tensor_tensor(out=n2_lo[:, k, cols], in0=psum[:, 2 + k % 4, :], scalar=n2w[:, k:k + 1],
                                               in1=n2_hi[:, k, cols].bitcast(F32), op0=ALU.mult,
                                               op1=ALU.subtract).then_inc(r_lo, 1)
                    v.wait_ge(small_in, 32)
                    for t in range(FSLOTS):
                        vec_ffn(v, 0, t)
                    with v.Fori(1, GROUPS) as g:
                        for t in range(FSLOTS):
                            vec_ffn(v, g, t)
                    def final(i):
                        v.wait_ge(e_std, i + 1)
                        v.reciprocal(stdf[:, i:i + 1], stdf[:, i:i + 1]).then_inc(e_rec, 1)
                        v.wait_ge(e_rec, i + 1)
                        v.scalar_tensor_tensor(out=x1[:, i, :], in0=x1[:, i, :], scalar=stdf[:, i:i + 1], in1=wf[:, :],
                                               op0=ALU.mult, op1=ALU.mult).then_inc(e_out, 1)
                    for t in range(4):
                        vec_ffn(v, GROUPS, t, only_events=True)
                    for n in range(3, 2 * TB):
                        down_add(v, GROUPS - 1, n)
                        if n % 2 and n >= 5:
                            final(n // 2 - 2)
                    final(TB - 2)
                    final(TB - 1)


def kernel(**inputs):
    import concourse.bacc as bacc
    from concourse.bass_utils import run_bass_kernel_spmd

    nc = bacc.Bacc("TRN2", target_bir_lowering=False, num_devices=1)
    arrays, args = {}, []
    for name, a in layout(inputs).items():
        arrays[name] = a
        args.append(nc.dram_tensor(name, a.shape, mybir.dt.from_np(a.dtype), kind="ExternalInput").ap())
    shape = inputs["x"].shape
    out = nc.dram_tensor("out", shape, F32, kind="ExternalOutput").ap()
    build(nc, *args, out)
    results = run_bass_kernel_spmd(nc, [arrays], core_ids=[0])
    return results.results[0]["out"]


def layout(inputs):
    def units(w):
        k, n = w.shape
        return np.ascontiguousarray(w.reshape(k // P, P, n // P, P).transpose(2, 1, 0, 3))

    def columns(v):
        return np.ascontiguousarray(v.reshape(-1, P).T)

    a = {k: np.asarray(v) for k, v in inputs.items()}
    w = a["w_in"][0]
    qkv = 3 * HEADS * P
    taps = a["dn_conv_w"][0]
    up_taps = a["ffn_conv_w"][0]
    return {
        "x_in": a["x"],
        "norm1": columns(a["norm1_w"][0]),
        "w_main": units(np.concatenate([w[:, :qkv], w[:, qkv + 2 * HEADS:]], axis=1)),
        "w_ab": np.ascontiguousarray(w[:, qkv:qkv + 2 * HEADS].reshape(-1, P, 2 * HEADS).transpose(1, 0, 2)),
        "conv": np.ascontiguousarray(taps.reshape(taps.shape[0], 3, HEADS, P).transpose(3, 2, 1, 0)),
        "a_log": a["dn_A_log"],
        "dt_bias": a["dn_dt_bias"],
        "dn_norm": columns(a["dn_norm_w"][0]),
        "proj_dn": units(a["w_proj_dn"][0]),
        "proj_sb": units(a["w_proj_sb"][0]),
        "w_out_u": np.ascontiguousarray(a["w_out"][0].reshape(-1, P, 2, HALF).transpose(2, 1, 0, 3)),
        "norm2": columns(a["norm2_w"][0]),
        "w_up": units(a["ffn_w_up"][0]),
        "ffn_conv": np.ascontiguousarray(up_taps.reshape(up_taps.shape[0], -1, P).transpose(2, 1, 0)),
        "w_down": np.ascontiguousarray(a["ffn_w_down"][0].reshape(-1, 2, P, a["x"].shape[-1]).transpose(0, 2, 1, 3)),
        "norm_f": a["norm_f_w"].reshape(1, -1),
    }
```
